# Optimizing a Trainium2 kernel written in Bass

```python
import functools
import jax, jax.numpy as jnp
from jax import lax
import numpy as np

D_MODEL = 2048
BATCH = 1
SEQ = 256
DEPTH = 1
DEC_BATCH = 8
DEC_SEQ = 8
PAST_LEN = 1024
PAGE_SIZE = 128

HEAD_DIM = 64
N_HEADS = (D_MODEL // 2) // HEAD_DIM
N_KV_HEADS = N_HEADS // 4
ATTN_W = N_HEADS * HEAD_DIM
KV_W = N_KV_HEADS * HEAD_DIM
N_IDX_HEADS = 8
IDX_DIM = 64
TOPK_MAX = 256
Q_BLOCK = 128
ROPE_THETA = 10000.0
D_RNN = D_MODEL // 2
N_RNN_BLOCKS = 16
RNN_BLOCK = D_RNN // N_RNN_BLOCKS
CONV_W = 4
LRU_C = 8.0
N_GROUPS = 4
EXPERTS_PER_GROUP = 8
N_EXPERTS = N_GROUPS * EXPERTS_PER_GROUP
TOP_K_EXPERTS = 2
D_EXPERT = D_MODEL // 8
PLE_DIM = 256
EPS = 1e-6
IN_SPLITS = (D_RNN, D_RNN, ATTN_W, KV_W, KV_W, N_IDX_HEADS * IDX_DIM, IDX_DIM, N_IDX_HEADS, D_MODEL, D_MODEL)
D_IN = 2 * D_RNN + ATTN_W + 2 * KV_W + N_IDX_HEADS * IDX_DIM + IDX_DIM + N_IDX_HEADS + 2 * D_MODEL

kernel_name = 'hawk_dsa_hmoe_decode_step'

def _rmsnorm(x, g):
    xf = x.astype(jnp.float32)
    y = xf * lax.rsqrt(jnp.mean(xf * xf, axis=-1, keepdims=True) + EPS)
    return (y * g.astype(jnp.float32)).astype(x.dtype)

def _rope(x, pos):
    half = x.shape[-1] // 2
    inv = ROPE_THETA ** (-jnp.arange(half, dtype=jnp.float32) / half)
    ang = pos.astype(jnp.float32)[:, None] * inv[None, :]
    cos = jnp.cos(ang)[None, :, None, :]
    sin = jnp.sin(ang)[None, :, None, :]
    xf = x.astype(jnp.float32)
    x1, x2 = xf[..., :half], xf[..., half:]
    return jnp.concatenate([x1 * cos - x2 * sin, x2 * cos + x1 * sin], axis=-1).astype(x.dtype)

def _take(a, idx):
    return jax.vmap(lambda ab, ib: ab[ib])(a, idx)

def _dsa_attend(q, qi, wi, qpos, kidx, gather_kv, topk):
    f32 = jnp.float32
    L = kidx.shape[1]
    s = jnp.einsum('bthd,bsd->bths', qi.astype(f32), kidx.astype(f32)) * (IDX_DIM ** -0.5)
    score = jnp.einsum('bths,bth->bts', jax.nn.relu(s), wi.astype(f32)) * (N_IDX_HEADS ** -0.5)
    causal = jnp.arange(L, dtype=jnp.int32)[None, :] <= qpos[:, None]
    score = jnp.where(causal[None], score, jnp.finfo(f32).min)
    _, idx = lax.top_k(score, topk)
    valid = idx <= qpos[None, :, None]
    k_sel, v_sel = gather_kv(idx)
    b, tq = q.shape[:2]
    qg = q.reshape(b, tq, N_KV_HEADS, N_HEADS // N_KV_HEADS, HEAD_DIM).astype(f32)
    logits = jnp.einsum('btkgd,btskd->btkgs', qg, k_sel.astype(f32)) * (HEAD_DIM ** -0.5)
    logits = jnp.where(valid[:, :, None, None, :], logits, -jnp.inf)
    prob = jax.nn.softmax(logits, axis=-1)
    out = jnp.einsum('btkgs,btskd->btkgd', prob, v_sel.astype(f32))
    return out.reshape(b, tq, ATTN_W).astype(q.dtype)

def _prompt_attention(q, k, v, qi, ki, wi, pos):
    b, t = q.shape[:2]
    topk = min(TOPK_MAX, t // 4)
    nb = t // Q_BLOCK

    def gather_kv(idx):
        return _take(k, idx), _take(v, idx)

    def to_blocks(a):
        return jnp.swapaxes(a.reshape(b, nb, Q_BLOCK, *a.shape[2:]), 0, 1)

    def one_block(args):
        qb, qib, wib, pb = args
        return _dsa_attend(qb, qib, wib, pb, ki, gather_kv, topk)

    out = lax.map(one_block, (to_blocks(q), to_blocks(qi), to_blocks(wi), pos.reshape(nb, Q_BLOCK)))
    return jnp.swapaxes(out, 0, 1).reshape(b, t, ATTN_W)

def _sample_attention(q, k, v, qi, ki, wi, pos, cache_k, cache_v, cache_kidx, page_table):
    b, t = q.shape[:2]
    past = page_table.shape[1] * PAGE_SIZE
    topk = min(TOPK_MAX, (past + t) // 4)
    kidx_past = cache_kidx[page_table].reshape(b, past, IDX_DIM).astype(ki.dtype)
    kidx_all = jnp.concatenate([kidx_past, ki], axis=1)
    k_pool = cache_k.reshape(-1, N_KV_HEADS, HEAD_DIM)
    v_pool = cache_v.reshape(-1, N_KV_HEADS, HEAD_DIM)

    def gather_kv(idx):
        in_past = (idx < past)[..., None, None]
        pi = jnp.minimum(idx, past - 1)
        rows = _take(page_table, pi // PAGE_SIZE) * PAGE_SIZE + pi % PAGE_SIZE
        ni = jnp.clip(idx - past, 0, t - 1)
        k_sel = jnp.where(in_past, k_pool[rows].astype(k.dtype), _take(k, ni))
        v_sel = jnp.where(in_past, v_pool[rows].astype(v.dtype), _take(v, ni))
        return k_sel, v_sel

    return _dsa_attend(q, qi, wi, pos, kidx_all, gather_kv, topk)

def _rglru_branch(xr, gr, conv_prev, h_prev, conv_w, conv_b, w_a, b_a, w_x, b_x, lam):
    f32 = jnp.float32
    b, t, _ = xr.shape
    xpad = jnp.concatenate([conv_prev.astype(xr.dtype), xr], axis=1)
    xc = conv_b + sum(xpad[:, j:j + t] * conv_w[j] for j in range(CONV_W))
    conv_new = xpad[:, t:]
    xb = xc.reshape(b, t, N_RNN_BLOCKS, RNN_BLOCK)
    r = jax.nn.sigmoid(jnp.einsum('btni,nij->btnj', xb, w_a).reshape(b, t, D_RNN) + b_a)
    i = jax.nn.sigmoid(jnp.einsum('btni,nij->btnj', xb, w_x).reshape(b, t, D_RNN) + b_x)
    log_a = -LRU_C * r.astype(f32) * jax.nn.softplus(-lam.astype(f32))
    a = jnp.exp(log_a)
    u = jnp.sqrt(-jnp.expm1(2.0 * log_a)) * (i * xc).astype(f32)

    def step(h, au):
        a_t, u_t = au
        h = a_t * h + u_t
        return h, h

    h_last, hs = lax.scan(step, h_prev.astype(f32), (jnp.swapaxes(a, 0, 1), jnp.swapaxes(u, 0, 1)))
    hs = jnp.swapaxes(hs, 0, 1).astype(xr.dtype)
    return hs * jax.nn.gelu(gr), conv_new, h_last.astype(xr.dtype)

def _hier_moe(h, w_rg, b_rg, w_re, b_re, w1, w3, w2):
    f32 = jnp.float32
    b, t, _ = h.shape
    g_logit = (h @ w_rg).astype(f32) + b_rg.astype(f32)
    g_prob = jax.nn.softmax(g_logit, axis=-1)
    g_sel = jnp.argmax(g_logit, axis=-1)
    g_onehot = jax.nn.one_hot(g_sel, N_GROUPS, dtype=f32)
    e_logit = ((h @ w_re).astype(f32) + b_re.astype(f32)).reshape(b, t, N_GROUPS, EXPERTS_PER_GROUP)
    e_in_group = jnp.einsum('btge,btg->bte', e_logit, g_onehot)
    top_v, top_i = lax.top_k(e_in_group, TOP_K_EXPERTS)
    w_top = jax.nn.softmax(top_v, axis=-1) * jnp.max(g_prob, axis=-1, keepdims=True)
    e_idx = g_sel[..., None] * EXPERTS_PER_GROUP + top_i
    gates = jnp.einsum('btke,btk->bte', jax.nn.one_hot(e_idx, N_EXPERTS, dtype=f32), w_top).astype(h.dtype)
    hid = jax.nn.silu(jnp.einsum('btd,edf->btef', h, w1)) * jnp.einsum('btd,edf->btef', h, w3)
    return jnp.einsum('btef,efd->btd', hid * gates[..., None], w2)

def _layer(x, p, pos, conv_prev, h_prev, attend, ln1, w_in, q_norm, k_norm, conv_w, conv_b,
           w_a, b_a, w_x, b_x, lam, w_br_rnn, w_br_attn, w_out, ln2, w_rg, b_rg, w_re, b_re,
           w1, w3, w2, ln3, w_ple_gate, w_ple_proj):
    b, t, _ = x.shape
    h = _rmsnorm(x, ln1)
    offs = np.cumsum(IN_SPLITS)[:-1].tolist()
    xr, gr, q, k, v, qi, ki, wi, gm_r, gm_a = jnp.split(h @ w_in, offs, axis=-1)
    q = _rope(_rmsnorm(q.reshape(b, t, N_HEADS, HEAD_DIM), q_norm), pos)
    k = _rope(_rmsnorm(k.reshape(b, t, N_KV_HEADS, HEAD_DIM), k_norm), pos)
    v = v.reshape(b, t, N_KV_HEADS, HEAD_DIM)
    qi = _rope(qi.reshape(b, t, N_IDX_HEADS, IDX_DIM), pos)
    ki = _rope(ki[:, :, None, :], pos)[:, :, 0, :]
    attn = attend(q, k, v, qi, ki, wi, pos)
    rnn, conv_new, h_new = _rglru_branch(xr, gr, conv_prev, h_prev, conv_w, conv_b, w_a, b_a, w_x, b_x, lam)
    mixed = jax.nn.sigmoid(gm_r) * (rnn @ w_br_rnn) + jax.nn.sigmoid(gm_a) * (attn @ w_br_attn)
    x = x + mixed @ w_out
    x = x + _hier_moe(_rmsnorm(x, ln2), w_rg, b_rg, w_re, b_re, w1, w3, w2)
    x = x + jax.nn.sigmoid(_rmsnorm(x, ln3) @ w_ple_gate) * (p @ w_ple_proj)
    return x, (k, v, ki, conv_new, h_new)

def setup_inputs(seed: int = 0) -> dict:
    key = jax.random.key(seed)
    keys = jax.random.split(key, 40)
    ctr = [0]

    def nk():
        ctr[0] += 1
        return keys[ctr[0] - 1]

    def nrm(shape, scale):
        return scale * jax.random.normal(nk(), shape, jnp.float32)

    def gain(shape):
        return 1.0 + nrm(shape, 0.05)

    n_pages = PAST_LEN // PAGE_SIZE
    n_used = DEC_BATCH * n_pages
    n_pool = n_used + max(1, n_used // 4)
    page_table = jax.random.permutation(nk(), n_pool)[:n_used].reshape(DEC_BATCH, n_pages).astype(jnp.int32)
    a_pow = jax.random.uniform(nk(), (DEPTH, D_RNN), jnp.float32, 0.9, 0.999)
    a_base = a_pow ** (1.0 / LRU_C)
    lam = jnp.log(a_base) - jnp.log1p(-a_base)
    return {
        'x_prompt': nrm((BATCH, SEQ, D_MODEL), 1.0),
        'x_sample': nrm((DEC_BATCH, DEC_SEQ, D_MODEL), 1.0),
        'p_prompt': nrm((DEPTH, BATCH, SEQ, PLE_DIM), 1.0),
        'p_sample': nrm((DEPTH, DEC_BATCH, DEC_SEQ, PLE_DIM), 1.0),
        'cache_k': nrm((DEPTH, n_pool, PAGE_SIZE, N_KV_HEADS, HEAD_DIM), 1.0),
        'cache_v': nrm((DEPTH, n_pool, PAGE_SIZE, N_KV_HEADS, HEAD_DIM), 1.0),
        'cache_kidx': nrm((DEPTH, n_pool, PAGE_SIZE, IDX_DIM), 1.0),
        'state_conv': nrm((DEPTH, DEC_BATCH, CONV_W - 1, D_RNN), 1.0),
        'state_h': nrm((DEPTH, DEC_BATCH, D_RNN), 0.5),
        'page_table': page_table,
        'ln1': gain((DEPTH, D_MODEL)),
        'w_in': nrm((DEPTH, D_MODEL, D_IN), D_MODEL ** -0.5),
        'q_norm': gain((DEPTH, HEAD_DIM)),
        'k_norm': gain((DEPTH, HEAD_DIM)),
        'conv_w': nrm((DEPTH, CONV_W, D_RNN), CONV_W ** -0.5),
        'conv_b': nrm((DEPTH, D_RNN), 0.01),
        'w_a': nrm((DEPTH, N_RNN_BLOCKS, RNN_BLOCK, RNN_BLOCK), RNN_BLOCK ** -0.5),
        'b_a': nrm((DEPTH, D_RNN), 0.01),
        'w_x': nrm((DEPTH, N_RNN_BLOCKS, RNN_BLOCK, RNN_BLOCK), RNN_BLOCK ** -0.5),
        'b_x': nrm((DEPTH, D_RNN), 0.01),
        'lam': lam,
        'w_br_rnn': nrm((DEPTH, D_RNN, D_MODEL), D_RNN ** -0.5),
        'w_br_attn': nrm((DEPTH, ATTN_W, D_MODEL), ATTN_W ** -0.5),
        'w_out': nrm((DEPTH, D_MODEL, D_MODEL), D_MODEL ** -0.5),
        'ln2': gain((DEPTH, D_MODEL)),
        'w_rg': nrm((DEPTH, D_MODEL, N_GROUPS), D_MODEL ** -0.5),
        'b_rg': nrm((DEPTH, N_GROUPS), 0.01),
        'w_re': nrm((DEPTH, D_MODEL, N_EXPERTS), D_MODEL ** -0.5),
        'b_re': nrm((DEPTH, N_EXPERTS), 0.01),
        'w1': nrm((DEPTH, N_EXPERTS, D_MODEL, D_EXPERT), D_MODEL ** -0.5),
        'w3': nrm((DEPTH, N_EXPERTS, D_MODEL, D_EXPERT), D_MODEL ** -0.5),
        'w2': nrm((DEPTH, N_EXPERTS, D_EXPERT, D_MODEL), D_EXPERT ** -0.5),
        'ln3': gain((DEPTH, D_MODEL)),
        'w_ple_gate': nrm((DEPTH, D_MODEL, D_MODEL), D_MODEL ** -0.5),
        'w_ple_proj': nrm((DEPTH, PLE_DIM, D_MODEL), PLE_DIM ** -0.5),
    }

def reference(x_prompt, x_sample, p_prompt, p_sample, cache_k, cache_v, cache_kidx, state_conv, state_h,
              page_table, ln1, w_in, q_norm, k_norm, conv_w, conv_b, w_a, b_a, w_x, b_x, lam,
              w_br_rnn, w_br_attn, w_out, ln2, w_rg, b_rg, w_re, b_re, w1, w3, w2, ln3,
              w_ple_gate, w_ple_proj):
    bp, tp, _ = x_prompt.shape
    ts = x_sample.shape[1]
    past = page_table.shape[1] * PAGE_SIZE
    pos_p = jnp.arange(tp, dtype=jnp.int32)
    pos_s = past + jnp.arange(ts, dtype=jnp.int32)
    conv0 = jnp.zeros((bp, CONV_W - 1, D_RNN), x_prompt.dtype)
    h0 = jnp.zeros((bp, D_RNN), x_prompt.dtype)
    weights = (ln1, w_in, q_norm, k_norm, conv_w, conv_b, w_a, b_a, w_x, b_x, lam, w_br_rnn, w_br_attn,
               w_out, ln2, w_rg, b_rg, w_re, b_re, w1, w3, w2, ln3, w_ple_gate, w_ple_proj)
    yp, ys = x_prompt, x_sample
    st_p, st_s = [], []
    for i in range(DEPTH):
        lw = [w[i] for w in weights]
        yp, sp = _layer(yp, p_prompt[i], pos_p, conv0, h0, _prompt_attention, *lw)
        sample_attend = functools.partial(_sample_attention, cache_k=cache_k[i], cache_v=cache_v[i],
                                          cache_kidx=cache_kidx[i], page_table=page_table)
        ys, ss = _layer(ys, p_sample[i], pos_s, state_conv[i], state_h[i], sample_attend, *lw)
        st_p.append(sp)
        st_s.append(ss)

    def stack(sts, j):
        return jnp.stack([s[j] for s in sts])

    return (yp, ys, stack(st_p, 0), stack(st_p, 1), stack(st_p, 2), stack(st_p, 3), stack(st_p, 4),
            stack(st_s, 0), stack(st_s, 1), stack(st_s, 2), stack(st_s, 3), stack(st_s, 4))


_drawn_inputs = setup_inputs


def setup_inputs(seed=0):
    import zlib

    import numpy as np

    out = dict(_drawn_inputs(seed))
    spreads = {}
    factors = {'q_norm': 4.26, 'b_a': 24.297, 'b_x': 8.0, 'b_rg': 13.268, 'b_re': 3.571, 'ln3': 6.091}
    for name, (base, spread) in spreads.items():
        noise = np.random.default_rng([zlib.crc32(name.encode()), seed]).standard_normal(out[name].shape)
        drawn = base * np.exp(spread * noise) if base else spread * noise
        out[name] = __import__('jax').numpy.asarray(drawn.astype(out[name].dtype))
    for name, factor in factors.items():
        out[name] = (out[name] * factor).astype(out[name].dtype)
    return out
```

```python
from contextlib import ExitStack

import numpy as np

import concourse.bass as bass
from concourse import mybir

ALU = mybir.AluOpType
ACT = mybir.ActivationFunctionType
F32 = mybir.dt.float32
F32R = mybir.dt.float32r
I32 = mybir.dt.int32
AX_X = mybir.AxisListType.X

P = 128
D = 2048
KD = D // P
SEQ = 256
NB = 8
TS = 8
NS = NB * TS
T = SEQ + NS
TILES = [(0, 128), (128, 128), (256, 64)]
PAST = 1024
PAGE = 128
NPG = PAST // PAGE
HD = 64
NH = 16
NKV = 4
KVW = NKV * HD
NIH = 8
DR = 1024
CR = DR // P
CW = 4
NG = 4
EPG = 8
NE = NG * EPG
F = 256
PLE = 256
EPS = 1e-6
FMIN = -3.4028234663852886e38
BIG = 1e30
TOPK_P = SEQ // 4
TOPK_S = 256
KEYS = PAST + NS
QK_SCALE = HD ** -0.5
WI_SCALE = (HD ** -0.5) * (NIH ** -0.5)
O_XR, O_GR, O_Q = 0, DR, 2 * DR
O_K = O_Q + NH * HD
O_V = O_K + KVW
O_QI = O_V + KVW
O_KI = O_QI + NIH * HD
O_WI = O_KI + HD
O_GMR = O_WI + NIH
O_GMA = O_GMR + D
PAD = CW - 1
SEGB = PAD + TS
S0 = PAD + SEQ
XP = S0 + NB * SEGB
XC = XP - PAD
V_LN1, V_LN2, V_LN3, V_CW, V_CB, V_BA, V_BX, V_LAM, V_QN, V_KN = 0, 16, 32, 48, 80, 88, 96, 104, 112, 113
NV = 114


def constants():
    half = HD // 2
    inv = (10000.0 ** (-np.arange(half) / half)).astype(np.float32)
    pos = np.concatenate([np.arange(SEQ), np.tile(PAST + np.arange(TS), NB)]).astype(np.float32)
    ang = (inv[:, None] * pos[None, :]).astype(np.float64)
    d = np.arange(P)
    cos = np.cos(ang)[d % half]
    sin = np.sin(ang)[d % half]
    rot = np.zeros((P, P), np.float32)
    for i in range(P):
        if i % HD < half:
            rot[i + half, i] = -1.0
        else:
            rot[i - half, i] = 1.0
    bones = (d[:, None] // HD == d[None, :] // HD).astype(np.float32)
    ones = np.ones((P, P), np.float32)
    ident = np.eye(P, dtype=np.float32)
    utri = (d[:, None] <= d[None, :]).astype(np.float32)
    tri = (d[None, :] <= d[:, None]).astype(np.float32)
    trib = np.where(tri > 0, 0.0, FMIN).astype(np.float32)
    e8 = np.zeros((P, P), np.float32)
    for r in range(P):
        e8[(r % 64) // TS, r] = 1.0
    mpair = np.zeros((P, 4, NS), np.float32)
    for p in range(4):
        for r in range(P):
            mpair[r, p, (2 * p + r // 64) * TS + r % TS] = 1.0
    s = np.arange(NS)
    nk = np.zeros((P, NS), np.float32)
    nk[:NS] = (s[:, None] // TS == s[None, :] // TS) & (s[None, :] <= s[:, None])
    nkb = np.where(nk > 0, 0.0, FMIN).astype(np.float32)
    rep = np.zeros((P, NB, P), np.float32)
    for b in range(NB):
        for r in range(P):
            rep[b * TS + r % TS, b, r] = 1.0
    iota = np.tile(np.arange(1, P + 1, dtype=np.float32), (P, 1))
    parts = [("cos", cos), ("sin", sin), ("rot", rot), ("bones", bones), ("ones", ones), ("ident", ident),
             ("utri", utri), ("tri", tri), ("trib", trib), ("e8", e8), ("mpair", mpair.reshape(P, -1)),
             ("nk", nk), ("nkb", nkb), ("rep", rep.reshape(P, -1)), ("iota", iota)]
    at, n = {}, 0
    for name, a in parts:
        at[name] = (n, a.shape[1])
        n += a.shape[1]
    return np.concatenate([a for _, a in parts], 1).astype(np.float32), at


def plan():
    units, loads = [], []

    def load(*what):
        loads.append([what, None])
        return len(loads) - 1

    def unit(kind, i, ls):
        units.append((kind, i, ls))
        for n in ls:
            loads[n][1] = len(units) - 1

    for i in range(8):
        unit("q", i, [load("w_in", O_Q + P * i, P)])
    for i in range(2):
        unit("k", i, [load("w_in", O_K + P * i, P)])
    for i in range(4):
        unit("qi", i, [load("w_in", O_QI + P * i, P)])
    n = load("w_in", O_KI, HD + NIH)
    unit("ki", 0, [n])
    unit("wi", 0, [n])
    va, vb = load("v", 0), load("v", 1)
    for i in range(3):
        unit("v", i, [va, vb])
    for c in range(CR):
        unit("xr", c, [load("w_in", O_XR + P * c, P)])
        unit("gr", c, [load("w_in", O_GR + P * c, P)])
        if c:
            unit("ga", c - 1, [])
            unit("gx", c - 1, [])
    unit("ga", CR - 1, [])
    unit("gx", CR - 1, [])
    for j0 in range(0, KD, 4):
        for j in range(j0, j0 + 4):
            unit("gmr", j, [load("w_in", O_GMR + P * j, P)])
        for j in range(j0, j0 + 4, 2):
            n = load("w_br_rnn", P * j)
            unit("brr", j, [n])
            unit("brr", j + 1, [n])
    for j in range(KD):
        unit("gma", j, [load("w_in", O_GMA + P * j, P)])
    for j in range(0, KD, 2):
        n = load("w_br_attn", P * j)
        unit("bra", j, [n])
        unit("bra", j + 1, [n])
    for j in range(KD):
        unit("out", j, [load("w_out", P * j)])
    return units, loads


def schedule(units):
    first = next(i for i, u in enumerate(units) if u[0] == "xr")
    last = next(i for i, u in enumerate(units) if u[0] == "bra")
    fill = list(range(first, last))
    steps = []

    def u():
        work = 0
        while fill and work < 2:
            n = fill.pop(0)
            work += {"brr": 1, "ga": 0, "gx": 0}.get(units[n][0], 2)
            steps.append(("unit", n))

    for qt in range(2):
        steps.append(("pi", qt))
        u()
    for x in range(13):
        if x < 12:
            steps.append(("si_t", x))
        if x:
            steps.append(("si_w", x - 1))
        if x % 3 < 2:
            u()
        if x < 12:
            steps.append(("si_s", x))
    steps.append(("sc", 0))
    u()
    u()
    rounds = iter(range(TOPK_S // 8))

    def top(n):
        for _ in range(n):
            steps.append(("tk", next(rounds)))

    for m in range(8):
        steps.append(("pa_l", m))
        top(1)
        u()
        steps.append(("pa_t", m))
        top(2)
        u()
        steps.append(("pa_v", m))
        top(1)
        if m == 0:
            steps.append(("ptk", 1))
    steps.append(("sel", 0))
    for b in range(NB):
        steps.append(("sa_t", b))
        u()
        steps.append(("sa_l", b))
        u()
        steps.append(("sa_p", b))
        u()
        steps.append(("sa_v", b))
    while fill:
        u()
    return steps


def vector_order(steps, units):
    out, held = [], []
    for what, i in steps:
        if what == "unit":
            held.append((what, i))
            if units[i][0] in ("ga", "gx"):
                out += held
                held = []
        elif what in ("pa_t", "pa_v", "sa_l", "sa_p", "sa_v"):
            out += [(what, i)] + held
            held = []
        elif what in ("tk", "sa_t"):
            out.append((what, i))
        else:
            out += held + [(what, i)]
            held = []
    return out + held


def expert_slot(m):
    if m < 4:
        return "up", 0, m
    e, q = divmod(m - 4, 6)
    if e == EPG - 1:
        return "down", e, q
    return ("up", e + 1, q) if q < 4 else ("down", e, q - 4)


def used_up(e):
    return 4 if e == 0 else 6 * e + 2


def turned(e):
    return 6 * e + 5 if e < EPG - 1 else 6 * EPG - 3


def build_program(nc, A, O):
    units, loads = plan()
    steps = schedule(units)
    _, const_at = constants()
    unit_at = {(k, i): n for n, (k, i, _) in enumerate(units)}
    n_front = unit_at[("xr", 0)]
    first_bra = unit_at[("bra", 0)]
    first_out = unit_at[("out", 0)]
    ropes = [("q", i) for i in range(8)] + [("k", 0), ("k", 1)] + [("qi", i) for i in range(4)] + [("ki", 0)]
    RING = 4
    MRING = 6
    STG = 3
    PER = 48
    GSPILL = KD - 4

    with ExitStack() as ctx:
        def sem(name):
            return ctx.enter_context(nc.semaphore(name))

        ARENA = 53200
        base = nc.sbuf_base
        arena = ctx.enter_context(nc.sbuf_tensor("arena", [P, ARENA], F32))
        base = (base + 31) // 32 * 32
        psum = ctx.enter_context(nc.psum_tensor("psum", [P, 8, 512], F32))
        flags_i = ctx.enter_context(nc.sbuf_tensor("flags_i", [1, 4], I32))
        x_spill = nc.dram_tensor("x_spill", [P, KD * T], F32, kind="Internal").ap()
        gate_spill = nc.dram_tensor("gate_spill", [P, GSPILL * T], F32, kind="Internal").ap()
        top = [0]

        def take(n):
            at = top[0]
            top[0] += (n + 7) // 8 * 8
            assert top[0] <= ARENA, (top[0], ARENA)
            return arena[:, at:at + n]

        def halves(name, at, n):
            return [nc.alloc_sbuf_tensor_at(f"{name}_{w}", [P, n], F32R, offset=base + 4 * (at + n * i))
                    for i, w in enumerate(("high", "low"))]

        def parts3(a, b):
            return ((a[0], b[0]), (a[0], b[1]), (a[1], b[0]))

        slots = [take(2048) for _ in range(RING)]
        n_const = sum(w for _, w in const_at.values())
        const = take(n_const)

        def C(name):
            at, w = const_at[name]
            return const[:, at:at + w]

        h_at = top[0]
        H = take(KD * T).rearrange("p (k t) -> p k t", k=KD)
        g_at = top[0]
        g_flat = take(KD * T)
        G = g_flat.rearrange("p (k t) -> p k t", k=KD)
        vec = take(NV)
        epsc = take(1)
        rstd = take(T)
        wr = take(KD * 36).rearrange("p (k n) -> p k n", k=KD)
        rb = take(36)
        pT = take(2 * T).rearrange("p (k t) -> p k t", k=2)
        shared = top[0]
        kraw = take(2048)
        vraw = take(2048)
        ktbuf = take(2 * KEYS)
        top_x = shared + 6144
        xtok = arena[:, shared:top_x].rearrange("p (t d) -> p t d", t=3)
        prob = take(KEYS)
        probT = take(9 * P)
        score = take(KEYS)
        sq = take(2 * T).rearrange("p (b t) -> p b t", b=2)
        ropeb = take(2 * T).rearrange("p (b t) -> p b t", b=2)
        qT = take(8 * T).rearrange("p (k t) -> p k t", k=8)
        kT = take(2 * T).rearrange("p (k t) -> p k t", k=2)
        kTs = take(2 * T).rearrange("p (k t) -> p k t", k=2)
        vtok = take(3 * KVW).rearrange("p (t d) -> p t d", t=3)
        qiT = take(4 * T).rearrange("p (k t) -> p k t", k=4)
        kiT = take(T)
        wiT = take(T)
        wtok = take(2 * NIH).rearrange("p (t h) -> p t h", t=2)
        wp = take(4 * NS).rearrange("p (a s) -> p a s", a=4)
        qz = take(2 * NB * P).rearrange("p (j b r) -> p j b r", j=2, b=NB)
        qiz = take(NB * 64).rearrange("p (b r) -> p b r", b=NB)
        pbias = [take(P), take(2 * P)]
        rnnT = take(CR * T).rearrange("p (c t) -> p c t", c=CR)
        wa = take(CR * P).rearrange("p (c j) -> p c j", c=CR)
        wx = take(CR * P).rearrange("p (c j) -> p c j", c=CR)
        xpad = take(2 * XP).rearrange("p (b t) -> p b t", b=2)
        xc = take(2 * XC).rearrange("p (b t) -> p b t", b=2)
        g_r, g_i, g_a, g_th, g_u = (take(XC) for _ in range(5))
        sgm = qiT
        stT = take(CR * 32).rearrange("p (c s) -> p c s", c=CR)
        tail = take(CR * 36).rearrange("p (c s) -> p c s", c=CR)
        sp8, nsp8 = take(CR), take(CR)
        spt = take(4 * CR).rearrange("p (a c) -> p a c", a=4)
        small = take(64)
        m8 = take(8)
        ptok = prob[:, 0:768].rearrange("p (t d) -> p t d", t=3)
        vec_raw = probT[:, 0:P]
        st_raw = score[:, 0:DR]
        tail_raw = qz.rearrange("p j b r -> p (j b r)")[:, 0:DR]
        kout = prob[:, 0:3 * 320].rearrange("p (t d) -> p t d", t=3)
        pi_tmp = vraw.rearrange("p (h k) -> p h k", h=NIH)
        kx_raw = kraw.rearrange("p (q b g d) -> p q b g d", q=2, b=2, g=NPG)
        kxT = ktbuf.rearrange("p (b k) -> p b k", b=2)
        srelu = prob[:, 0:1024].rearrange("p (q k) -> p q k", q=2)
        work = ktbuf[:, 0:KEYS]
        eqb = ktbuf[:, KEYS:2 * KEYS]
        k_r = kraw.rearrange("p (g d) -> p g d", g=NPG)
        v_r = vraw.rearrange("p (g d) -> p g d", g=NPG)
        KT = ktbuf.rearrange("p (j k) -> p j k", j=2)
        probT3 = probT.rearrange("p (g r) -> p g r", g=9)
        pT4 = probT[:, 0:1024].rearrange("p (k h q) -> p k h q", k=2, h=4)
        t1, t2 = sq[:, 0, :], sq[:, 1, :]
        top[0] = shared
        XT = take(KD * T).rearrange("p (k t) -> p k t", k=KD)
        gback = arena[:, top[0]:top[0] + GSPILL * T].rearrange("p (k t) -> p k t", k=GSPILL)
        htok = take(3 * D).rearrange("p (t d) -> p t d", t=3)
        mslots = slots + [take(2048) for _ in range(MRING - RING)]
        stage = []
        for i in range(STG):
            stage.append(halves(f"weights_{i}", top[0], 2048))
            take(4096)
        sq2 = take(2 * T).rearrange("p (b t) -> p b t", b=2)
        lg = take(3 * 36).rearrange("p (t n) -> p t n", t=3)
        rt = [take(3 * 32).rearrange("p (t n) -> p t n", t=3) for _ in range(5)]
        gates = take(3 * NE).rearrange("p (t n) -> p t n", t=3)
        goh = take(3 * NG).rearrange("p (t n) -> p t n", t=3)
        pos = take(3 * NG).rearrange("p (t n) -> p t n", t=3)
        r1 = [take(12).rearrange("p (t n) -> p t n", t=3) for _ in range(6)]
        v8 = take(24).rearrange("p (t n) -> p t n", t=3)
        w4 = take(4)
        fl = take(32)
        pc = take(3)
        gg = take(NE)
        geg = take(EPG)
        outst = g_flat[:, 0:2048]
        S = g_flat[:, 2048:2048 + 384].rearrange("p (t s) -> p t s", t=3)
        ST = g_flat[:, 2432:2432 + T]
        silu = g_flat[:, 2752:2752 + 512].rearrange("p (b f) -> p b f", b=2)
        hid = g_flat[:, 3264:3264 + 512].rearrange("p (b f) -> p b f", b=2)
        hidT = [halves(f"hidden_{i}", g_at + 3776 + 512 * i, F) for i in range(2)]
        proj = g_flat[:, 0:4096].rearrange("p (k n) -> p k n", k=2)
        plg = g_flat[:, 4096:4096 + 2 * T].rearrange("p (b t) -> p b t", b=2)
        hg = halves("gathered", h_at, 2048)
        ytok = htok

        ident = C("ident")

        def bank(b, n=512):
            return psum[:, b, 0:n]

        consts_in, vecs_in, x_in, gates_in, router_in, ple_in = (sem(n) for n in (
            "consts_in", "vecs_in", "x_in", "gates_in", "router_in", "ple_in"))
        wfull = [sem(f"weights_in_{i}") for i in range(RING)]
        mfull = [sem(f"expert_weights_in_{i}") for i in range(MRING)]
        tfull = [sem(f"extra_weights_in_{i}") for i in range(MRING)]
        states_out = sem("states_out")
        kx_in = [sem("index_keys_in_0"), sem("index_keys_in_1")]
        k_in, v_in, spill_out, spill_in, proj_in, outs_out = (sem(n) for n in (
            "keys_in", "values_in", "spill_out", "spill_in", "proj_in", "outs_out"))
        zeroed, pre_t, pre_cp, xt_mm, xt_cp, p_mm, p_cp, st_mm = (sem(n) for n in (
            "gates_zeroed", "pre_transposed", "pre_copied", "x_transposed", "x_copied", "p_transposed", "p_copied",
            "states_transposed"))
        sq_ready, ss_mm, var_ready, rstd_ready, h_ready = (sem(n) for n in (
            "squares_ready", "sums_done", "variance_ready", "rstd_ready", "h_ready"))
        acc_ready = sem("acc_ready")
        acc_free = [sem("acc_free_0"), sem("acc_free_1")]
        rope_mm, rope_var, rope_rstd, rope_out = (sem(n) for n in ("rope_mm", "rope_var", "rope_rstd", "rope_out"))
        wi_mm, wi_done, kout_mm, kout_cp, prep_done = (sem(n) for n in (
            "wi_mm", "wi_done", "kout_mm", "kout_copied", "prep_done"))
        lam_act, lam_dve = sem("lam_act"), sem("lam_dve")
        conv_ready, lru_a, lru_w, lru_s, lru_done = (sem(n) for n in (
            "conv_ready", "decay_ready", "gain_sq_ready", "gain_ready", "lru_done"))
        pi_mm, pi_read, pi_red, si_tmm, kx_cp, kx_dup, si_smm, si_relu, si_wmm, sc_read = (sem(n) for n in (
            "pi_mm", "pi_read", "pi_reduced", "si_transposed", "kx_copied", "kx_doubled", "si_scores", "si_relu",
            "si_weighted", "scores_read"))
        pbias_ready, sbias_ready = sem("pbias_ready"), sem("sbias_ready")
        pa_lmm, pa_lg, pa_nb, pa_exp, pa_prob, pa_tmm, pa_pT, pa_vmm, pa_out = (sem(n) for n in (
            "pa_logits", "pa_logits_read", "pa_max", "pa_exp", "pa_prob", "pa_transposed", "pa_probT", "pa_pv",
            "pa_out"))
        sa_tmm, sa_kcp, sa_lmm, sa_nb, sa_exp, sa_prob, sa_pmm, sa_pT, sa_vmm, sa_out = (sem(n) for n in (
            "sa_keys_transposed", "sa_keys_copied", "sa_logits", "sa_max", "sa_exp", "sa_prob", "sa_transposed",
            "sa_probT", "sa_pv", "sa_out"))
        mix_ready, tail_mm, tail_cp = sem("mix_ready"), sem("states_out_mm"), sem("states_out_copied")
        ht_mm, ht_cp, rl_mm, rl_a, rl_e, rl_x, goh_ready, cum_mm, router_done = (sem(n) for n in (
            "h2_transposed", "h2_copied", "router_logits", "router_shifted", "router_exp", "router_parts", "group_onehot_ready",
            "group_counted", "router_done"))

        def pass_sems(w):
            return {n: sem(f"{w}_{n}") for n in (
                "used", "select", "st_mm", "st_cp", "hg_mm", "hg_cp", "silu", "hid", "tr", "hT", "oa", "ob",
                "sc_mm", "sc_add", "places", "gates", "split", "high", "hg_hi", "hT_hi")}

        main, extra = pass_sems("main"), pass_sems("extra")
        ple_g, ple_p, ple_sg, ple_y, ple_t, ple_o = (sem(n) for n in (
            "ple_gate_mm", "ple_proj_mm", "ple_sigmoid", "ple_y", "ple_transposed", "ple_copied"))
        experts_done = sem("experts_done")
        act_chain, dve_chain = sem("act_chain"), sem("dve_chain")
        block = ctx.enter_context(nc.Block())

        def freed(u):
            return acc_free[u % 2], u // 2 + 1

        def tokens(ap, b):
            return ap[..., SEQ + TS * b:SEQ + TS * (b + 1)]

        def second_pe(pe, sum_sq):
            mm = nc.tensor.matmul
            pe.wait_ge(*freed(len(units) - 1))
            for k in range(KD):
                sum_sq(1, k)
            pe.wait_ge(router_in, 64)
            pe.wait_ge(h_ready, 2 * KD)
            for tt, (t0, n) in enumerate(TILES):
                for k in range(KD):
                    last = mm(bank(2)[0:n, 64 * tt:64 * tt + 36], H[:, k, t0:t0 + n], wr[:, k, :], start=(k == 0),
                              stop=(k == KD - 1))
            last.then_inc(rl_mm, 1)
            for n_ in range(12):
                tt, q = divmod(n_, 4)
                t0, n = TILES[tt]
                if n_ >= 4:
                    pe.wait_ge(ht_cp, n_ - 3)
                for a in range(4):
                    last = nc.tensor.transpose(bank(4 + n_ % 4)[0:n, P * a:P * (a + 1)], H[:, 4 * q + a, t0:t0 + n],
                                               ident)
                last.then_inc(ht_mm, 1)
            pe.wait_ge(goh_ready, 2)
            for tt, (t0, n) in enumerate(TILES):
                for t2 in range(tt + 1):
                    n2 = TILES[t2][1]
                    mm(bank(3)[0:n, NG * tt:NG * (tt + 1)], (C("utri") if t2 == tt else C("ones"))[0:n2, 0:n],
                       goh[0:n2, t2, :], start=(t2 == 0), stop=(t2 == tt))
            for t2 in range(3):
                n2 = TILES[t2][1]
                last = mm(bank(3)[:, 16:20], C("ones")[0:n2, :], goh[0:n2, t2, :], start=(t2 == 0), stop=(t2 == 2))
            last.then_inc(cum_mm, 1)
            pe.wait_ge(router_done, 1)
            pe.wait_ge(ht_cp, 12)

            def experts(s, g):
                pe.wait_ge(s["select"], g + 1)
                for tt, (t0, n) in enumerate(TILES):
                    nc.tensor.transpose(bank(3)[:, t0:t0 + n], S[0:n, tt, :], ident[0:n, 0:n])
                for tt, (t0, n) in enumerate(TILES):
                    last = mm(bank(3)[:, T:T + NE], S[0:n, tt, :], gates[0:n, tt, :], start=(tt == 0), stop=(tt == 2))
                last.then_inc(s["st_mm"], 1)
                for q in range(4):
                    if q == 3:
                        pe.wait_ge(s["st_cp"], g + 1)
                    for a in range(4):
                        for tt, (t0, n) in enumerate(TILES):
                            k = 4 * q + a
                            last = mm(bank(q)[:, P * a:P * (a + 1)], htok[0:n, tt, P * k:P * (k + 1)], S[0:n, tt, :],
                                      start=(tt == 0), stop=(tt == 2))
                    last.then_inc(s["hg_mm"], 1)

                def take_slot(m):
                    pe.wait_ge(s["split"], MRING + g * PER + m + 1)
                    return stage[m % STG]

                def up(e, quarters):
                    for q in quarters:
                        m = q if e == 0 else 4 + 6 * (e - 1) + q
                        w = take_slot(m)
                        if e == 0:
                            pe.wait_ge(s["hg_cp"], g * 4 + q + 1)
                        for k in range(4):
                            c = P * (4 * q + k)
                            for n, (x, y) in enumerate(parts3(hg, w)):
                                last = mm(bank(e % 2), x[:, c:c + P], y[:, 512 * k:512 * (k + 1)],
                                          start=(q == 0 and k == 0 and n == 0), stop=(q == 3 and k == 3 and n == 2))
                        last.then_inc(s["used"], 1)

                def turn(e):
                    pe.wait_ge(s["hid"], g * EPG + e + 1)
                    for k in range(2):
                        last = nc.tensor.transpose(bank(2)[:, P * k:P * (k + 1)], hid[:, e % 2, P * k:P * (k + 1)],
                                                   ident)
                    last.then_inc(s["tr"], 1)

                def down(e):
                    pe.wait_ge(s["hT"], g * EPG + e + 1)
                    for k in range(2):
                        w = take_slot(4 + 6 * e + (4 if e < EPG - 1 else 0) + k)
                        for n in range(4):
                            for a, (x, y) in enumerate(parts3(hidT[e % 2], w)):
                                last = mm(bank(4 + n), x[:, P * k:P * (k + 1)], y[:, 512 * n:512 * (n + 1)],
                                          start=(e == 0 and k == 0 and a == 0),
                                          stop=(e == EPG - 1 and k == 1 and a == 2))
                        last.then_inc(s["used"], 1)

                up(0, range(4))
                for e in range(EPG):
                    if e < EPG - 1:
                        up(e + 1, (0, 1))
                    turn(e)
                    if e < EPG - 1:
                        up(e + 1, (2, 3))
                    down(e)
                pe.wait_ge(s["oa"], g + 1)
                pe.wait_ge(s["ob"], g + 1)
                for d in range(KD):
                    if d >= 2:
                        pe.wait_ge(s["sc_add"], g * KD + d - 1)
                    mm(bank(2 + d % 2, T), outst[:, P * d:P * (d + 1)], ST[:], start=True,
                       stop=True).then_inc(s["sc_mm"], 1)
                pe.wait_ge(s["sc_add"], g * KD + KD)

            pe.sem_inc(main["used"], STG)
            with pe.Fori(0, NG) as g:
                experts(main, g)
            more = pe.value_load(flags_i[0:1, 0:1], min_val=0, max_val=2)
            with pe.If(more > 0):
                pe.sem_inc(extra["used"], STG)
                experts(extra, 0)
                with pe.If(more > 1):
                    experts(extra, 1)

            for k in range(KD):
                sum_sq(2, k)
            pe.wait_ge(h_ready, 3 * KD)
            pe.wait_ge(proj_in, 16)

            def back(j):
                pe.wait_ge(ple_y, j + 1)
                q, a = divmod(j, 4)
                if a == 0 and q:
                    pe.wait_ge(ple_o, 3 * q)
                for tt, (t0, n) in enumerate(TILES):
                    last = nc.tensor.transpose(bank(4 + tt)[0:n, P * a:P * (a + 1)], plg[:, j % 2, t0:t0 + n], ident)
                last.then_inc(ple_t, 1)

            for j in range(KD):
                if j >= 2:
                    pe.wait_ge(ple_y, j - 1)
                pe.wait_ge(mfull[j % MRING], PER * NG // MRING * 32 + 16 * (j // MRING + 1))
                w = mslots[j % MRING].rearrange("p (k c) -> p k c", k=KD)
                for k in range(2):
                    last = mm(bank(2 + j % 2, T), proj[:, k, P * j:P * (j + 1)], pT[:, k, :], start=(k == 0),
                              stop=(k == 1))
                for k in range(KD):
                    last = mm(bank(j % 2, T), w[:, k, :], H[:, k, :], start=(k == 0), stop=(k == KD - 1))
                last.then_inc(ple_g, 1)
                if j:
                    back(j - 1)
            back(KD - 1)

        def second_act(act, squares, root):
            for k in range(KD):
                act.wait_ge(*freed(first_out + k))
                squares(1, k, XT[:, k, :])
            root(1)

            def ht(n_):
                tt, q = divmod(n_, 4)
                n = TILES[tt][1]
                act.wait_ge(ht_mm, n_ + 1)
                nc.scalar.activation(htok[0:n, tt, 512 * q:512 * (q + 1)], bank(4 + n_ % 4)[0:n, :],
                                     ACT.Identity).then_inc(ht_cp, 1)

            act.wait_ge(states_out, 64)
            act.wait_ge(rl_a, 1)
            for n in (P, NS):
                sl = slice(0, 2) if n == P else slice(2, 3)
                nc.scalar.activation(r1[1][0:n, sl, :], r1[1][0:n, sl, :], ACT.Exp).then_inc(rl_e, 1)
            for n_ in range(12):
                ht(n_)
                if n_ == 3:
                    act.wait_ge(rl_a, 2)
                    for n in (P, NS):
                        sl = slice(0, 2) if n == P else slice(2, 3)
                        nc.scalar.activation(rt[2][0:n, sl, :], rt[2][0:n, sl, :], ACT.Exp).then_inc(rl_e, 1)

            def experts(s, g, full, first):
                def high(m):
                    if m < PER:
                        act.wait_ge(full[m % MRING], first(m))
                        act.wait_ge(s["used"], g * PER + m + 1)
                        nc.scalar.activation(stage[m % STG][0][:], mslots[m % MRING], ACT.Identity
                                             ).then_inc(s["high"], 1)

                for m in range(STG):
                    high(m)
                for q in range(4):
                    act.wait_ge(s["hg_mm"], g * 4 + q + 1)
                    nc.scalar.activation(hg[0][:, 512 * q:512 * (q + 1)], bank(q), ACT.Identity
                                         ).then_inc(s["hg_hi"], 1)
                for m in range(PER):
                    for e in range(EPG):
                        if m == used_up(e) - 1:
                            act.wait_ge(s["used"], g * PER + STG + used_up(e))
                            nc.scalar.activation(silu[:, e % 2, :], bank(e % 2)[:, 0:F], ACT.Silu
                                                 ).then_inc(s["silu"], 1)
                        if m == turned(e):
                            act.wait_ge(s["tr"], g * EPG + e + 1)
                            nc.scalar.activation(hidT[e % 2][0][:], bank(2)[:, 0:F], ACT.Identity
                                                 ).then_inc(s["hT_hi"], 1)
                    high(m + STG)
                act.wait_ge(s["used"], g * PER + STG + PER)
                nc.scalar.activation(outst[:, 0:1024], psum[:, 4:6, :].rearrange("p a b -> p (a b)"),
                                     ACT.Identity).then_inc(s["oa"], 1)

            with act.Fori(0, NG) as g:
                experts(main, g, mfull, lambda m: g * (PER // MRING * 32) + 32 * (m // MRING + 1))
            more = act.value_load(flags_i[0:1, 0:1], min_val=0, max_val=2)
            with act.If(more > 0):
                experts(extra, 0, tfull, lambda m: 32 * (m // MRING + 1))
                with act.If(more > 1):
                    experts(extra, 1, tfull, lambda m: PER // MRING * 32 + 32 * (m // MRING + 1))
            for k in range(KD):
                act.wait_ge(experts_done, 1)
                squares(2, k, XT[:, k, :])
            root(2)
            for j in range(KD):
                act.wait_ge(ple_g, j + 1)
                if j >= 2:
                    act.wait_ge(ple_y, j - 1)
                nc.scalar.activation(sq2[:, j % 2, :], bank(j % 2, T), ACT.Sigmoid).then_inc(ple_sg, 1)
                if j % 4 == 0 and j:
                    turn_out(act, j // 4 - 1)
            turn_out(act, 3)

        def turn_out(act, q):
            act.wait_ge(ple_t, 4 * q + 4)
            for tt, (t0, n) in enumerate(TILES):
                nc.scalar.activation(ytok[0:n, tt, 512 * q:512 * (q + 1)], bank(4 + tt)[0:n, :],
                                     ACT.Identity).then_inc(ple_o, 1)

        def second_dve(dve, link, normalise):
            v = nc.vector
            for k in range(KD):
                dve.wait_ge(*freed(first_out + k))
            normalise(1, XT, V_LN2)
            dve.wait_ge(router_in, 64)
            dve.wait_ge(rl_mm, 1)
            parts = [(P, slice(0, 2), 2), (NS, slice(2, 3), 1)]
            lgp = bank(2)[:, 0:192].rearrange("p (t n) -> p t n", t=3)
            gmax, gexp, gsum, eqs, r_a, r_b = r1

            def wide(ap, n):
                return ap.broadcast_to((ap.shape[0], ap.shape[1], n))

            link(v.memset(pos[:], 0.0))
            link(v.tensor_scalar(w4[:], C("iota")[:, 0:4], -1.0, 5.0, ALU.mult, ALU.add))
            for n, sl, nt in parts:
                biasb = rb[0:n].rearrange("p (t k) -> p t k", t=1).broadcast_to((n, nt, 36))
                link(v.tensor_tensor(lg[0:n, sl, :], lgp[0:n, sl, 0:36], biasb, ALU.add))
                link(v.tensor_reduce(gmax[0:n, sl, 0:1], lg[0:n, sl, 0:NG], AX_X, ALU.max))
                v.tensor_tensor(gexp[0:n, sl, :], lg[0:n, sl, 0:NG], wide(gmax[0:n, sl, 0:1], NG), ALU.subtract
                                ).then_inc(rl_x, 1)
            dve.wait_ge(rl_x, 2)
            link(v.memset(geg[:], 0.0))
            v.memset(gg[:], 0.0).then_inc(rl_a, 1)
            for n, sl, nt in parts:
                link(v.tensor_tensor(eqs[0:n, sl, :], lg[0:n, sl, 0:NG], wide(gmax[0:n, sl, 0:1], NG), ALU.is_equal))
                w4b = w4[0:n].rearrange("p (t k) -> p t k", t=1).broadcast_to((n, nt, NG))
                link(v.tensor_tensor(eqs[0:n, sl, :], eqs[0:n, sl, :], w4b, ALU.mult))
                link(v.tensor_reduce(r_a[0:n, sl, 0:1], eqs[0:n, sl, :], AX_X, ALU.max))
                v.tensor_tensor(goh[0:n, sl, :], eqs[0:n, sl, :], wide(r_a[0:n, sl, 0:1], NG),
                                ALU.is_equal).then_inc(goh_ready, 1)
            dve.wait_ge(goh_ready, 2)
            em, gt, pe_, eq, cum = rt
            for n, sl, nt in parts:
                link(v.tensor_scalar(r_b[0:n, sl, :], goh[0:n, sl, :], BIG, -BIG, ALU.mult, ALU.add))
                for t in range(sl.start, sl.stop):
                    link(v.tensor_tensor(em[0:n, t, :].rearrange("p (g e) -> p g e", g=NG),
                                         lg[0:n, t, NG:36].rearrange("p (g e) -> p g e", g=NG),
                                         r_b[0:n, t, :].rearrange("p (g e) -> p g e", e=1).broadcast_to((n, NG, EPG)),
                                         ALU.add))
                    link(v.max(v8[0:n, t, :], em[0:n, t, :]))
                v.tensor_tensor(pe_[0:n, sl, :], em[0:n, sl, :], wide(v8[0:n, sl, 0:1], NE), ALU.subtract
                                ).then_inc(rl_x, 1)
            dve.wait_ge(rl_x, 4)
            v.memset(gg[:], 0.0).then_inc(rl_a, 1)
            for n, sl, nt in parts:
                link(v.tensor_tensor(gt[0:n, sl, :], em[0:n, sl, :], wide(v8[0:n, sl, 1:2], NE), ALU.is_gt))
                link(v.tensor_tensor(eq[0:n, sl, :], em[0:n, sl, :], wide(v8[0:n, sl, 1:2], NE), ALU.is_equal))
                link(v.tensor_reduce(r_a[0:n, sl, 0:1], gt[0:n, sl, :], AX_X, ALU.add))
                link(v.tensor_scalar(r_a[0:n, sl, 0:1], r_a[0:n, sl, 0:1], -1.0, 2.0, ALU.mult, ALU.add))
                for t in range(sl.start, sl.stop):
                    link(v.tensor_tensor_scan(cum[0:n, t, :], eq[0:n, t, :], eq[0:n, t, :], 0.0, ALU.add, ALU.bypass))
                link(v.tensor_tensor(cum[0:n, sl, :], cum[0:n, sl, :], wide(r_a[0:n, sl, 0:1], NE), ALU.is_le))
                link(v.tensor_tensor(cum[0:n, sl, :], cum[0:n, sl, :], eq[0:n, sl, :], ALU.mult))
                link(v.tensor_tensor(gt[0:n, sl, :], gt[0:n, sl, :], cum[0:n, sl, :], ALU.add))
            dve.wait_ge(rl_e, 4)
            for n, sl, nt in parts:
                link(v.tensor_tensor(gates[0:n, sl, :], pe_[0:n, sl, :], gt[0:n, sl, :], ALU.mult))
                link(v.tensor_reduce(r_a[0:n, sl, 0:1], gates[0:n, sl, :], AX_X, ALU.add))
                link(v.tensor_reduce(gsum[0:n, sl, 0:1], gexp[0:n, sl, :], AX_X, ALU.add))
                link(v.tensor_tensor(r_a[0:n, sl, 0:1], r_a[0:n, sl, 0:1], gsum[0:n, sl, 0:1], ALU.mult))
                link(v.reciprocal(r_a[0:n, sl, 0:1], r_a[0:n, sl, 0:1]))
                link(v.tensor_tensor(gates[0:n, sl, :], gates[0:n, sl, :], wide(r_a[0:n, sl, 0:1], NE), ALU.mult))
            dve.wait_ge(cum_mm, 1)
            for n, sl, nt in parts:
                link(v.tensor_tensor(pos[0:n, sl, :],
                                     bank(3)[:, 0:12].rearrange("p (t g) -> p t g", t=3)[0:n, sl, :],
                                     goh[0:n, sl, :], ALU.mult))
            cnt, more1, more2, a1, a2 = (fl[:, 4 * a:4 * a + 4] for a in range(5))
            out4 = fl[:, 20:24]
            link(v.tensor_copy(cnt, bank(3)[:, 16:20]))
            link(v.tensor_scalar(more1, cnt, float(P), None, ALU.is_gt))
            link(v.tensor_scalar(more2, cnt, 2.0 * P, None, ALU.is_gt))
            link(v.tensor_tensor(more2, more2, more1, ALU.add))
            link(v.tensor_reduce(out4[:, 0:1], more2, AX_X, ALU.add))
            link(v.tensor_tensor(a1, more1, w4[:], ALU.mult))
            link(v.tensor_tensor(a2, more1, C("iota")[:, 0:4], ALU.mult))
            link(v.tensor_reduce(out4[:, 1:2], a1, AX_X, ALU.max))
            link(v.tensor_reduce(out4[:, 2:3], a2, AX_X, ALU.max))
            link(v.tensor_scalar(out4[:, 1:2], out4[:, 1:2], -1.0, 4.0, ALU.mult, ALU.add))
            link(v.tensor_scalar(out4[:, 1:2], out4[:, 1:2], 3.0, None, ALU.min))
            link(v.tensor_scalar(out4[:, 2:3], out4[:, 2:3], -1.0, 0.0, ALU.add, ALU.max))
            link(v.tensor_tensor(fl[:, 24:25], out4[:, 1:2], out4[:, 2:3], ALU.is_equal))
            link(v.tensor_scalar(fl[:, 24:25], fl[:, 24:25], -float(P), -float(P), ALU.mult, ALU.add))
            link(v.tensor_copy(flags_i[0:1, 0:3], out4[0:1, 0:3]))
            v.memset(gg[:], 0.0).then_inc(router_done, 1)
            more = dve.value_load(flags_i[0:1, 0:1], min_val=0, max_val=2)
            groups = [dve.value_load(flags_i[0:1, n:n + 1], min_val=0, max_val=NG - 1) for n in (1, 2)]

            def experts(s, g, group, shift):
                def low(m):
                    if m < PER:
                        dve.wait_ge(s["high"], g * PER + m + 1)
                        hi, lo = stage[m % STG]
                        v.tensor_tensor(lo[:], mslots[m % MRING], hi[:].bitcast(F32), ALU.subtract
                                        ).then_inc(s["split"], 1)

                v.tensor_scalar(pc[:], pos[:, :, bass.ds(group, 1)].rearrange("p t a -> p (t a)"), shift, None,
                                ALU.add).then_inc(s["places"], 1)
                dve.wait_ge(s["places"], g + 1)
                for tt in range(3):
                    last = v.tensor_scalar(S[:, tt, :], C("iota"), pc[:, tt:tt + 1], None, ALU.is_equal)
                last.then_inc(s["select"], 1)
                for m in range(STG):
                    low(m)
                dve.wait_ge(s["st_mm"], g + 1)
                v.tensor_copy(ST[:], bank(3, T))
                v.tensor_copy(gg[:], bank(3)[:, T:T + NE]).then_inc(s["gates"], 1)
                dve.wait_ge(s["gates"], g + 1)
                v.tensor_copy(geg[:], gg[:, bass.ds(group * EPG, EPG)]).then_inc(s["st_cp"], 1)
                dve.wait_ge(s["st_cp"], g + 1)
                for q in range(4):
                    dve.wait_ge(s["hg_hi"], g * 4 + q + 1)
                    c = slice(512 * q, 512 * (q + 1))
                    v.tensor_tensor(hg[1][:, c], bank(q), hg[0][:, c].bitcast(F32), ALU.subtract
                                    ).then_inc(s["hg_cp"], 1)
                for m in range(PER):
                    for e in range(EPG):
                        if m == used_up(e) - 1:
                            dve.wait_ge(s["silu"], g * EPG + e + 1)
                            v.scalar_tensor_tensor(out=hid[:, e % 2, :], in0=bank(e % 2)[:, F:2 * F],
                                                   scalar=geg[:, e:e + 1], in1=silu[:, e % 2, :], op0=ALU.mult,
                                                   op1=ALU.mult).then_inc(s["hid"], 1)
                        if m == turned(e):
                            dve.wait_ge(s["hT_hi"], g * EPG + e + 1)
                            hi, lo = hidT[e % 2]
                            v.tensor_tensor(lo[:], bank(2)[:, 0:F], hi[:].bitcast(F32), ALU.subtract
                                            ).then_inc(s["hT"], 1)
                    low(m + STG)
                dve.wait_ge(s["used"], g * PER + STG + PER)
                v.tensor_copy(outst[:, 1024:2048], psum[:, 6:8, :].rearrange("p a b -> p (a b)")).then_inc(s["ob"], 1)
                for d in range(KD):
                    dve.wait_ge(s["sc_mm"], g * KD + d + 1)
                    v.tensor_tensor(XT[:, d, :], XT[:, d, :], bank(2 + d % 2, T), ALU.add).then_inc(s["sc_add"], 1)

            with dve.Fori(0, NG) as g:
                experts(main, g, g, 0.0)
            with dve.If(more > 0):
                experts(extra, 0, groups[0], -float(P))
                with dve.If(more > 1):
                    experts(extra, 1, groups[1], fl[:, 24:25])
            v.memset(gg[:], 0.0).then_inc(experts_done, 1)
            normalise(2, XT, V_LN3)
            for j in range(KD):
                dve.wait_ge(ple_sg, j + 1)
                if j >= 2:
                    dve.wait_ge(ple_t, j - 1)
                y = plg[:, j % 2, :]
                link(v.tensor_tensor(y, bank(2 + j % 2, T), sq2[:, j % 2, :], ALU.mult))
                v.tensor_tensor(y, y, XT[:, j, :], ALU.add).then_inc(ple_y, 1)

        def second_sp(sp):
            sp.wait_ge(acc_ready, first_out)
            sp.wait_ge(mix_ready, KD)
            sp.wait_ge(states_out, 64)
            sp.wait_ge(outs_out, 16 * 9)

            def expert_load(m, group, full, free, count):
                ring = len(full)
                slot = mslots[m % ring]
                sp.wait_ge(free, count)
                kind, e, q = expert_slot(m)
                if kind == "up":
                    dst = slot.rearrange("p (k w f) -> p k w f", k=4, w=2)
                    for w, name in enumerate(("w1", "w3")):
                        src = A[name][0, bass.ds(group * EPG + e, 1), 512 * q:512 * (q + 1), :].rearrange(
                            "a (k p) f -> p (a k) f", p=P)
                        sp.dma_start(dst[:, :, w, :], src).then_inc(full[m % ring], 16)
                else:
                    src = A["w2"][0, bass.ds(group * EPG + e, 1), P * q:P * (q + 1), :].rearrange(
                        "a p n -> p (a n)")
                    sp.dma_start(slot[:, 0:1024], src[:, 0:1024]).then_inc(full[m % ring], 16)
                    sp.dma_start(slot[:, 1024:2048], src[:, 1024:2048]).then_inc(full[m % ring], 16)

            sp.sem_inc(main["split"], MRING)
            sp.wait_ge(acc_ready, len(units))
            with sp.Fori(0, NG) as g:
                for m in range(PER):
                    expert_load(m, g, mfull, main["split"], g * PER + m + 1)

            sp.wait_ge(router_done, 1)
            more = sp.value_load(flags_i[0:1, 0:1], min_val=0, max_val=2)

            def tail_loads(n, which):
                group = sp.value_load(flags_i[0:1, which:which + 1], min_val=0, max_val=NG - 1)
                for m in range(PER):
                    expert_load(m, group, tfull, extra["split"], n * PER + m + 1)

            with sp.If(more > 0):
                sp.wait_ge(main["split"], MRING + PER * NG)
                sp.sem_inc(extra["split"], MRING)
                tail_loads(0, 1)
                with sp.If(more > 1):
                    tail_loads(1, 2)
                    sp.wait_ge(extra["split"], MRING + 2 * PER)
                with sp.If(more < 2):
                    sp.wait_ge(extra["split"], MRING + PER)

            for j in range(KD):
                if j < MRING:
                    sp.wait_ge(main["split"], PER * NG + j + 1)
                else:
                    sp.wait_ge(ple_g, j - MRING + 1)
                sp.dma_start(mslots[j % MRING].rearrange("p (k c) -> p k c", k=KD),
                             A["w_ple_gate"][0, :, P * j:P * (j + 1)].rearrange("(k p) c -> p k c", p=P)
                             ).then_inc(mfull[j % MRING], 16)
                if j == 5:
                    sp.wait_ge(ss_mm, 3 * KD)
                    sp.dma_start(proj, A["w_ple_proj"][0].rearrange("(k p) n -> p k n", p=P)).then_inc(proj_in, 16)
            for q in range(4):
                for tt, (t0, n) in enumerate(TILES):
                    sp.wait_ge(ple_o, 3 * q + tt + 1)
                    dst = O["y_prompt"][0, t0:t0 + n, 512 * q:512 * (q + 1)] if tt < 2 else O["y_sample"].rearrange(
                        "b t d -> (b t) d")[:, 512 * q:512 * (q + 1)]
                    sp.dma_start(dst, ytok[0:n, tt, 512 * q:512 * (q + 1)]).then_inc(outs_out, 16)
            sp.wait_ge(outs_out, 16 * (9 + 12))

        @block.sync
        def _(sp):
            sp.dma_start(const[:], A["consts"]).then_inc(consts_in, 16)
            for tt in range(2):
                sp.dma_start(xtok[:, tt, :], A["x_prompt"][0, P * tt:P * (tt + 1), :]).then_inc(x_in, 16)
            sp.dma_start(xtok[0:NS, 2, :], A["x_sample"].rearrange("b t d -> (b t) d")).then_inc(x_in, 16)
            rows = [("ln1", V_LN1, 16), ("ln2", V_LN2, 16), ("ln3", V_LN3, 16), ("conv_b", V_CB, 8), ("b_a", V_BA, 8),
                    ("b_x", V_BX, 8), ("lam", V_LAM, 8)]
            for name, at, n in rows:
                sp.dma_start(vec_raw[at:at + n, :], A[name][0].rearrange("(k p) -> k p", p=P)).then_inc(vecs_in, 16)
            sp.dma_start(vec_raw[V_CW:V_CW + 32, :],
                         A["conv_w"][0].rearrange("j (c p) -> (j c) p", p=P)).then_inc(vecs_in, 16)
            for name, at in (("q_norm", V_QN), ("k_norm", V_KN)):
                for hf in range(2):
                    sp.dma_start(vec_raw[at:at + 1, HD * hf:HD * (hf + 1)], A[name]).then_inc(vecs_in, 16)
            sp.dma_start(st_raw[0:24, :], A["state_conv"][0].rearrange("b j c -> (b j) c")).then_inc(vecs_in, 16)
            sp.dma_start(st_raw[24:32, :], A["state_h"][0]).then_inc(vecs_in, 16)

            def weight(n):
                what, _ = loads[n]
                s = slots[n % RING]
                if n >= RING:
                    sp.wait_ge(acc_ready, loads[n - RING][1] + 1)
                if what[0] == "w_in":
                    _, c0, w = what
                    dst = s.rearrange("p (k c) -> p k c", k=KD)[:, :, 0:w]
                    src = A["w_in"][0, :, c0:c0 + w].rearrange("(k p) c -> p k c", p=P)
                elif what[0] == "v":
                    dst = s.rearrange("p (k c) -> p k c", k=8)
                    src = A["w_in"][0, DR * what[1]:DR * (what[1] + 1), O_V:O_V + KVW].rearrange(
                        "(k p) c -> p k c", p=P)
                elif what[0] == "w_out":
                    dst = s.rearrange("p (k c) -> p k c", k=KD)
                    src = A["w_out"][0, :, what[1]:what[1] + P].rearrange("(k p) c -> p k c", p=P)
                else:
                    dst = s.rearrange("p (k c) -> p k c", k=8)
                    src = A[what[0]][0, :, what[1]:what[1] + 2 * P].rearrange("(k p) c -> p k c", p=P)
                sp.dma_start(dst, src).then_inc(wfull[n % RING], 16)

            for n in range(RING):
                weight(n)
            sp.wait_ge(zeroed, 1)
            for w, name in ((wa, "w_a"), (wx, "w_x")):
                for hf in range(2):
                    sp.dma_start(w[HD * hf:HD * (hf + 1), :, HD * hf:HD * (hf + 1)],
                                 A[name][0].rearrange("(c f) i j -> f i c j", f=2)[hf]).then_inc(gates_in, 16)
            sp.dma_start(wr[:, :, 0:NG], A["w_rg"][0].rearrange("(k p) n -> p k n", p=P)).then_inc(router_in, 16)
            sp.dma_start(wr[:, :, NG:NG + NE], A["w_re"][0].rearrange("(k p) n -> p k n", p=P)).then_inc(router_in, 16)
            sp.dma_start(rb[:, 0:NG], A["b_rg"].partition_broadcast(P)).then_inc(router_in, 16)
            sp.dma_start(rb[:, NG:NG + NE], A["b_re"].partition_broadcast(P)).then_inc(router_in, 16)
            sp.wait_ge(xt_cp, KD)
            sp.dma_start(x_spill, g_flat[:]).then_inc(spill_out, 16)
            front = next(n for n in range(len(loads)) if loads[n][1] >= unit_at[("gr", 1)])
            for n in range(RING, front):
                weight(n)
            sp.wait_ge(kout_cp, 3)
            for u in (unit_at[("v", 1)], unit_at[("v", 2)]):
                sp.wait_ge(*freed(u))
            for tt, (t0, n) in enumerate(TILES):
                w = "prompt" if tt < 2 else "sample"

                def dst(name, width):
                    if tt < 2:
                        return O[f"{name}_prompt"][0, 0, t0:t0 + n].rearrange(
                            "s h d -> s (h d)" if name != "kidx" else "s d -> s d")
                    return O[f"{name}_sample"][0].rearrange(
                        "b t h d -> (b t) (h d)" if name != "kidx" else "b t d -> (b t) d")

                sp.dma_start(dst("k", KVW), kout[0:n, tt, 0:KVW]).then_inc(outs_out, 16)
                sp.dma_start(dst("kidx", HD), kout[0:n, tt, KVW:KVW + HD]).then_inc(outs_out, 16)
                sp.dma_start(dst("v", KVW), vtok[0:n, tt, :]).then_inc(outs_out, 16)
            for n in range(front, len(loads)):
                weight(n)
                kind, j, _ = units[loads[n - RING][1]]
                if kind == "gma" and j < GSPILL:
                    sp.wait_ge(*freed(unit_at[("gma", j)]))
                    sp.wait_ge(spill_out, 16 * (j + 1))
                    sp.dma_start(gate_spill[:, T * j:T * (j + 1)], sgm[:, j % 4, :]).then_inc(spill_out, 16)
                    if j == GSPILL - 1:
                        sp.wait_ge(spill_out, 16 * (GSPILL + 1))
                        sp.wait_ge(sa_vmm, NB)
                        sp.dma_start(gback, gate_spill.rearrange("p (k t) -> p k t", k=GSPILL)).then_inc(spill_in, 16)
                        sp.dma_start(XT, x_spill.rearrange("p (k t) -> p k t", k=KD)).then_inc(spill_in, 16)
            sp.wait_ge(tail_cp, 2)
            sp.dma_start(O["conv_prompt"][0, 0], tail_raw[0:3, :]).then_inc(states_out, 16)
            sp.dma_start(O["conv_sample"][0].rearrange("b j c -> (b j) c"), tail_raw[3:27, :]).then_inc(states_out, 16)
            sp.dma_start(O["h_prompt"][0], tail_raw[27:28, :]).then_inc(states_out, 16)
            sp.dma_start(O["h_sample"][0], tail_raw[28:36, :]).then_inc(states_out, 16)
            second_sp(sp)

        @block.gpsimd
        def _(pool):
            nc.gpsimd.memset(wa[:], 0.0)
            nc.gpsimd.memset(wx[:], 0.0).then_inc(zeroed, 1)
            pool.dma_start(ptok[:, 0:2, :], A["p_prompt"][0, 0].rearrange("(t p) d -> p t d", p=P)).then_inc(ple_in, 16)
            pool.dma_start(ptok[0:NS, 2, :], A["p_sample"][0].rearrange("b t d -> (b t) d")).then_inc(ple_in, 16)
            nc.gpsimd.memset(qz[:], 0.0)
            nc.gpsimd.memset(qiz[:], 0.0)
            nc.gpsimd.memset(xpad[:], 0.0).then_inc(zeroed, 1)

            def page(b, g):
                return pool.value_load(A["page_table"][b:b + 1, g:g + 1], min_val=0, max_val=A["cache_k"].shape[1] - 1)

            for p in range(4):
                if p == 0:
                    pool.wait_ge(xt_cp, KD)
                if p >= 2:
                    pool.wait_ge(si_tmm, 2 * p - 2)
                for b2 in range(2):
                    for g in range(NPG):
                        r = page(2 * p + b2, g)
                        pool.dma_start(kx_raw[:, p % 2, b2, g, :],
                                       A["cache_kidx"][0, bass.ds(r, 1)].rearrange("a p d -> (a p) d")
                                       ).then_inc(kx_in[p % 2], 16)
            for b in range(NB):
                if b == 0:
                    pool.wait_ge(si_tmm, 8)
                else:
                    pool.wait_ge(sa_tmm, 4 * b)
                for g in range(NPG):
                    r = page(b, g)
                    pool.dma_start(k_r[:, g, :], A["cache_k"][0, bass.ds(r, 1)].rearrange("a p h d -> (a p) (h d)")
                                   ).then_inc(k_in, 16)
                if b == 0:
                    pool.wait_ge(pbias_ready, 2)
                else:
                    pool.wait_ge(sa_vmm, b)
                for g in range(NPG):
                    r = page(b, g)
                    pool.dma_start(v_r[:, g, :], A["cache_v"][0, bass.ds(r, 1)].rearrange("a p h d -> (a p) (h d)")
                                   ).then_inc(v_in, 16)

        @block.tensor
        def _(pe):
            mm = nc.tensor.matmul

            pe.wait_ge(consts_in, 16)
            pe.wait_ge(vecs_in, 16 * 14)
            nc.tensor.transpose(bank(2)[:, 0:NV], vec_raw[0:NV, :], ident[0:NV, 0:NV]).then_inc(pre_t, 1)
            for c in range(CR):
                last = nc.tensor.transpose(bank(3)[:, 32 * c:32 * c + 32], st_raw[0:32, P * c:P * (c + 1)],
                                           ident[0:32, 0:32])
            last.then_inc(pre_t, 1)
            pe.wait_ge(ple_in, 32)
            for k in range(2):
                for tt, (t0, n) in enumerate(TILES):
                    last = nc.tensor.transpose(bank(4 + k)[:, t0:t0 + n], ptok[0:n, tt, P * k:P * (k + 1)],
                                               ident[0:n, 0:n])
            last.then_inc(p_mm, 1)
            pe.wait_ge(x_in, 48)
            pe.wait_ge(p_cp, 1)

            def sum_sq(norm, k):
                pe.wait_ge(sq_ready, KD * norm + k + 1)
                mm(bank(1, T), C("ones"), (sq if norm == 0 else sq2)[:, k % 2, :], start=(k == 0),
                   stop=(k == KD - 1)).then_inc(ss_mm, 1)

            for k in range(KD):
                if k >= 4:
                    pe.wait_ge(xt_cp, k - 3)
                for tt, (t0, n) in enumerate(TILES):
                    last = nc.tensor.transpose(bank(4 + k % 4)[:, t0:t0 + n], xtok[0:n, tt, P * k:P * (k + 1)],
                                               ident[0:n, 0:n])
                last.then_inc(xt_mm, 1)
                if k >= 2:
                    sum_sq(0, k - 2)
            sum_sq(0, KD - 2)
            sum_sq(0, KD - 1)

            def unit(u):
                kind, i, ls = units[u]
                if u >= 2:
                    pe.wait_ge(acc_free[u % 2], u // 2)
                for n in ls:
                    pe.wait_ge(wfull[n % RING], 16 * (n // RING + 1))
                acc = bank(u % 2)
                if kind == "v":
                    t0, n = TILES[i]
                    wv = [slots[l % RING].rearrange("p (k c) -> p k c", k=8) for l in ls]
                    for k in range(KD):
                        last = mm(acc[0:n, 0:KVW], H[:, k, t0:t0 + n], wv[k // 8][:, k % 8, :], start=(k == 0),
                                  stop=(k == KD - 1))
                elif kind in ("ga", "gx"):
                    pe.wait_ge(conv_ready, i + 1)
                    last = mm(acc[:, 0:XC], (wa if kind == "ga" else wx)[:, i, :], xc[:, i % 2, :], start=True,
                              stop=True)
                elif kind in ("brr", "bra"):
                    if kind == "brr":
                        pe.wait_ge(lru_done, CR)
                    w = slots[ls[0] % RING].rearrange("p (k c) -> p k c", k=8)[:, :, P * (i % 2):P * (i % 2 + 1)]
                    for k in range(8):
                        last = mm(acc[:, 0:T], w[:, k, :], (rnnT if kind == "brr" else qT)[:, k, :], start=(k == 0),
                                  stop=(k == 7))
                else:
                    w = slots[ls[0] % RING].rearrange("p (k c) -> p k c", k=KD)
                    c0, m = {"ki": (0, HD), "wi": (HD, NIH)}.get(kind, (0, P))
                    for k in range(KD):
                        if u == 0:
                            pe.wait_ge(h_ready, k + 1)
                        if kind == "out" and i == 0:
                            pe.wait_ge(mix_ready, k + 1)
                        last = mm(acc[0:m, 0:T], w[:, k, c0:c0 + m], (G if kind == "out" else H)[:, k, :],
                                  start=(k == 0), stop=(k == KD - 1))
                last.then_inc(acc_ready, 1)

            def rope(t):
                kind, i = ropes[t]
                u = unit_at[(kind, i)]
                pe.wait_ge(*freed(u))
                if t >= 2:
                    pe.wait_ge(rope_out, t - 1)
                m = HD if kind == "ki" else P
                if kind in "qk":
                    mm(bank(2 + 2 * (t % 2), T), C("bones"), sq[:, t % 2, :], start=True, stop=True)
                mm(bank(3 + 2 * (t % 2))[0:m, 0:T], C("rot")[0:m, 0:m], ropeb[0:m, t % 2, :], start=True,
                   stop=True).then_inc(rope_mm, 1)

            for t in range(len(ropes)):
                unit(unit_at[ropes[t]])
                if t:
                    rope(t - 1)
            unit(unit_at[("wi", 0)])
            rope(len(ropes) - 1)
            for i in range(3):
                unit(unit_at[("v", i)])
            pe.wait_ge(*freed(unit_at[("wi", 0)]))
            pe.wait_ge(rope_out, len(ropes))
            for qt in range(2):
                nc.tensor.transpose(bank(2)[:, NIH * qt:NIH * (qt + 1)], wiT[0:NIH, P * qt:P * (qt + 1)],
                                    ident[0:NIH, 0:NIH])
            mm(bank(3)[:, 0:NS], C("e8")[0:NIH, :], wiT[0:NIH, SEQ:T], start=True, stop=True).then_inc(wi_mm, 1)
            for tt, (t0, n) in enumerate(TILES):
                if tt == 2:
                    pe.wait_ge(kout_cp, 1)
                b = 6 + tt % 2
                for j in range(2):
                    nc.tensor.transpose(bank(b)[0:n, P * j:P * (j + 1)], kT[:, j, t0:t0 + n], ident)
                nc.tensor.transpose(bank(b)[0:n, KVW:KVW + HD], kiT[0:HD, t0:t0 + n],
                                    ident[0:HD, 0:HD]).then_inc(kout_mm, 1)
            pe.wait_ge(prep_done, 1)

            def half(ap, h):
                return ap[HD * h:HD * (h + 1)]

            def pi(qt):
                if qt == 0:
                    pe.wait_ge(wi_done, 1)
                    pe.wait_ge(kout_cp, 3)
                else:
                    pe.wait_ge(pi_read, 1)
                nk = P * (qt + 1)
                for h in range(NIH):
                    b, c = 2 + 2 * (h % 2) + h // 4, 256 * (h // 2 % 2)
                    last = mm(psum[:, b, c:c + nk],
                              half(qiT, h % 2)[:, h // 2, P * qt:P * (qt + 1)], half(kiT, h % 2)[:, 0:nk],
                              start=True, stop=True)
                last.then_inc(pi_mm, 1)

            def si_t(x):
                p, c = divmod(x, 3)
                if c == 2:
                    return
                if c == 0:
                    pe.wait_ge(kx_in[p % 2], 16 * 16 * (p // 2 + 1))
                n = 2 * p + c
                if n == 0:
                    pe.wait_ge(pi_read, 2)
                else:
                    pe.wait_ge(kx_cp, n)
                for b2 in range(2):
                    for g in range(4):
                        last = nc.tensor.transpose(bank(2 + b2)[0:HD, P * g:P * (g + 1)],
                                                   kx_raw[:, p % 2, b2, 4 * c + g, :], ident)
                last.then_inc(si_tmm, 1)

            def si_s(x):
                p, c = divmod(x, 3)
                if c < 2:
                    pe.wait_ge(kx_dup, 2 * p + c + 1)
                if x:
                    pe.wait_ge(si_relu, x)
                w = 512 if c < 2 else NS
                for b2 in range(2):
                    last = mm(bank(4)[HD * b2:HD * (b2 + 1), 0:w], qiz[:, 2 * p + b2, :],
                              kxT[:, b2, 512 * c:512 * c + w], start=True, stop=True)
                last.then_inc(si_smm, 1)

            def si_w(x):
                p, c = divmod(x, 3)
                pe.wait_ge(si_relu, x + 1)
                w = 512 if c < 2 else NS
                mm(bank(5 + c)[0:NS, 0:w], wp[:, p, :], srelu[:, x % 2, 0:w], start=(p == 0),
                   stop=(p == 3)).then_inc(si_wmm, 1)

            def pa_l(m):
                qt, g = divmod(m, NKV)
                if m == 0:
                    pe.wait_ge(kx_cp, 8)
                    pe.wait_ge(sc_read, 1)
                else:
                    pe.wait_ge(pa_lg, m)
                nk = P * (qt + 1)
                for i in range(4):
                    h = 4 * g + i
                    src = kT if g % 2 == h % 2 else kTs
                    last = mm(psum[:, 2 + i % 2, 256 * (i // 2):256 * (i // 2) + nk],
                              half(qT, h % 2)[:, h // 2, P * qt:P * (qt + 1)], half(src, h % 2)[:, g // 2, 0:nk],
                              start=True, stop=True)
                last.then_inc(pa_lmm, 1)

            def pa_t(m):
                qt, g = divmod(m, NKV)
                pe.wait_ge(pa_prob, m + 1)
                if m:
                    pe.wait_ge(pa_pT, m)
                pl = prob[:, 0:4 * P * (qt + 1)].rearrange("p (h k) -> p h k", h=4)
                for kb in range(qt + 1):
                    for i in range(4):
                        last = nc.tensor.transpose(bank(4 + kb)[:, P * i:P * (i + 1)],
                                                   pl[:, i, P * kb:P * (kb + 1)], ident)
                last.then_inc(pa_tmm, 1)

            def pa_v(m):
                qt, g = divmod(m, NKV)
                pe.wait_ge(pa_pT, m + 1)
                if m:
                    pe.wait_ge(pa_out, m)
                for ip in range(2):
                    for kb in range(qt + 1):
                        last = mm(bank(6)[HD * ip:HD * (ip + 1), 0:2 * P], vtok[:, kb, HD * g:HD * (g + 1)],
                                  pT4[:, kb, 2 * ip:2 * ip + 2, :], start=(kb == 0),
                                  stop=(kb == qt))
                last.then_inc(pa_vmm, 1)

            def sa_t(b):
                pe.wait_ge(k_in, 16 * NPG * (b + 1))
                if b == 0:
                    pe.wait_ge(pa_lg, 8)
                for s in range(4):
                    j, hp = divmod(s, 2)
                    if 4 * b + s >= 2:
                        pe.wait_ge(sa_kcp, 4 * b + s - 1)
                    for g in range(4):
                        last = nc.tensor.transpose(bank(2 + s % 2)[:, P * g:P * (g + 1)],
                                                   k_r[:, 4 * hp + g, P * j:P * (j + 1)], ident)
                    last.then_inc(sa_tmm, 1)

            def sa_l(b):
                pe.wait_ge(sa_kcp, 4 * b + 4)
                if b == 0:
                    pe.wait_ge(sbias_ready, 2)
                    pe.wait_ge(pa_pT, 8)
                    pe.wait_ge(pa_out, 8)
                else:
                    pe.wait_ge(sa_exp, b)
                for c in range(3):
                    w = 512 if c < 2 else NS
                    mm(bank(5 + c, w), C("rep")[0:NS, P * b:P * (b + 1)], score[0:NS, 512 * c:512 * c + w],
                       start=True, stop=False)
                    for j in range(2):
                        last = mm(bank(5 + c, w), qz[:, j, b, :], KT[:, j, 512 * c:512 * c + w], start=False,
                                  stop=(j == 1))
                last.then_inc(sa_lmm, 1)

            def sa_p(b):
                pe.wait_ge(sa_prob, b + 1)
                if b:
                    pe.wait_ge(sa_out, b)
                for g in range(8):
                    nc.tensor.transpose(bank(2 + g // 4)[:, P * (g % 4):P * (g % 4 + 1)], prob[:, P * g:P * (g + 1)],
                                        ident)
                nc.tensor.transpose(bank(4)[0:NS, 0:P], prob[:, PAST:KEYS], ident).then_inc(sa_pmm, 1)

            def sa_v(b):
                pe.wait_ge(sa_pT, b + 1)
                pe.wait_ge(v_in, 16 * NPG * (b + 1))
                for j in range(2):
                    out = bank(4)[:, 64 * j:64 * (j + 1)]
                    for g in range(9):
                        if g < 8:
                            last = mm(out, v_r[:, g, P * j:P * (j + 1)], probT3[:, g, 64 * j:64 * (j + 1)],
                                      start=(g == 0), stop=False)
                        else:
                            last = mm(out, vtok[0:NS, 2, P * j:P * (j + 1)], probT3[0:NS, 8, 64 * j:64 * (j + 1)],
                                      start=False, stop=True)
                last.then_inc(sa_vmm, 1)

            todo = {"pi": pi, "si_t": si_t, "si_s": si_s, "si_w": si_w, "pa_l": pa_l, "pa_t": pa_t, "pa_v": pa_v,
                    "sa_t": sa_t, "sa_l": sa_l, "sa_p": sa_p, "sa_v": sa_v, "unit": unit}
            for what, i in steps:
                if what in todo:
                    todo[what](i)
            pe.wait_ge(lru_done, CR)
            pe.wait_ge(sa_pT, NB)
            for c in range(CR):
                nc.tensor.transpose(bank(2 + c // 4)[0:36, P * (c % 4):P * (c % 4 + 1)], tail[:, c, :],
                                    ident).then_inc(tail_mm, 1)
            pe.wait_ge(sa_out, NB)
            for u in range(first_bra, len(units)):
                unit(u)
            second_pe(pe, sum_sq)

        @block.scalar
        def _(act):
            act_n = [0]

            def link(ins):
                act_n[0] += 1
                ins.then_inc(act_chain, 1)
                act.wait_ge(act_chain, act_n[0])

            def squares(norm, k, src):
                if k >= 2:
                    act.wait_ge(ss_mm, KD * norm + k - 1)
                nc.scalar.activation((sq if norm == 0 else sq2)[:, k % 2, :], src, ACT.Square).then_inc(sq_ready, 1)

            def root(norm):
                act.wait_ge(var_ready, norm + 1)
                nc.scalar.activation(rstd[:], rstd[:], ACT.Sqrt).then_inc(rstd_ready, 1)

            act.wait_ge(lam_dve, 1)
            link(nc.scalar.activation(spt[:, 1, :], spt[:, 0, :], ACT.Abs))
            nc.scalar.activation(spt[:, 1, :], spt[:, 1, :], ACT.Exp, scale=-1.0).then_inc(lam_act, 1)
            for k in range(KD):
                act.wait_ge(xt_cp, k + 1)
                squares(0, k, G[:, k, :])
            root(0)

            def evac(u):
                kind, i, _ = units[u]
                acc = bank(u % 2)
                if kind in ("gxx", "brr", "bra", "out"):
                    return
                act.wait_ge(acc_ready, u + 1)
                free = acc_free[u % 2]
                if kind in ("q", "k", "qi", "ki"):
                    t = ropes.index((kind, i))
                    m = HD if kind == "ki" else P
                    if t >= 2:
                        act.wait_ge(rope_out, t - 1)
                    if kind in "qk":
                        at = V_QN if kind == "q" else V_KN
                        nc.scalar.activation(ropeb[:, t % 2, :], acc[:, 0:T], ACT.Identity, scale=vec[:, at:at + 1])
                        nc.scalar.activation(sq[:, t % 2, :], acc[:, 0:T], ACT.Square).then_inc(free, 1)
                    else:
                        nc.scalar.activation(ropeb[0:m, t % 2, :], acc[0:m, 0:T], ACT.Identity).then_inc(free, 1)
                elif kind == "wi":
                    nc.scalar.activation(wiT[0:NIH, :], acc[0:NIH, 0:T], ACT.Identity, scale=WI_SCALE).then_inc(free, 1)
                elif kind == "v":
                    n = TILES[i][1]
                    nc.scalar.activation(vtok[0:n, i, :], acc[0:n, 0:KVW], ACT.Identity).then_inc(free, 1)
                elif kind == "xr":
                    if i == 0:
                        act.wait_ge(zeroed, 2)
                    if i >= 2:
                        act.wait_ge(conv_ready, i - 1)
                    if i == 0 or i >= 2:
                        act.wait_ge(pre_cp, 2)
                    seg = xpad[:, i % 2, S0:XP].rearrange("p (b s) -> p b s", b=NB)
                    nc.scalar.activation(xpad[:, i % 2, PAD:S0], acc[:, 0:SEQ], ACT.Identity)
                    nc.scalar.activation(seg[:, :, 0:PAD], stT[:, i, 0:24].rearrange("p (b j) -> p b j", b=NB),
                                         ACT.Identity)
                    nc.scalar.activation(seg[:, :, PAD:SEGB], acc[:, SEQ:T].rearrange("p (b t) -> p b t", b=NB),
                                         ACT.Identity).then_inc(free, 1)
                elif kind == "gr":
                    nc.scalar.activation(rnnT[:, i, :], acc[:, 0:T], ACT.Gelu_apprx_tanh).then_inc(free, 1)
                    if i >= 2:
                        lru_root(i - 2)
                elif kind == "ga":
                    if i == CR - 1:
                        lru_root(CR - 2)
                    nc.scalar.activation(g_r[:], acc[:, 0:XC], ACT.Sigmoid, bias=vec[:, V_BA + i:V_BA + i + 1]
                                         ).then_inc(free, 1)
                elif kind == "gx":
                    if i == 0:
                        act.wait_ge(lam_dve, 2)
                    else:
                        act.wait_ge(lru_done, i)
                    nc.scalar.activation(g_i[:], acc[:, 0:XC], ACT.Sigmoid, bias=vec[:, V_BX + i:V_BX + i + 1]
                                         ).then_inc(free, 1)
                    act.wait_ge(*freed(u))
                    nc.scalar.activation(g_th[:], g_r[:], ACT.Tanh, scale=sp8[:, i:i + 1])
                    nc.scalar.activation(g_a[:], g_r[:], ACT.Exp, scale=nsp8[:, i:i + 1]).then_inc(lru_a, 1)
                    if i == CR - 1:
                        lru_root(CR - 1)
                elif kind == "gmr":
                    nc.scalar.activation(G[:, i, :], acc[:, 0:T], ACT.Sigmoid).then_inc(free, 1)
                elif kind == "gma":
                    if i >= 4:
                        act.wait_ge(spill_out, 16 * (i - 2))
                    nc.scalar.activation(sgm[:, i % 4, :], acc[:, 0:T], ACT.Sigmoid).then_inc(free, 1)

            def lru_root(c):
                act.wait_ge(lru_w, c + 1)
                nc.scalar.activation(g_th[:], g_th[:], ACT.Sqrt, scale=2.0).then_inc(lru_s, 1)

            def rope_root(t):
                if ropes[t][0] in "qk":
                    act.wait_ge(rope_var, t + 1)
                    nc.scalar.activation(rstd[:], rstd[:], ACT.Sqrt).then_inc(rope_rstd, 1)

            for t in range(len(ropes)):
                evac(unit_at[ropes[t]])
                if t:
                    rope_root(t - 1)
            evac(unit_at[("wi", 0)])
            for i in range(3):
                evac(unit_at[("v", i)])

            def si_t(x):
                p, c = divmod(x, 3)
                if c == 2:
                    return
                n = 2 * p + c
                act.wait_ge(si_tmm, n + 1)
                if p:
                    act.wait_ge(si_smm, 3 * (p - 1) + c + 1)
                nc.scalar.activation(kxT[0:HD, 0, 512 * c:512 * (c + 1)], bank(2)[0:HD, :], ACT.Identity)
                nc.scalar.activation(kxT[0:HD, 1, 512 * c:512 * (c + 1)], bank(3)[0:HD, :],
                                     ACT.Identity).then_inc(kx_cp, 1)

            def si_s(x):
                w = 512 if x % 3 < 2 else NS
                act.wait_ge(si_smm, x + 1)
                if x == 0:
                    act.wait_ge(outs_out, 16 * 9)
                if x >= 2:
                    act.wait_ge(si_wmm, x - 1)
                nc.scalar.activation(srelu[:, x % 2, 0:w], bank(4, w), ACT.Relu).then_inc(si_relu, 1)

            def pa_l(m):
                nk = P * (m // NKV + 1)
                act.wait_ge(pa_nb, m + 1)
                pl = prob[:, 0:4 * nk].rearrange("p (h k) -> p h k", h=4)
                for i in range(4):
                    last = nc.scalar.activation(pl[:, i, :], pl[:, i, :], ACT.Exp, bias=small[:, 4 + i:5 + i],
                                                scale=QK_SCALE, accum_out=small[:, 8 + i:9 + i])
                last.then_inc(pa_exp, 1)

            def pa_t(m):
                qt = m // NKV
                act.wait_ge(pa_tmm, m + 1)
                if m:
                    act.wait_ge(pa_vmm, m)
                for kb in range(qt + 1):
                    last = nc.scalar.activation(pT4[:, kb], bank(4 + kb).rearrange("p (h q) -> p h q", h=4),
                                                ACT.Identity)
                last.then_inc(pa_pT, 1)

            def sa_t(b):
                for s in range(4):
                    j, hp = divmod(s, 2)
                    act.wait_ge(sa_tmm, 4 * b + s + 1)
                    if b == 0:
                        act.wait_ge(sbias_ready, 1)
                    else:
                        act.wait_ge(sa_lmm, b)
                    nc.scalar.activation(KT[:, j, 512 * hp:512 * (hp + 1)], bank(2 + s % 2),
                                         ACT.Identity).then_inc(sa_kcp, 1)

            def sa_l(b):
                act.wait_ge(sa_nb, b + 1)
                if b:
                    act.wait_ge(sa_pmm, b)
                else:
                    act.wait_ge(pa_tmm, 8)
                logits = psum[:, 5:8, :].rearrange("p a b -> p (a b)")[:, 0:KEYS]
                nc.scalar.activation(prob[:], logits, ACT.Exp, bias=small[:, 17:18], scale=QK_SCALE,
                                     accum_out=small[:, 18:19]).then_inc(sa_exp, 1)

            def sa_p(b):
                act.wait_ge(sa_pmm, b + 1)
                if b:
                    act.wait_ge(sa_vmm, b)
                else:
                    act.wait_ge(pa_vmm, 8)
                nc.scalar.activation(probT[:, 0:512], bank(2), ACT.Identity)
                nc.scalar.activation(probT[:, 512:1024], bank(3), ACT.Identity)
                nc.scalar.activation(probT[0:NS, 1024:1152], bank(4)[0:NS, 0:P], ACT.Identity).then_inc(sa_pT, 1)

            todo = {"si_t": si_t, "si_s": si_s, "pa_l": pa_l, "pa_t": pa_t, "sa_t": sa_t, "sa_l": sa_l, "sa_p": sa_p,
                    "unit": evac}
            for what, i in steps:
                if what in todo:
                    todo[what](i)
            act.wait_ge(sa_lmm, NB)
            act.wait_ge(tail_mm, CR)
            act.wait_ge(sa_vmm, NB)
            for hf in range(2):
                nc.scalar.activation(tail_raw[0:36, 512 * hf:512 * (hf + 1)], bank(2 + hf)[0:36, :],
                                     ACT.Identity).then_inc(tail_cp, 1)
            second_act(act, squares, root)

        @block.vector
        def _(dve):
            v = nc.vector
            dve_n = [0]

            def link(ins):
                dve_n[0] += 1
                ins.then_inc(dve_chain, 1)
                dve.wait_ge(dve_chain, dve_n[0])

            dve.wait_ge(pre_t, 1)
            link(v.tensor_copy(vec[:], bank(2)[:, 0:NV]))
            v.tensor_scalar(spt[:, 0, :], vec[:, V_LAM:V_LAM + CR], -1.0, None, ALU.mult).then_inc(lam_dve, 1)
            dve.wait_ge(pre_t, 2)
            v.tensor_copy(stT[:], bank(3)[:, 0:256].rearrange("p (c s) -> p c s", c=CR)).then_inc(pre_cp, 2)
            dve.wait_ge(p_mm, 1)
            v.tensor_copy(pT[:], psum[:, 4:6, 0:T]).then_inc(p_cp, 1)
            for k in range(KD):
                dve.wait_ge(xt_mm, k + 1)
                v.tensor_copy(G[:, k, :], bank(4 + k % 4, T)).then_inc(xt_cp, 1)
            dve.wait_ge(lam_act, 1)
            e, z, z2, acc = spt[:, 1, :], spt[:, 2, :], spt[:, 3, :], sp8[:]
            link(v.tensor_scalar(z, e, 2.0, None, ALU.add))
            link(v.reciprocal(z, z))
            link(v.tensor_tensor(z, z, e, ALU.mult))
            link(v.tensor_tensor(z2, z, z, ALU.mult))
            link(v.tensor_scalar(acc, z2, 1.0 / 19, 1.0 / 17, ALU.mult, ALU.add))
            for n in range(15, 0, -2):
                link(v.tensor_tensor(acc, acc, z2, ALU.mult))
                link(v.tensor_scalar(acc, acc, 1.0 / n, None, ALU.add))
            link(v.tensor_tensor(acc, acc, z, ALU.mult))
            link(v.tensor_scalar(acc, acc, 16.0, None, ALU.mult))
            link(v.tensor_scalar(z, spt[:, 0, :], 0.0, 8.0, ALU.max, ALU.mult))
            link(v.tensor_tensor(acc, acc, z, ALU.add))
            v.tensor_scalar(nsp8[:], acc, -1.0, None, ALU.mult).then_inc(lam_dve, 1)

            def normalise(norm, src, at):
                dve.wait_ge(ss_mm, KD * (norm + 1))
                link(v.tensor_scalar(rstd[:], bank(1, T), 1.0 / D, EPS, ALU.mult, ALU.add))
                v.reciprocal(rstd[:], rstd[:]).then_inc(var_ready, 1)
                dve.wait_ge(rstd_ready, norm + 1)
                for k in range(KD):
                    v.scalar_tensor_tensor(out=H[:, k, :], in0=src[:, k, :], scalar=vec[:, at + k:at + k + 1],
                                           in1=rstd[:], op0=ALU.mult, op1=ALU.mult).then_inc(h_ready, 1)

            normalise(0, G, V_LN1)

            def rope(t):
                kind, i = ropes[t]
                dst = {"q": qT, "k": kT, "qi": qiT}[kind][:, i, :] if kind != "ki" else kiT[0:HD, :]
                m = HD if kind == "ki" else P
                x = ropeb[0:m, t % 2, :]
                dve.wait_ge(rope_mm, t + 1)
                if kind in "qk":
                    dve.wait_ge(h_ready, KD)
                    if t:
                        dve.wait_ge(rope_out, t)
                    link(v.tensor_scalar(rstd[:], bank(2 + 2 * (t % 2), T), 1.0 / HD, EPS, ALU.mult, ALU.add))
                    v.reciprocal(rstd[:], rstd[:]).then_inc(rope_var, 1)
                v.tensor_tensor(x, x, C("cos")[0:m], ALU.mult)
                link(v.tensor_tensor(dst, bank(3 + 2 * (t % 2))[0:m, 0:T], C("sin")[0:m], ALU.mult))
                if kind in "qk":
                    link(v.tensor_tensor(x, x, dst, ALU.add))
                    dve.wait_ge(rope_rstd, t + 1)
                    v.tensor_tensor(dst, x, rstd[:], ALU.mult).then_inc(rope_out, 1)
                else:
                    v.tensor_tensor(dst, x, dst, ALU.add).then_inc(rope_out, 1)

            for t in range(len(ropes)):
                rope(t)
            dve.wait_ge(rope_out, len(ropes))
            dve.wait_ge(zeroed, 2)
            for hf in range(2):
                v.tensor_copy(kTs[HD * hf:HD * (hf + 1)], kT[HD * (1 - hf):HD * (2 - hf)])
            link(v.tensor_copy(kiT[HD:P, :], kiT[0:HD, :]))
            for hf in range(2):
                v.tensor_copy(qiz[HD * hf:HD * (hf + 1)].rearrange("p b (a f t) -> p a b f t", a=4, f=2)[:, :, :, hf, :],
                              qiT[HD * hf:HD * (hf + 1), :, SEQ:T].rearrange("p a (b t) -> p a b t", b=NB))
            for g in range(NKV):
                j, pp = divmod(g, 2)
                for i in range(4):
                    h = 4 * g + i
                    v.tensor_copy(qz[HD * pp:HD * (pp + 1), j, :, TS * h:TS * (h + 1)],
                                  qT[HD * (h % 2):HD * (h % 2 + 1), h // 2, SEQ:T].rearrange("p (b t) -> p b t", b=NB))
            dve.wait_ge(xt_cp, KD)
            for b2 in range(2):
                last = v.tensor_copy(kxT[:, b2, PAST:KEYS], kiT[:, SEQ:T])
            last.then_inc(prep_done, 1)
            dve.wait_ge(wi_mm, 1)
            v.tensor_copy(wtok.rearrange("p t (f a) -> p t f a", f=2),
                          bank(2)[:, 0:2 * NIH].rearrange("p (t a f) -> p t f a", t=2, f=2))
            v.tensor_tensor(wp[:], C("mpair").rearrange("p (a s) -> p a s", a=4),
                            bank(3)[:, 0:NS].rearrange("p (a s) -> p a s", a=1).broadcast_to((P, 4, NS)),
                            ALU.mult).then_inc(wi_done, 1)
            dve.wait_ge(p_cp, 1)
            for tt, (t0, n) in enumerate(TILES):
                dve.wait_ge(kout_mm, tt + 1)
                v.tensor_copy(kout[0:n, tt, :], bank(6 + tt % 2)[0:n, 0:320]).then_inc(kout_cp, 1)

            def select(sc, scr, n, k, thr, causal, done):
                gt, eq, cum = scr
                r = sc.shape[0]
                cnt = small[0:r, 20:21]
                link(v.tensor_scalar(gt, sc, thr, 0.0, ALU.is_gt, ALU.add, accum_out=cnt))
                v.tensor_scalar(eq, sc, thr, None, ALU.is_equal)
                link(v.tensor_scalar(cnt, cnt, -1.0, float(k), ALU.mult, ALU.add))
                link(v.tensor_tensor_scan(cum, eq, eq, 0.0, ALU.add, ALU.bypass))
                link(v.scalar_tensor_tensor(out=eq, in0=cum, scalar=cnt, in1=eq, op0=ALU.is_le, op1=ALU.mult))
                link(v.tensor_tensor(gt, gt, eq, ALU.add))
                if causal:
                    link(v.tensor_tensor(gt[:, n - P:n], gt[:, n - P:n], C("tri"), ALU.mult))
                v.tensor_scalar(sc, gt, BIG, -BIG, ALU.mult, ALU.add).then_inc(done, 1)

            def pi(qt):
                nk = P * (qt + 1)
                dve.wait_ge(pi_mm, qt + 1)
                s = psum[:, 2:6, :].rearrange("p a (b k) -> p (a b) k", b=2)[:, :, 0:nk]
                wb = wtok[:, qt, :].rearrange("p (h k) -> p h k", k=1).broadcast_to((P, NIH, nk))
                v.scalar_tensor_tensor(out=pi_tmp[:, :, 0:nk], in0=s, scalar=0.0, in1=wb, op0=ALU.max,
                                       op1=ALU.mult).then_inc(pi_read, 1)
                dve.wait_ge(pi_read, qt + 1)
                sc = pbias[qt]
                v.tensor_reduce(sc[:, 0:nk], pi_tmp[:, :, 0:nk].rearrange("p h k -> p k h"), AX_X,
                                ALU.add).then_inc(pi_red, 1)
                dve.wait_ge(pi_red, qt + 1)
                link(v.tensor_tensor(sc[:, nk - P:nk], sc[:, nk - P:nk], C("tri"), ALU.mult))
                link(v.tensor_tensor(sc[:, nk - P:nk], sc[:, nk - P:nk], C("trib"), ALU.add))

            def ptk(qt):
                nk = P * (qt + 1)
                w = vraw[:, 0:nk]
                sc = pbias[qt][:, 0:nk]
                link(v.tensor_copy(w, sc))
                for it in range(TOPK_P // 8):
                    link(v.max(m8[:], w))
                    if it < TOPK_P // 8 - 1:
                        link(v.match_replace(w, m8[:], w, FMIN))
                select(sc, [vraw[:, 256 * (a + 1):256 * (a + 1) + nk] for a in range(3)], nk, TOPK_P, m8[:, 7:8], True,
                       pbias_ready)

            def si_t(x):
                p, c = divmod(x, 3)
                if c == 2:
                    return
                dve.wait_ge(kx_cp, 2 * p + c + 1)
                v.tensor_copy(kxT[HD:P, :, 512 * c:512 * (c + 1)],
                              kxT[0:HD, :, 512 * c:512 * (c + 1)]).then_inc(kx_dup, 1)

            def sc(_):
                dve.wait_ge(si_wmm, 12)
                v.tensor_copy(score[0:NS, 0:PAST], psum[0:NS, 5:7, :].rearrange("p a b -> p (a b)"))
                link(v.tensor_tensor(score[0:NS, PAST:KEYS], bank(7)[0:NS, 0:NS], C("nk")[0:NS], ALU.mult))
                v.tensor_tensor(score[0:NS, PAST:KEYS], score[0:NS, PAST:KEYS], C("nkb")[0:NS],
                                ALU.add).then_inc(sc_read, 1)
                dve.wait_ge(sc_read, 1)
                link(v.tensor_copy(work[0:NS, :], score[0:NS, :]))
                ptk(0)

            def tk(it):
                link(v.max(small[0:NS, 24:32], work[0:NS, :]))
                if it < TOPK_S // 8 - 1:
                    link(v.match_replace(work[0:NS, :], small[0:NS, 24:32], work[0:NS, :], FMIN))

            def sel(_):
                dve.wait_ge(pa_tmm, 8)
                select(score[0:NS, :], [work[0:NS, :], eqb[0:NS, :], prob[0:NS, :]], KEYS, TOPK_S, small[0:NS, 31:32],
                       False, sbias_ready)
                dve.wait_ge(sbias_ready, 1)
                for j in range(2):
                    last = v.tensor_copy(KT[:, j, PAST:KEYS], kT[:, j, SEQ:T])
                last.then_inc(sbias_ready, 1)

            def pa_l(m):
                nk = P * (m // NKV + 1)
                dve.wait_ge(pa_lmm, m + 1)
                if m:
                    dve.wait_ge(pa_tmm, m)
                pl = prob[:, 0:4 * nk].rearrange("p (h k) -> p h k", h=4)
                s = psum[:, 2:4, :].rearrange("p a (b k) -> p (a b) k", b=2)[:, :, 0:nk]
                bias = pbias[m // NKV][:, 0:nk].rearrange("p (h k) -> p h k", h=1).broadcast_to((P, 4, nk))
                if m % 4 == 0:
                    dve.wait_ge(pbias_ready, m // 4 + 1)
                v.tensor_tensor(pl, s, bias, ALU.add).then_inc(pa_lg, 1)
                dve.wait_ge(pa_lg, m + 1)
                link(v.tensor_reduce(small[:, 0:4], pl, AX_X, ALU.max))
                v.tensor_scalar(small[:, 4:8], small[:, 0:4], -QK_SCALE, None, ALU.mult).then_inc(pa_nb, 1)

            def pa_t(m):
                nk = P * (m // NKV + 1)
                pl = prob[:, 0:4 * nk].rearrange("p (h k) -> p h k", h=4)
                dve.wait_ge(pa_exp, m + 1)
                link(v.reciprocal(small[:, 12:16], small[:, 8:12]))
                v.tensor_tensor(pl, pl, small[:, 12:16].rearrange("p (h k) -> p h k", k=1).broadcast_to((P, 4, nk)),
                                ALU.mult).then_inc(pa_prob, 1)

            def pa_v(m):
                qt, g = divmod(m, NKV)
                dve.wait_ge(pa_vmm, m + 1)
                v.tensor_copy(qT[:, 2 * g:2 * g + 2, P * qt:P * (qt + 1)],
                              bank(6)[:, 0:256].rearrange("p (a q) -> p a q", a=2)).then_inc(pa_out, 1)

            def sa_l(b):
                dve.wait_ge(sa_lmm, b + 1)
                if b:
                    dve.wait_ge(sa_exp, b)
                logits = psum[:, 5:8, :].rearrange("p a b -> p (a b)")[:, 0:KEYS]
                link(v.tensor_reduce(small[:, 16:17], logits, AX_X, ALU.max))
                v.tensor_scalar(small[:, 17:18], small[:, 16:17], -QK_SCALE, None, ALU.mult).then_inc(sa_nb, 1)

            def sa_p(b):
                dve.wait_ge(sa_exp, b + 1)
                link(v.reciprocal(small[:, 19:20], small[:, 18:19]))
                v.tensor_scalar(prob[:], prob[:], small[:, 19:20], None, ALU.mult).then_inc(sa_prob, 1)

            def sa_v(b):
                dve.wait_ge(sa_vmm, b + 1)
                for pp in range(2):
                    for ip in range(2):
                        src = bank(4)[HD * pp:HD * (pp + 1), 0:128].rearrange(
                            "p (j g a i t) -> p j g a i t", j=2, g=2, a=2, i=2)[:, :, pp, :, ip, :]
                        dst = tokens(qT, b)[HD * ip:HD * (ip + 1)].rearrange(
                            "p (j g a) t -> p j g a t", j=2, g=2)[:, :, pp]
                        last = v.tensor_copy(dst, src)
                last.then_inc(sa_out, 1)

            def lru_gain(c):
                dve.wait_ge(lru_a, c + 1)
                if c:
                    dve.wait_ge(lru_done, c)
                link(v.tensor_scalar(g_u[:], g_th[:], 1.0, None, ALU.add))
                link(v.reciprocal(g_u[:], g_u[:]))
                v.tensor_tensor(g_th[:], g_th[:], g_u[:], ALU.mult).then_inc(lru_w, 1)
                dve.wait_ge(lru_w, c + 1)
                link(v.tensor_tensor(g_u[:], g_i[:], xc[:, c % 2, :], ALU.mult))

            def starts(ap):
                return ap[:, SEQ + PAD - 1:SEQ + PAD - 1 + SEGB * (NB - 1) + 1:SEGB]

            def lru_scan(c):
                dve.wait_ge(lru_s, c + 1)
                link(v.tensor_tensor(g_u[:], g_u[:], g_th[:], ALU.mult))
                link(v.tensor_scalar(starts(g_a), starts(g_a), 0.0, None, ALU.mult))
                link(v.tensor_copy(starts(g_u), stT[:, c, 24:32]))
                link(v.tensor_tensor_scan(g_u[:], g_a[:], g_u[:], 0.0, ALU.mult, ALU.add))
                seg = g_u[:, S0:S0 + SEGB * (NB - 1) + TS]
                v.tensor_copy(tail[:, c, 27:28], g_u[:, SEQ - 1:SEQ])
                v.tensor_copy(tail[:, c, 28:36], g_u[:, S0 + TS - 1:S0 + TS - 1 + SEGB * (NB - 1) + 1:SEGB])
                v.tensor_tensor(rnnT[:, c, 0:SEQ], rnnT[:, c, 0:SEQ], g_u[:, 0:SEQ], ALU.mult)
                hs = arena_seg(g_u)
                v.tensor_tensor(rnnT[:, c, SEQ:T].rearrange("p (b t) -> p b t", b=NB),
                                rnnT[:, c, SEQ:T].rearrange("p (b t) -> p b t", b=NB), hs, ALU.mult).then_inc(lru_done, 1)

            def arena_seg(ap):
                a = ap[:, S0:S0 + TS]
                return bass.AP(tensor=a.tensor, offset=a.offset, ap=[a.ap[0], [SEGB, NB], [1, TS]])

            def evac(u):
                kind, i, _ = units[u]
                acc = bank(u % 2)
                free = acc_free[u % 2]
                if kind == "xr":
                    dve.wait_ge(*freed(u))
                    x = xpad[:, i % 2, :]
                    cw = [vec[:, V_CW + CR * j + i:V_CW + CR * j + i + 1] for j in range(CW)]
                    c = xc[:, i % 2, :]
                    v.tensor_copy(tail[:, i, 0:3], x[:, S0 - 3:S0])
                    v.tensor_copy(tail[:, i, 3:27].rearrange("p (b j) -> p b j", b=NB),
                                  x[:, S0:XP].rearrange("p (b s) -> p b s", b=NB)[:, :, TS:SEGB])
                    if i >= 2:
                        dve.wait_ge(acc_ready, unit_at[("gx", i - 2)] + 1)
                    link(v.tensor_scalar(c, x[:, 0:XC], cw[0], vec[:, V_CB + i:V_CB + i + 1], ALU.mult, ALU.add))
                    for j in range(1, CW):
                        last = v.scalar_tensor_tensor(out=c, in0=x[:, j:j + XC], scalar=cw[j], in1=c, op0=ALU.mult,
                                                      op1=ALU.add)
                        if j < CW - 1:
                            link(last)
                    last.then_inc(conv_ready, 1)
                elif kind == "gr":
                    if i >= 2:
                        lru_scan(i - 2)
                elif kind == "ga":
                    if i == CR - 1:
                        lru_scan(CR - 2)
                elif kind == "gx":
                    lru_gain(i)
                    if i == CR - 1:
                        lru_scan(CR - 1)
                elif kind == "brr":
                    dve.wait_ge(acc_ready, u + 1)
                    dve.wait_ge(*freed(unit_at[("gmr", i)]))
                    v.tensor_tensor(G[:, i, :], bank(u % 2, T), G[:, i, :], ALU.mult).then_inc(free, 1)
                elif kind == "bra":
                    dve.wait_ge(acc_ready, u + 1)
                    dve.wait_ge(*freed(unit_at[("gma", i)]))
                    if i == 0:
                        dve.wait_ge(spill_in, 32)
                    gate = gback[:, i, :] if i < GSPILL else sgm[:, i % 4, :]
                    v.tensor_tensor(gate, bank(u % 2, T), gate, ALU.mult).then_inc(free, 1)
                    dve.wait_ge(*freed(u))
                    v.tensor_tensor(G[:, i, :], G[:, i, :], gate, ALU.add).then_inc(mix_ready, 1)
                elif kind == "out":
                    dve.wait_ge(acc_ready, u + 1)
                    v.tensor_tensor(XT[:, i, :], bank(u % 2, T), XT[:, i, :], ALU.add).then_inc(free, 1)

            todo = {"pi": pi, "si_t": si_t, "sc": sc, "tk": tk, "ptk": ptk, "sel": sel, "pa_l": pa_l, "pa_t": pa_t, "pa_v": pa_v,
                    "sa_l": sa_l, "sa_p": sa_p, "sa_v": sa_v, "unit": evac}
            for what, i in vector_order(steps, units):
                if what in todo:
                    todo[what](i)
            for u in range(first_bra, len(units)):
                evac(u)
            second_dve(dve, link, normalise)


_INS = ["x_prompt", "x_sample", "p_prompt", "p_sample", "cache_k", "cache_v", "cache_kidx", "state_conv", "state_h",
        "page_table", "ln1", "w_in", "q_norm", "k_norm", "conv_w", "conv_b", "w_a", "b_a", "w_x", "b_x", "lam",
        "w_br_rnn", "w_br_attn", "w_out", "ln2", "w_rg", "b_rg", "w_re", "b_re", "w1", "w3", "w2", "ln3",
        "w_ple_gate", "w_ple_proj"]
_OUTS = [("y_prompt", (1, SEQ, D)), ("y_sample", (NB, TS, D)), ("k_prompt", (1, 1, SEQ, NKV, HD)),
         ("v_prompt", (1, 1, SEQ, NKV, HD)), ("kidx_prompt", (1, 1, SEQ, HD)), ("conv_prompt", (1, 1, PAD, DR)),
         ("h_prompt", (1, 1, DR)), ("k_sample", (1, NB, TS, NKV, HD)), ("v_sample", (1, NB, TS, NKV, HD)),
         ("kidx_sample", (1, NB, TS, HD)), ("conv_sample", (1, NB, PAD, DR)), ("h_sample", (1, NB, DR))]


def kernel(**inputs):
    import concourse.bacc as _bacc
    from concourse.bass_utils import run_bass_kernel_spmd as _run

    nc = _bacc.Bacc("TRN2", target_bir_lowering=False, num_devices=1)
    arrays, A, O = {}, {}, {}
    data = {name: np.ascontiguousarray(inputs[name]) for name in _INS}
    data["consts"] = constants()[0]
    for name, a in data.items():
        arrays[f"in_{name}"] = a
        A[name] = nc.dram_tensor(f"in_{name}", a.shape, mybir.dt.from_np(a.dtype), kind="ExternalInput").ap()
    for name, shape in _OUTS:
        O[name] = nc.dram_tensor(f"out_{name}", shape, F32, kind="ExternalOutput").ap()
    build_program(nc, A, O)
    r = _run(nc, [arrays], core_ids=[0])
    return tuple(r.results[0][f"out_{name}"] for name, _ in _OUTS)
```

```python
from contextlib import ExitStack

import numpy as np

import concourse.bass as bass
from concourse import mybir

ALU = mybir.AluOpType
ACT = mybir.ActivationFunctionType
F32 = mybir.dt.float32
F32R = mybir.dt.float32r
I32 = mybir.dt.int32
AX_X = mybir.AxisListType.X

P = 128
D = 2048
KD = D // P
SEQ = 256
NB = 8
TS = 8
NS = NB * TS
T = SEQ + NS
TILES = [(0, 128), (128, 128), (256, 64)]
PAST = 1024
PAGE = 128
NPG = PAST // PAGE
HD = 64
NH = 16
NKV = 4
KVW = NKV * HD
NIH = 8
DR = 1024
CR = DR // P
CW = 4
NG = 4
EPG = 8
NE = NG * EPG
F = 256
PLE = 256
EPS = 1e-6
FMIN = -3.4028234663852886e38
BIG = 1e30
TOPK_P = SEQ // 4
TOPK_S = 256
KEYS = PAST + NS
QK_SCALE = HD ** -0.5
WI_SCALE = (HD ** -0.5) * (NIH ** -0.5)
O_XR, O_GR, O_Q = 0, DR, 2 * DR
O_K = O_Q + NH * HD
O_V = O_K + KVW
O_QI = O_V + KVW
O_KI = O_QI + NIH * HD
O_WI = O_KI + HD
O_GMR = O_WI + NIH
O_GMA = O_GMR + D
PAD = CW - 1
SEGB = PAD + TS
S0 = PAD + SEQ
XP = S0 + NB * SEGB
XC = XP - PAD
V_LN1, V_LN2, V_LN3, V_CW, V_CB, V_BA, V_BX, V_LAM, V_QN, V_KN = 0, 16, 32, 48, 80, 88, 96, 104, 112, 113
NV = 114


def constants():
    half = HD // 2
    inv = (10000.0 ** (-np.arange(half) / half)).astype(np.float32)
    pos = np.concatenate([np.arange(SEQ), np.tile(PAST + np.arange(TS), NB)]).astype(np.float32)
    ang = (inv[:, None] * pos[None, :]).astype(np.float64)
    d = np.arange(P)
    cos = np.cos(ang)[d % half]
    sin = np.sin(ang)[d % half]
    rot = np.zeros((P, P), np.float32)
    for i in range(P):
        if i % HD < half:
            rot[i + half, i] = -1.0
        else:
            rot[i - half, i] = 1.0
    bones = (d[:, None] // HD == d[None, :] // HD).astype(np.float32)
    ones = np.ones((P, P), np.float32)
    ident = np.eye(P, dtype=np.float32)
    utri = (d[:, None] <= d[None, :]).astype(np.float32)
    tri = (d[None, :] <= d[:, None]).astype(np.float32)
    trib = np.where(tri > 0, 0.0, FMIN).astype(np.float32)
    e8 = np.zeros((P, P), np.float32)
    for r in range(P):
        e8[(r % 64) // TS, r] = 1.0
    mpair = np.zeros((P, 4, NS), np.float32)
    for p in range(4):
        for r in range(P):
            mpair[r, p, (2 * p + r // 64) * TS + r % TS] = 1.0
    s = np.arange(NS)
    nk = np.zeros((P, NS), np.float32)
    nk[:NS] = (s[:, None] // TS == s[None, :] // TS) & (s[None, :] <= s[:, None])
    nkb = np.where(nk > 0, 0.0, FMIN).astype(np.float32)
    rep = np.zeros((P, NB, P), np.float32)
    for b in range(NB):
        for r in range(P):
            rep[b * TS + r % TS, b, r] = 1.0
    iota = np.tile(np.arange(1, P + 1, dtype=np.float32), (P, 1))
    parts = [("cos", cos), ("sin", sin), ("rot", rot), ("bones", bones), ("ones", ones), ("ident", ident),
             ("utri", utri), ("tri", tri), ("trib", trib), ("e8", e8), ("mpair", mpair.reshape(P, -1)),
             ("nk", nk), ("nkb", nkb), ("rep", rep.reshape(P, -1)), ("iota", iota)]
    at, n = {}, 0
    for name, a in parts:
        at[name] = (n, a.shape[1])
        n += a.shape[1]
    return np.concatenate([a for _, a in parts], 1).astype(np.float32), at


def plan():
    units, loads = [], []

    def load(*what):
        loads.append([what, None])
        return len(loads) - 1

    def unit(kind, i, ls):
        units.append((kind, i, ls))
        for n in ls:
            loads[n][1] = len(units) - 1

    for i in range(8):
        unit("q", i, [load("w_in", O_Q + P * i, P)])
    for i in range(2):
        unit("k", i, [load("w_in", O_K + P * i, P)])
    for i in range(4):
        unit("qi", i, [load("w_in", O_QI + P * i, P)])
    n = load("w_in", O_KI, HD + NIH)
    unit("ki", 0, [n])
    va, vb = load("v", 0), load("v", 1)
    unit("v", 0, [va, vb])
    unit("v", 1, [va, vb])
    for c in range(CR):
        unit("xr", c, [load("w_in", O_XR + P * c, P)])
        unit("gr", c, [load("w_in", O_GR + P * c, P)])
        if c:
            unit("ga", c - 1, [])
            unit("gx", c - 1, [])
        if c == 3:
            for j in range(2):
                unit("gmr", j, [load("w_in", O_GMR + P * j, P)])
    unit("ga", CR - 1, [])
    unit("gx", CR - 1, [])
    for j0 in range(0, KD, 4):
        for j in range(j0 or 2, j0 + 4):
            unit("gmr", j, [load("w_in", O_GMR + P * j, P)])
        for j in range(j0, j0 + 4, 2):
            n = load("w_br_rnn", P * j)
            unit("brr", j, [n])
            unit("brr", j + 1, [n])
    for j in range(KD):
        unit("gma", j, [load("w_in", O_GMA + P * j, P)])
    for j in range(0, KD, 2):
        n = load("w_br_attn", P * j)
        unit("bra", j, [n])
        unit("bra", j + 1, [n])
    for j in range(KD):
        unit("out", j, [load("w_out", P * j)])
    return units, loads


def schedule(units):
    first = next(i for i, u in enumerate(units) if u[0] == "xr")
    last = next(i for i, u in enumerate(units) if u[0] == "bra")
    fill, steps = [], []
    for n in range(first, last):
        fill.append(("split", n))
        if units[n][0] not in ("brr", "ga", "gx"):
            fill.append(("half", n))
        fill.append(("unit", n))

    def fill_in(n=1):
        work = 0
        while fill and work < n:
            what, i = fill.pop(0)
            work += what == "half" or (what == "unit" and units[i][0] not in ("ga", "gx"))
            steps.append((what, i))

    for qt in range(2):
        steps.append(("pi", qt))
        fill_in()
    for x in range(13):
        if x < 12:
            steps.append(("si_t", x))
        fill_in()
        if x:
            steps.append(("si_w", x - 1))
        if x < 12:
            steps.append(("si_s", x))
    steps.append(("sc", 0))
    for part in range(3):
        steps.append(("ptk", part))
    fill_in(10)
    rounds = iter(range(TOPK_S // 8))

    def top(n):
        for _ in range(n):
            steps.append(("tk", next(rounds)))

    for m in range(8):
        steps.append(("pa_l", m))
        top(1)
        fill_in(3)
        steps.append(("pa_t", m))
        top(2)
        fill_in()
        steps.append(("pa_v", m))
        top(1)
        if m == 0:
            steps += [("ptk", 3), ("ptk", 4), ("ptk", 5)]
    steps.append(("sel", 0))
    fill_in(3)
    steps.append(("sa_t", 0))
    fill_in()
    steps.append(("sa_t", 1))
    for b in range(NB):
        fill_in()
        steps.append(("sa_l", b))
        if b < NB - 1:
            steps.append(("sa_t", 2 * b + 2))
        fill_in(2)
        steps.append(("sa_p", b))
        fill_in()
        steps.append(("sa_v", b))
        if b < NB - 1:
            steps.append(("sa_t", 2 * b + 3))
    return steps + fill


def tile_plan(units, loads, ring):
    tiles = [n for n, (what, _) in enumerate(loads) if what[0] not in ("w_br_rnn", "w_br_attn")]
    before = [[] for _ in units]
    for t, n in enumerate(tiles):
        u = 0
        if t >= 2:
            u = loads[tiles[t - 2]][1] + 1
        if n >= ring and n - ring not in tiles:
            u = max(u, loads[n - ring][1] + 1)
        before[u].append(t)
    return tiles, before


def vector_order(steps, units):
    out, held = [], []
    for what, i in steps:
        if what == "unit":
            out += held
            held = [(what, i)]
            if units[i][0] in ("ga", "gx"):
                out += held
                held = []
        elif what in ("pa_t", "pa_v", "sa_l", "sa_p", "sa_v"):
            out += [(what, i)] + held
            held = []
        elif what in ("tk", "sa_t", "split", "half"):
            out.append((what, i))
        else:
            out += held + [(what, i)]
            held = []
    return out + held


def expert_slot(m):
    if m < 4:
        return "up", 0, m
    e, q = divmod(m - 4, 6)
    if e == EPG - 1:
        return "down", e, q
    return ("up", e + 1, q) if q < 4 else ("down", e, q - 4)


def used_up(e):
    return 4 if e == 0 else 6 * e + 2


def turned(e):
    return 6 * e + 5 if e < EPG - 1 else 6 * EPG - 3


def build_program(nc, A, O):
    units, loads = plan()
    steps = schedule(units)
    _, const_at = constants()
    unit_at = {(k, i): n for n, (k, i, _) in enumerate(units)}
    n_front = unit_at[("xr", 0)]
    first_bra = unit_at[("bra", 0)]
    first_out = unit_at[("out", 0)]
    ropes = [("q", i) for i in range(8)] + [("k", 0), ("k", 1)] + [("qi", i) for i in range(4)] + [("ki", 0)]
    RING = 2
    MRING = 6
    STG = 3
    tiles, split_before = tile_plan(units, loads, RING)
    tile_at = {n: t for t, n in enumerate(tiles)}
    NT = len(tiles)
    pool_steps = steps[steps.index(("sc", 0)):steps.index(("sel", 0))]
    on_pool = {t for what, i in pool_steps if what == "split" for t in split_before[i]}
    PER = 48
    GSPILL = KD - 4

    with ExitStack() as ctx:
        def sem(name):
            return ctx.enter_context(nc.semaphore(name))

        ARENA = 53200
        base = nc.sbuf_base
        arena = ctx.enter_context(nc.sbuf_tensor("arena", [P, ARENA], F32))
        base = (base + 31) // 32 * 32
        psum = ctx.enter_context(nc.psum_tensor("psum", [P, 8, 512], F32))
        flags_i = ctx.enter_context(nc.sbuf_tensor("flags_i", [1, 4], I32))
        x_spill = nc.dram_tensor("x_spill", [P, KD * T], F32, kind="Internal").ap()
        branch_spill = nc.dram_tensor("branch_spill", [P, (KD + GSPILL) * T], F32, kind="Internal").ap()
        top = [0]

        def take(n):
            at = top[0]
            top[0] += (n + 7) // 8 * 8
            assert top[0] <= ARENA, (top[0], ARENA)
            return arena[:, at:at + n]

        def halves(name, at, n, low_at=None):
            return [nc.alloc_sbuf_tensor_at(f"{name}_{w}", [P, n], F32R, offset=base + 4 * a)
                    for w, a in (("high", at), ("low", at + n if low_at is None else low_at))]

        def parts3(a, b):
            return ((a[0], b[0]), (a[0], b[1]), (a[1], b[0]))

        slots = [take(2048) for _ in range(RING)]
        stage_at = [top[0], top[0] + 4096]
        take(8192)
        n_const = sum(w for _, w in const_at.values())
        const = take(n_const)

        def C(name):
            at, w = const_at[name]
            return const[:, at:at + w]

        h_at = top[0]
        H = take(KD * T).rearrange("p (k t) -> p k t", k=KD)
        g_at = top[0]
        g_flat = take(KD * T)
        G = g_flat.rearrange("p (k t) -> p k t", k=KD)
        parts_in = [halves(f"input_{k}", h_at + T * k, T, g_at + T * k) for k in range(KD)]
        vec = take(NV)
        epsc = take(1)
        rstd = take(T)
        shared = top[0]
        kraw = take(2048)
        vraw = take(2048)
        ktbuf = take(2 * KEYS)
        top_x = shared + 6144
        xtok = arena[:, shared:top_x].rearrange("p (t d) -> p t d", t=3)
        prob = take(KEYS)
        probT = take(9 * P)
        score = take(KEYS)
        x0 = arena[:, top[0]:top[0] + KD * T].rearrange("p (k t) -> p k t", k=KD)
        qz = take(2 * NB * P).rearrange("p (j b r) -> p j b r", j=2, b=NB)
        qiz = take(NB * 64).rearrange("p (b r) -> p b r", b=NB)
        rnnT = take(CR * T).rearrange("p (c t) -> p c t", c=CR)
        qT = take(8 * T).rearrange("p (k t) -> p k t", k=8)
        kT = take(2 * T).rearrange("p (k t) -> p k t", k=2)
        kTs = take(2 * T).rearrange("p (k t) -> p k t", k=2)
        vtok = take(3 * KVW).rearrange("p (t d) -> p t d", t=3)
        qiT = take(4 * T).rearrange("p (k t) -> p k t", k=4)
        kiT = take(T)
        wtok = take(2 * NIH).rearrange("p (t h) -> p t h", t=2)
        wp = take(4 * NS).rearrange("p (a s) -> p a s", a=4)
        pbias = [take(P), take(2 * P)]
        wa = take(CR * P).rearrange("p (c j) -> p c j", c=CR)
        wx = take(CR * P).rearrange("p (c j) -> p c j", c=CR)
        xpad_at = top[0]
        xpad = take(2 * XP).rearrange("p (b t) -> p b t", b=2)
        cos_at = const_at["cos"][0]
        xc = const[:, cos_at:cos_at + 2 * XC].rearrange("p (b t) -> p b t", b=2)
        rope_at = top[0]
        g_r, g_i, g_a, g_th, g_u = (take(XC) for _ in range(5))
        sq = arena[:, rope_at:rope_at + 2 * T].rearrange("p (b t) -> p b t", b=2)
        ropeb = arena[:, rope_at + 2 * T:rope_at + 4 * T].rearrange("p (b t) -> p b t", b=2)
        wiT = g_u[:, 0:T]
        sgm = qiT
        stT = take(CR * 32).rearrange("p (c s) -> p c s", c=CR)
        tail = take(CR * 36).rearrange("p (c s) -> p c s", c=CR)
        sp8, nsp8 = take(CR), take(CR)
        spt = take(4 * CR).rearrange("p (a c) -> p a c", a=4)
        small = take(64)
        m8 = take(8)
        vec_raw = probT[:, 0:P]
        st_raw = score[:, 0:DR]
        tail_raw = arena[:, xpad_at:xpad_at + DR]
        kout = prob[:, 0:3 * 320].rearrange("p (t d) -> p t d", t=3)
        pi_tmp = vraw.rearrange("p (h k) -> p h k", h=NIH)
        kx_raw = kraw.rearrange("p (q b g d) -> p q b g d", q=2, b=2, g=NPG)
        kxT = ktbuf.rearrange("p (b k) -> p b k", b=2)
        srelu = prob[:, 0:1024].rearrange("p (q k) -> p q k", q=2)
        work = ktbuf[:, 0:KEYS]
        eqb = ktbuf[:, KEYS:2 * KEYS]
        k_r = kraw.rearrange("p (g d) -> p g d", g=NPG)
        v_r = vraw.rearrange("p (g d) -> p g d", g=NPG)
        KT = ktbuf.rearrange("p (j k) -> p j k", j=2)
        probT3 = probT.rearrange("p (g r) -> p g r", g=9)
        pT4 = probT[:, 0:1024].rearrange("p (k h q) -> p k h q", k=2, h=4)
        t1, t2 = sq[:, 0, :], sq[:, 1, :]
        top[0] = shared
        XT = take(KD * T).rearrange("p (k t) -> p k t", k=KD)
        back = arena[:, top[0]:top[0] + (KD + GSPILL) * T].rearrange("p (k t) -> p k t", k=KD + GSPILL)
        ptok = arena[:, top[0]:top[0] + 768].rearrange("p (t d) -> p t d", t=3)
        htok = take(3 * D).rearrange("p (t d) -> p t d", t=3)
        mslots = slots + [take(2048) for _ in range(MRING - RING)]
        stage_at.append(top[0])
        take(4096)
        stage = [halves(f"weights_{i}", at, 2048) for i, at in enumerate(stage_at)]
        sq2 = take(2 * T).rearrange("p (b t) -> p b t", b=2)
        lg = take(3 * 36).rearrange("p (t n) -> p t n", t=3)
        rt = [take(3 * 32).rearrange("p (t n) -> p t n", t=3) for _ in range(5)]
        gates = take(3 * NE).rearrange("p (t n) -> p t n", t=3)
        goh = take(3 * NG).rearrange("p (t n) -> p t n", t=3)
        pos = take(3 * NG).rearrange("p (t n) -> p t n", t=3)
        r1 = [take(12).rearrange("p (t n) -> p t n", t=3) for _ in range(6)]
        v8 = take(24).rearrange("p (t n) -> p t n", t=3)
        w4 = take(4)
        fl = take(32)
        pc = take(3)
        gg = take(NE)
        geg = take(EPG)
        plg = take(2 * T).rearrange("p (b t) -> p b t", b=2)
        wr = take(KD * 36).rearrange("p (k n) -> p k n", k=KD)
        rb = take(36)
        pT = take(2 * T).rearrange("p (k t) -> p k t", k=2)
        outst = g_flat[:, 0:2048]
        S = g_flat[:, 2048:2048 + 384].rearrange("p (t s) -> p t s", t=3)
        ST = g_flat[:, 2432:2432 + T]
        silu = g_flat[:, 2752:2752 + 512].rearrange("p (b f) -> p b f", b=2)
        hid = g_flat[:, 3264:3264 + 512].rearrange("p (b f) -> p b f", b=2)
        hidT = [halves(f"hidden_{i}", g_at + 3776 + 512 * i, F) for i in range(2)]
        proj = arena[:, stage_at[2]:stage_at[2] + 4096].rearrange("p (k n) -> p k n", k=2)
        hg = halves("gathered", h_at, 2048)
        ytok = htok

        ident = C("ident")

        def bank(b, n=512):
            return psum[:, b, 0:n]

        consts_in, vecs_in, x_in, gates_in, router_in, ple_in = (sem(n) for n in (
            "consts_in", "vecs_in", "x_in", "gates_in", "router_in", "ple_in"))
        wfull = [sem(f"weights_in_{i}") for i in range(RING)]
        mfull = [sem(f"expert_weights_in_{i}") for i in range(MRING)]
        tfull = [sem(f"extra_weights_in_{i}") for i in range(MRING)]
        states_out = sem("states_out")
        kx_in = [sem("index_keys_in_0"), sem("index_keys_in_1")]
        k_in = [sem("keys_in_0"), sem("keys_in_1")]
        v_in, spill_out, spill_in, proj_in, outs_out = (sem(n) for n in (
            "values_in", "spill_out", "spill_in", "proj_in", "outs_out"))
        zeroed, pre_t, pre_cp, xt_mm, xt_cp, p_cp = (sem(n) for n in (
            "gates_zeroed", "pre_transposed", "pre_copied", "x_transposed", "x_copied", "p_copied"))
        sq_ready, ss_mm, var_ready, rstd_ready, h_ready = (sem(n) for n in (
            "squares_ready", "sums_done", "variance_ready", "rstd_ready", "h_ready"))
        acc_ready = sem("acc_ready")
        acc_free = [sem("acc_free_0"), sem("acc_free_1")]
        rope_mm, rope_var, rope_rstd, rope_out = (sem(n) for n in ("rope_mm", "rope_var", "rope_rstd", "rope_out"))
        wi_mm, wi_done, kout_mm, kout_cp, prep_done = (sem(n) for n in (
            "wi_mm", "wi_done", "kout_mm", "kout_copied", "prep_done"))
        lam_act, lam_dve = sem("lam_act"), sem("lam_dve")
        conv_ready, lru_a, lru_w, lru_s, lru_done = (sem(n) for n in (
            "conv_ready", "decay_ready", "gain_sq_ready", "gain_ready", "lru_done"))
        pi_mm, pi_read, pi_red, si_tmm, kx_cp, kx_dup, si_smm, si_relu, si_wmm, sc_read = (sem(n) for n in (
            "pi_mm", "pi_read", "pi_reduced", "si_transposed", "kx_copied", "kx_doubled", "si_scores", "si_relu",
            "si_weighted", "scores_read"))
        pbias_ready, sbias_ready = sem("pbias_ready"), sem("sbias_ready")
        pa_lmm, pa_lg, pa_nb, pa_exp, pa_prob, pa_tmm, pa_pT, pa_vmm, pa_out = (sem(n) for n in (
            "pa_logits", "pa_logits_read", "pa_max", "pa_exp", "pa_prob", "pa_transposed", "pa_probT", "pa_pv",
            "pa_out"))
        sa_tmm, sa_kcp, sa_lmm, sa_nb, sa_exp, sa_prob, sa_pmm, sa_pT, sa_vmm, sa_out = (sem(n) for n in (
            "sa_keys_transposed", "sa_keys_copied", "sa_logits", "sa_max", "sa_exp", "sa_prob", "sa_transposed",
            "sa_probT", "sa_pv", "sa_out"))
        mix_ready, tail_mm, tail_cp = sem("mix_ready"), sem("states_out_mm"), sem("states_out_copied")
        in_high, in_split, tile_high, tile_split = (sem(n) for n in (
            "input_high", "input_split", "weights_high", "weights_split"))
        ht_mm, ht_cp, rl_mm, rl_a, rl_e, rl_x, goh_ready, cum_mm, router_done = (sem(n) for n in (
            "h2_transposed", "h2_copied", "router_logits", "router_shifted", "router_exp", "router_parts", "group_onehot_ready",
            "group_counted", "router_done"))

        def pass_sems(w):
            return {n: sem(f"{w}_{n}") for n in (
                "used", "select", "st_mm", "st_cp", "hg_mm", "hg_cp", "silu", "hid", "tr", "hT", "oa", "ob",
                "sc_mm", "sc_add", "places", "gates", "split", "high", "hg_hi", "hT_hi")}

        main, extra = pass_sems("main"), pass_sems("extra")
        ple_g, ple_sg, ple_y, ple_t, ple_o = (sem(n) for n in (
            "ple_gate_mm", "ple_sigmoid", "ple_y", "ple_transposed", "ple_copied"))
        experts_done = sem("experts_done")
        act_chain, dve_chain = sem("act_chain"), sem("dve_chain")
        block = ctx.enter_context(nc.Block())

        def freed(u):
            return acc_free[u % 2], u // 2 + 1

        def tokens(ap, b):
            return ap[..., SEQ + TS * b:SEQ + TS * (b + 1)]

        def second_pe(pe, sum_sq):
            mm = nc.tensor.matmul
            pe.wait_ge(*freed(len(units) - 1))
            pe.sem_inc(main["used"], STG)
            pe.wait_ge(ple_in, 32)
            for k in range(2):
                for tt, (t0, n) in enumerate(TILES):
                    last = nc.tensor.transpose(bank(4 + k)[:, t0:t0 + n], ptok[0:n, tt, P * k:P * (k + 1)],
                                               ident[0:n, 0:n])
            last.then_inc(pre_t, 1)
            for k in range(KD):
                sum_sq(1, k)
            def turn_input(n_):
                q, tt = divmod(n_, 3)
                t0, n = TILES[tt]
                pe.wait_ge(h_ready, KD + 4 * q + 4)
                if n_ >= 4:
                    pe.wait_ge(ht_cp, n_ - 3)
                for a in range(4):
                    last = nc.tensor.transpose(bank(4 + n_ % 4)[0:n, P * a:P * (a + 1)], H[:, 4 * q + a, t0:t0 + n],
                                               ident)
                last.then_inc(ht_mm, 1)

            pe.wait_ge(router_in, 64)
            for k in range(KD):
                pe.wait_ge(h_ready, KD + k + 1)
                for tt, (t0, n) in enumerate(TILES):
                    last = mm(bank(1 + tt)[0:n, 0:36], H[:, k, t0:t0 + n], wr[:, k, :], start=(k == 0),
                              stop=(k == KD - 1))
            last.then_inc(rl_mm, 1)
            pe.wait_ge(p_cp, 1)
            for n_ in range(12):
                turn_input(n_)
            pe.wait_ge(goh_ready, 2)
            for tt, (t0, n) in enumerate(TILES):
                for t2 in range(tt + 1):
                    n2 = TILES[t2][1]
                    mm(bank(3)[0:n, NG * tt:NG * (tt + 1)], (C("utri") if t2 == tt else C("ones"))[0:n2, 0:n],
                       goh[0:n2, t2, :], start=(t2 == 0), stop=(t2 == tt))
            for t2 in range(3):
                n2 = TILES[t2][1]
                last = mm(bank(3)[:, 16:20], C("ones")[0:n2, :], goh[0:n2, t2, :], start=(t2 == 0), stop=(t2 == 2))
            last.then_inc(cum_mm, 1)
            pe.wait_ge(router_done, 1)
            pe.wait_ge(ht_cp, 12)

            def experts(s, g):
                pe.wait_ge(s["select"], g + 1)
                for tt, (t0, n) in enumerate(TILES):
                    nc.tensor.transpose(bank(3)[:, t0:t0 + n], S[0:n, tt, :], ident[0:n, 0:n])
                for tt, (t0, n) in enumerate(TILES):
                    last = mm(bank(3)[:, T:T + NE], S[0:n, tt, :], gates[0:n, tt, :], start=(tt == 0), stop=(tt == 2))
                last.then_inc(s["st_mm"], 1)
                for q in range(4):
                    if q == 3:
                        pe.wait_ge(s["st_cp"], g + 1)
                    for a in range(4):
                        for tt, (t0, n) in enumerate(TILES):
                            k = 4 * q + a
                            last = mm(bank(q)[:, P * a:P * (a + 1)], htok[0:n, tt, P * k:P * (k + 1)], S[0:n, tt, :],
                                      start=(tt == 0), stop=(tt == 2))
                    last.then_inc(s["hg_mm"], 1)

                def take_slot(m):
                    pe.wait_ge(s["split"], MRING + g * PER + m + 1)
                    return stage[m % STG]

                def up(e, quarters):
                    for q in quarters:
                        m = q if e == 0 else 4 + 6 * (e - 1) + q
                        w = take_slot(m)
                        if e == 0:
                            pe.wait_ge(s["hg_cp"], g * 4 + q + 1)
                        for k in range(4):
                            c = P * (4 * q + k)
                            for n, (x, y) in enumerate(parts3(hg, w)):
                                last = mm(bank(e % 2), x[:, c:c + P], y[:, 512 * k:512 * (k + 1)],
                                          start=(q == 0 and k == 0 and n == 0), stop=(q == 3 and k == 3 and n == 2))
                        last.then_inc(s["used"], 1)

                def turn(e):
                    pe.wait_ge(s["hid"], g * EPG + e + 1)
                    for k in range(2):
                        last = nc.tensor.transpose(bank(2)[:, P * k:P * (k + 1)], hid[:, e % 2, P * k:P * (k + 1)],
                                                   ident)
                    last.then_inc(s["tr"], 1)

                def down(e):
                    pe.wait_ge(s["hT"], g * EPG + e + 1)
                    for k in range(2):
                        w = take_slot(4 + 6 * e + (4 if e < EPG - 1 else 0) + k)
                        for n in range(4):
                            for a, (x, y) in enumerate(parts3(hidT[e % 2], w)):
                                last = mm(bank(4 + n), x[:, P * k:P * (k + 1)], y[:, 512 * n:512 * (n + 1)],
                                          start=(e == 0 and k == 0 and a == 0),
                                          stop=(e == EPG - 1 and k == 1 and a == 2))
                        last.then_inc(s["used"], 1)

                up(0, range(4))
                for e in range(EPG):
                    if e < EPG - 1:
                        up(e + 1, (0, 1))
                    turn(e)
                    if e < EPG - 1:
                        up(e + 1, (2, 3))
                    down(e)
                pe.wait_ge(s["oa"], g + 1)
                pe.wait_ge(s["ob"], g + 1)
                for d in range(KD):
                    if d >= 2:
                        pe.wait_ge(s["sc_add"], g * KD + d - 1)
                    mm(bank(2 + d % 2, T), outst[:, P * d:P * (d + 1)], ST[:], start=True,
                       stop=True).then_inc(s["sc_mm"], 1)
                pe.wait_ge(s["sc_add"], g * KD + KD)

            with pe.Fori(0, NG) as g:
                experts(main, g)
            more = pe.value_load(flags_i[0:1, 0:1], min_val=0, max_val=2)
            with pe.If(more > 0):
                pe.sem_inc(extra["used"], STG)
                experts(extra, 0)
                with pe.If(more > 1):
                    experts(extra, 1)

            for k in range(KD):
                sum_sq(2, k)
            pe.wait_ge(proj_in, 16)

            def back(j):
                pe.wait_ge(ple_y, j + 1)
                q, a = divmod(j, 4)
                if a == 0 and q:
                    pe.wait_ge(ple_o, 3 * q)
                for tt, (t0, n) in enumerate(TILES):
                    last = nc.tensor.transpose(bank(4 + tt)[0:n, P * a:P * (a + 1)], plg[:, j % 2, t0:t0 + n], ident)
                last.then_inc(ple_t, 1)

            for j in range(KD):
                if j >= 2:
                    pe.wait_ge(ple_y, j - 1)
                for k in range(2):
                    last = mm(bank(2 + j % 2, T), proj[:, k, P * j:P * (j + 1)], pT[:, k, :], start=(k == 0),
                              stop=(k == 1))
                pe.wait_ge(tile_split, 2 * NT + j + 1)
                for k in range(KD):
                    if j == 0:
                        pe.wait_ge(in_split, 2 * KD + k + 1)
                    for n, (x, y) in enumerate(parts3(stage[j % 2], parts_in[k])):
                        last = mm(bank(j % 2, T), x[:, P * k:P * (k + 1)], y[:],
                                  start=(k == 0 and n == 0), stop=(k == KD - 1 and n == 2))
                last.then_inc(ple_g, 1)
                if j:
                    back(j - 1)
            back(KD - 1)

        def second_act(act, squares, root, input_high):
            act.wait_ge(states_out, 64)
            for k in range(KD):
                act.wait_ge(*freed(first_out + k))
                squares(1, k, XT[:, k, :])
            root(1)

            def ht(n_):
                q, tt = divmod(n_, 3)
                n = TILES[tt][1]
                act.wait_ge(ht_mm, n_ + 1)
                nc.scalar.activation(htok[0:n, tt, 512 * q:512 * (q + 1)], bank(4 + n_ % 4)[0:n, :],
                                     ACT.Identity).then_inc(ht_cp, 1)

            def high(s, g, full, first, m):
                act.wait_ge(full[m % MRING], first(g, m))
                act.wait_ge(s["used"], g * PER + m + 1)
                nc.scalar.activation(stage[m % STG][0][:], mslots[m % MRING], ACT.Identity).then_inc(s["high"], 1)

            def first_main(g, m):
                return g * (PER // MRING * 32) + 32 * (m // MRING + 1)

            for m in range(STG):
                high(main, 0, mfull, first_main, m)

            for n_ in range(12):
                ht(n_)
                if n_ == 1:
                    act.wait_ge(rl_a, 1)
                    for n in (P, NS):
                        sl = slice(0, 2) if n == P else slice(2, 3)
                        nc.scalar.activation(r1[1][0:n, sl, :], r1[1][0:n, sl, :], ACT.Exp).then_inc(rl_e, 1)
                if n_ == 7:
                    act.wait_ge(rl_a, 2)
                    for n in (P, NS):
                        sl = slice(0, 2) if n == P else slice(2, 3)
                        nc.scalar.activation(rt[2][0:n, sl, :], rt[2][0:n, sl, :], ACT.Exp).then_inc(rl_e, 1)

            def experts(s, g, full, first, more):
                for q in range(4):
                    act.wait_ge(s["hg_mm"], g * 4 + q + 1)
                    nc.scalar.activation(hg[0][:, 512 * q:512 * (q + 1)], bank(q), ACT.Identity
                                         ).then_inc(s["hg_hi"], 1)
                for m in range(PER):
                    for e in range(EPG):
                        if m == used_up(e) - 1:
                            act.wait_ge(s["used"], g * PER + STG + used_up(e))
                            nc.scalar.activation(silu[:, e % 2, :], bank(e % 2)[:, 0:F], ACT.Silu
                                                 ).then_inc(s["silu"], 1)
                        if m == turned(e):
                            act.wait_ge(s["tr"], g * EPG + e + 1)
                            nc.scalar.activation(hidT[e % 2][0][:], bank(2)[:, 0:F], ACT.Identity
                                                 ).then_inc(s["hT_hi"], 1)
                    if m + STG < PER or (more and m == PER - STG):
                        high(s, g, full, first, m + STG)
                act.wait_ge(s["used"], g * PER + STG + PER)
                nc.scalar.activation(outst[:, 0:1024], psum[:, 4:6, :].rearrange("p a b -> p (a b)"),
                                     ACT.Identity).then_inc(s["oa"], 1)
                if more:
                    for m in range(PER + 1, PER + STG):
                        high(s, g, full, first, m)

            with act.Fori(0, NG - 1) as g:
                experts(main, g, mfull, first_main, True)
            experts(main, NG - 1, mfull, first_main, False)
            more = act.value_load(flags_i[0:1, 0:1], min_val=0, max_val=2)
            with act.If(more > 0):
                for m in range(STG):
                    high(extra, 0, tfull, first_main, m)
                experts(extra, 0, tfull, first_main, False)
                with act.If(more > 1):
                    for m in range(STG):
                        high(extra, 1, tfull, first_main, m)
                    experts(extra, 1, tfull, first_main, False)

            def gate_high(j):
                if j < KD:
                    act.wait_ge(mfull[j % MRING], PER * NG // MRING * 32 + 16 * (j // MRING + 1))
                    if j >= 2:
                        act.wait_ge(ple_g, j - 1)
                    nc.scalar.activation(stage[j % 2][0][:], mslots[j % MRING], ACT.Identity).then_inc(tile_high, 1)

            act.wait_ge(experts_done, 1)
            gate_high(0)
            gate_high(1)
            for k in range(KD):
                squares(2, k, XT[:, k, :])
            root(2)
            for k in range(KD):
                act.wait_ge(h_ready, 2 * KD + k + 1)
                input_high(k)
            for j in range(KD):
                act.wait_ge(ple_g, j + 1)
                gate_high(j + 2)
                if j >= 2:
                    act.wait_ge(ple_y, j - 1)
                nc.scalar.activation(sq2[:, j % 2, :], bank(j % 2, T), ACT.Sigmoid).then_inc(ple_sg, 1)
                if j % 4 == 0 and j:
                    turn_out(act, j // 4 - 1)
            turn_out(act, 3)

        def turn_out(act, q):
            act.wait_ge(ple_t, 4 * q + 4)
            for tt, (t0, n) in enumerate(TILES):
                nc.scalar.activation(ytok[0:n, tt, 512 * q:512 * (q + 1)], bank(4 + tt)[0:n, :],
                                     ACT.Identity).then_inc(ple_o, 1)

        def second_dve(dve, link, normalise, input_low):
            v = nc.vector
            for k in range(KD):
                dve.wait_ge(*freed(first_out + k))
            dve.wait_ge(pre_t, 3)
            v.tensor_copy(pT[:], psum[:, 4:6, 0:T]).then_inc(p_cp, 1)
            normalise(1, XT, V_LN2, H)
            def low(s, g, m):
                dve.wait_ge(s["high"], g * PER + m + 1)
                hi, lo = stage[m % STG]
                v.tensor_tensor(lo[:], mslots[m % MRING], hi[:].bitcast(F32), ALU.subtract).then_inc(s["split"], 1)

            low(main, 0, 0)
            dve.wait_ge(router_in, 64)
            dve.wait_ge(rl_mm, 1)
            parts = [(P, slice(0, 2), 2), (NS, slice(2, 3), 1)]
            lgp = psum[:, 1:4, :]
            gmax, gexp, gsum, eqs, r_a, r_b = r1

            def wide(ap, n):
                return ap.broadcast_to((ap.shape[0], ap.shape[1], n))

            link(v.memset(pos[:], 0.0))
            link(v.tensor_scalar(w4[:], C("iota")[:, 0:4], -1.0, 5.0, ALU.mult, ALU.add))
            for n, sl, nt in parts:
                biasb = rb[0:n].rearrange("p (t k) -> p t k", t=1).broadcast_to((n, nt, 36))
                link(v.tensor_tensor(lg[0:n, sl, :], lgp[0:n, sl, 0:36], biasb, ALU.add))
                link(v.tensor_reduce(gmax[0:n, sl, 0:1], lg[0:n, sl, 0:NG], AX_X, ALU.max))
                v.tensor_tensor(gexp[0:n, sl, :], lg[0:n, sl, 0:NG], wide(gmax[0:n, sl, 0:1], NG), ALU.subtract
                                ).then_inc(rl_x, 1)
            dve.wait_ge(rl_x, 2)
            dve.sem_inc(rl_a, 1)
            for n, sl, nt in parts:
                link(v.tensor_tensor(eqs[0:n, sl, :], lg[0:n, sl, 0:NG], wide(gmax[0:n, sl, 0:1], NG), ALU.is_equal))
                w4b = w4[0:n].rearrange("p (t k) -> p t k", t=1).broadcast_to((n, nt, NG))
                link(v.tensor_tensor(eqs[0:n, sl, :], eqs[0:n, sl, :], w4b, ALU.mult))
                link(v.tensor_reduce(r_a[0:n, sl, 0:1], eqs[0:n, sl, :], AX_X, ALU.max))
                v.tensor_tensor(goh[0:n, sl, :], eqs[0:n, sl, :], wide(r_a[0:n, sl, 0:1], NG),
                                ALU.is_equal).then_inc(goh_ready, 1)
            dve.wait_ge(goh_ready, 2)
            em, gt, pe_, eq, cum = rt
            for n, sl, nt in parts:
                link(v.tensor_scalar(r_b[0:n, sl, :], goh[0:n, sl, :], BIG, -BIG, ALU.mult, ALU.add))
                for t in range(sl.start, sl.stop):
                    link(v.tensor_tensor(em[0:n, t, :].rearrange("p (g e) -> p g e", g=NG),
                                         lg[0:n, t, NG:36].rearrange("p (g e) -> p g e", g=NG),
                                         r_b[0:n, t, :].rearrange("p (g e) -> p g e", e=1).broadcast_to((n, NG, EPG)),
                                         ALU.add))
                    link(v.max(v8[0:n, t, :], em[0:n, t, :]))
                v.tensor_tensor(pe_[0:n, sl, :], em[0:n, sl, :], wide(v8[0:n, sl, 0:1], NE), ALU.subtract
                                ).then_inc(rl_x, 1)
            dve.wait_ge(rl_x, 4)
            dve.sem_inc(rl_a, 1)
            for n, sl, nt in parts:
                link(v.tensor_tensor(gt[0:n, sl, :], em[0:n, sl, :], wide(v8[0:n, sl, 1:2], NE), ALU.is_gt))
                link(v.tensor_tensor(eq[0:n, sl, :], em[0:n, sl, :], wide(v8[0:n, sl, 1:2], NE), ALU.is_equal))
                link(v.tensor_reduce(r_a[0:n, sl, 0:1], gt[0:n, sl, :], AX_X, ALU.add))
                link(v.tensor_scalar(r_a[0:n, sl, 0:1], r_a[0:n, sl, 0:1], -1.0, 2.0, ALU.mult, ALU.add))
                for t in range(sl.start, sl.stop):
                    link(v.tensor_tensor_scan(cum[0:n, t, :], eq[0:n, t, :], eq[0:n, t, :], 0.0, ALU.add, ALU.bypass))
                link(v.tensor_tensor(cum[0:n, sl, :], cum[0:n, sl, :], wide(r_a[0:n, sl, 0:1], NE), ALU.is_le))
                link(v.tensor_tensor(cum[0:n, sl, :], cum[0:n, sl, :], eq[0:n, sl, :], ALU.mult))
                link(v.tensor_tensor(gt[0:n, sl, :], gt[0:n, sl, :], cum[0:n, sl, :], ALU.add))
            dve.wait_ge(rl_e, 4)
            for n, sl, nt in parts:
                link(v.tensor_tensor(gates[0:n, sl, :], pe_[0:n, sl, :], gt[0:n, sl, :], ALU.mult))
                link(v.tensor_reduce(r_a[0:n, sl, 0:1], gates[0:n, sl, :], AX_X, ALU.add))
                link(v.tensor_reduce(gsum[0:n, sl, 0:1], gexp[0:n, sl, :], AX_X, ALU.add))
                link(v.tensor_tensor(r_a[0:n, sl, 0:1], r_a[0:n, sl, 0:1], gsum[0:n, sl, 0:1], ALU.mult))
                link(v.reciprocal(r_a[0:n, sl, 0:1], r_a[0:n, sl, 0:1]))
                link(v.tensor_tensor(gates[0:n, sl, :], gates[0:n, sl, :], wide(r_a[0:n, sl, 0:1], NE), ALU.mult))
            dve.wait_ge(cum_mm, 1)
            for n, sl, nt in parts:
                link(v.tensor_tensor(pos[0:n, sl, :],
                                     bank(3)[:, 0:12].rearrange("p (t g) -> p t g", t=3)[0:n, sl, :],
                                     goh[0:n, sl, :], ALU.mult))
            cnt, more1, more2, a1, a2 = (fl[:, 4 * a:4 * a + 4] for a in range(5))
            out4 = fl[:, 20:24]
            link(v.tensor_copy(cnt, bank(3)[:, 16:20]))
            link(v.tensor_scalar(more1, cnt, float(P), None, ALU.is_gt))
            link(v.tensor_scalar(more2, cnt, 2.0 * P, None, ALU.is_gt))
            link(v.tensor_tensor(more2, more2, more1, ALU.add))
            link(v.tensor_reduce(out4[:, 0:1], more2, AX_X, ALU.add))
            link(v.tensor_tensor(a1, more1, w4[:], ALU.mult))
            link(v.tensor_tensor(a2, more1, C("iota")[:, 0:4], ALU.mult))
            link(v.tensor_reduce(out4[:, 1:2], a1, AX_X, ALU.max))
            link(v.tensor_reduce(out4[:, 2:3], a2, AX_X, ALU.max))
            link(v.tensor_scalar(out4[:, 1:2], out4[:, 1:2], -1.0, 4.0, ALU.mult, ALU.add))
            link(v.tensor_scalar(out4[:, 1:2], out4[:, 1:2], 3.0, None, ALU.min))
            link(v.tensor_scalar(out4[:, 2:3], out4[:, 2:3], -1.0, 0.0, ALU.add, ALU.max))
            link(v.tensor_tensor(fl[:, 24:25], out4[:, 1:2], out4[:, 2:3], ALU.is_equal))
            link(v.tensor_scalar(fl[:, 24:25], fl[:, 24:25], -float(P), -float(P), ALU.mult, ALU.add))
            link(v.tensor_copy(flags_i[0:1, 0:3], out4[0:1, 0:3]))
            dve.sem_inc(router_done, 1)
            more = dve.value_load(flags_i[0:1, 0:1], min_val=0, max_val=2)
            groups = [dve.value_load(flags_i[0:1, n:n + 1], min_val=0, max_val=NG - 1) for n in (1, 2)]

            def experts(s, g, group, shift, more):
                v.tensor_scalar(pc[:], pos[:, :, bass.ds(group, 1)].rearrange("p t a -> p (t a)"), shift, None,
                                ALU.add).then_inc(s["places"], 1)
                dve.wait_ge(s["places"], g + 1)
                for tt in range(3):
                    last = v.tensor_scalar(S[:, tt, :], C("iota"), pc[:, tt:tt + 1], None, ALU.is_equal)
                last.then_inc(s["select"], 1)
                for m in range(1, STG):
                    low(s, g, m)
                dve.wait_ge(s["st_mm"], g + 1)
                v.tensor_copy(ST[:], bank(3, T))
                v.tensor_copy(gg[:], bank(3)[:, T:T + NE]).then_inc(s["gates"], 1)
                dve.wait_ge(s["gates"], g + 1)
                v.tensor_copy(geg[:], gg[:, bass.ds(group * EPG, EPG)]).then_inc(s["st_cp"], 1)
                dve.wait_ge(s["st_cp"], g + 1)
                for q in range(4):
                    dve.wait_ge(s["hg_hi"], g * 4 + q + 1)
                    c = slice(512 * q, 512 * (q + 1))
                    v.tensor_tensor(hg[1][:, c], bank(q), hg[0][:, c].bitcast(F32), ALU.subtract
                                    ).then_inc(s["hg_cp"], 1)
                for m in range(PER):
                    for e in range(EPG):
                        if m == used_up(e) - 1:
                            dve.wait_ge(s["silu"], g * EPG + e + 1)
                            v.scalar_tensor_tensor(out=hid[:, e % 2, :], in0=bank(e % 2)[:, F:2 * F],
                                                   scalar=geg[:, e:e + 1], in1=silu[:, e % 2, :], op0=ALU.mult,
                                                   op1=ALU.mult).then_inc(s["hid"], 1)
                        if m == turned(e):
                            dve.wait_ge(s["hT_hi"], g * EPG + e + 1)
                            hi, lo = hidT[e % 2]
                            v.tensor_tensor(lo[:], bank(2)[:, 0:F], hi[:].bitcast(F32), ALU.subtract
                                            ).then_inc(s["hT"], 1)
                    if m + STG < PER or (more and m == PER - STG):
                        low(s, g, m + STG)
                dve.wait_ge(s["used"], g * PER + STG + PER)
                v.tensor_copy(outst[:, 1024:2048], psum[:, 6:8, :].rearrange("p a b -> p (a b)")).then_inc(s["ob"], 1)
                for d in range(KD):
                    dve.wait_ge(s["sc_mm"], g * KD + d + 1)
                    v.tensor_tensor(XT[:, d, :], XT[:, d, :], bank(2 + d % 2, T), ALU.add).then_inc(s["sc_add"], 1)

            with dve.Fori(0, NG - 1) as g:
                experts(main, g, g, 0.0, True)
            experts(main, NG - 1, NG - 1, 0.0, False)
            with dve.If(more > 0):
                low(extra, 0, 0)
                experts(extra, 0, groups[0], -float(P), False)
                with dve.If(more > 1):
                    low(extra, 1, 0)
                    experts(extra, 1, groups[1], fl[:, 24:25], False)
            dve.sem_inc(experts_done, 1)

            def gate_low(j):
                if j < KD:
                    dve.wait_ge(tile_high, 2 * NT + j + 1)
                    hi, lo = stage[j % 2]
                    v.tensor_tensor(lo[:], mslots[j % MRING], hi[:].bitcast(F32), ALU.subtract
                                    ).then_inc(tile_split, 1)

            gate_low(0)
            gate_low(1)
            normalise(2, XT, V_LN3, G, lambda k: input_low(2, k))
            for j in range(KD):
                gate_low(j + 2)
                dve.wait_ge(ple_sg, j + 1)
                if j >= 2:
                    dve.wait_ge(ple_t, j - 1)
                y = plg[:, j % 2, :]
                link(v.tensor_tensor(y, bank(2 + j % 2, T), sq2[:, j % 2, :], ALU.mult))
                v.tensor_tensor(y, y, XT[:, j, :], ALU.add).then_inc(ple_y, 1)

        def second_sp(sp):
            sp.wait_ge(acc_ready, first_out)
            sp.wait_ge(mix_ready, KD)
            sp.wait_ge(states_out, 64)
            sp.wait_ge(outs_out, 16 * 9)
            sp.dma_start(wr[:, :, 0:NG], A["w_rg"][0].rearrange("(k p) n -> p k n", p=P)).then_inc(router_in, 16)
            sp.dma_start(wr[:, :, NG:NG + NE], A["w_re"][0].rearrange("(k p) n -> p k n", p=P)).then_inc(router_in, 16)
            sp.dma_start(rb[:, 0:NG], A["b_rg"].partition_broadcast(P)).then_inc(router_in, 16)
            sp.dma_start(rb[:, NG:NG + NE], A["b_re"].partition_broadcast(P)).then_inc(router_in, 16)
            sp.dma_start(ptok[:, 0:2, :], A["p_prompt"][0, 0].rearrange("(t p) d -> p t d", p=P)).then_inc(ple_in, 16)
            sp.dma_start(ptok[0:NS, 2, :], A["p_sample"][0].rearrange("b t d -> (b t) d")).then_inc(ple_in, 16)

            def expert_load(m, group, full, free, count):
                ring = len(full)
                slot = mslots[m % ring]
                sp.wait_ge(free, count)
                kind, e, q = expert_slot(m)
                if kind == "up":
                    dst = slot.rearrange("p (k w f) -> p k w f", k=4, w=2)
                    for w, name in enumerate(("w1", "w3")):
                        src = A[name][0, bass.ds(group * EPG + e, 1), 512 * q:512 * (q + 1), :].rearrange(
                            "a (k p) f -> p (a k) f", p=P)
                        sp.dma_start(dst[:, :, w, :], src).then_inc(full[m % ring], 16)
                else:
                    src = A["w2"][0, bass.ds(group * EPG + e, 1), P * q:P * (q + 1), :].rearrange(
                        "a p n -> p (a n)")
                    sp.dma_start(slot[:, 0:1024], src[:, 0:1024]).then_inc(full[m % ring], 16)
                    sp.dma_start(slot[:, 1024:2048], src[:, 1024:2048]).then_inc(full[m % ring], 16)

            sp.sem_inc(main["split"], MRING)
            sp.wait_ge(acc_ready, len(units))
            with sp.Fori(0, NG) as g:
                for m in range(PER):
                    expert_load(m, g, mfull, main["split"], g * PER + m + 1)

            sp.wait_ge(router_done, 1)
            more = sp.value_load(flags_i[0:1, 0:1], min_val=0, max_val=2)

            def tail_loads(n, which):
                group = sp.value_load(flags_i[0:1, which:which + 1], min_val=0, max_val=NG - 1)
                for m in range(PER):
                    expert_load(m, group, tfull, extra["split"], n * PER + m + 1)

            with sp.If(more > 0):
                sp.wait_ge(main["split"], MRING + PER * NG)
                sp.sem_inc(extra["split"], MRING)
                tail_loads(0, 1)
                with sp.If(more > 1):
                    tail_loads(1, 2)
                    sp.wait_ge(extra["split"], MRING + 2 * PER)
                with sp.If(more < 2):
                    sp.wait_ge(extra["split"], MRING + PER)

            for j in range(KD):
                if j < MRING:
                    sp.wait_ge(main["split"], PER * NG + j + 1)
                else:
                    sp.wait_ge(tile_split, 2 * NT + j - MRING + 1)
                sp.dma_start(mslots[j % MRING].rearrange("p (k c) -> p k c", k=KD),
                             A["w_ple_gate"][0, :, P * j:P * (j + 1)].rearrange("(k p) c -> p k c", p=P)
                             ).then_inc(mfull[j % MRING], 16)
                if j == 5:
                    sp.wait_ge(ss_mm, 3 * KD)
                    sp.dma_start(proj, A["w_ple_proj"][0].rearrange("(k p) n -> p k n", p=P)).then_inc(proj_in, 16)
            for q in range(4):
                for tt, (t0, n) in enumerate(TILES):
                    sp.wait_ge(ple_o, 3 * q + tt + 1)
                    dst = O["y_prompt"][0, t0:t0 + n, 512 * q:512 * (q + 1)] if tt < 2 else O["y_sample"].rearrange(
                        "b t d -> (b t) d")[:, 512 * q:512 * (q + 1)]
                    sp.dma_start(dst, ytok[0:n, tt, 512 * q:512 * (q + 1)]).then_inc(outs_out, 16)
            sp.wait_ge(outs_out, 16 * (9 + 12))

        @block.sync
        def _(sp):
            head = const_at["utri"][0]
            sp.dma_start(const[:, 0:head], A["consts"][:, 0:head]).then_inc(consts_in, 16)
            for tt in range(2):
                sp.dma_start(xtok[:, tt, :], A["x_prompt"][0, P * tt:P * (tt + 1), :]).then_inc(x_in, 16)
            sp.dma_start(xtok[0:NS, 2, :], A["x_sample"].rearrange("b t d -> (b t) d")).then_inc(x_in, 16)
            rows = [("ln1", V_LN1, 16), ("ln2", V_LN2, 16), ("ln3", V_LN3, 16), ("conv_b", V_CB, 8), ("b_a", V_BA, 8),
                    ("b_x", V_BX, 8), ("lam", V_LAM, 8)]
            for name, at, n in rows:
                sp.dma_start(vec_raw[at:at + n, :], A[name][0].rearrange("(k p) -> k p", p=P)).then_inc(vecs_in, 16)
            sp.dma_start(vec_raw[V_CW:V_CW + 32, :],
                         A["conv_w"][0].rearrange("j (c p) -> (j c) p", p=P)).then_inc(vecs_in, 16)
            for name, at in (("q_norm", V_QN), ("k_norm", V_KN)):
                for hf in range(2):
                    sp.dma_start(vec_raw[at:at + 1, HD * hf:HD * (hf + 1)], A[name]).then_inc(vecs_in, 16)
            sp.dma_start(st_raw[0:24, :], A["state_conv"][0].rearrange("b j c -> (b j) c")).then_inc(vecs_in, 16)
            sp.dma_start(st_raw[24:32, :], A["state_h"][0]).then_inc(vecs_in, 16)

            def weight(n):
                what, _ = loads[n]
                s = slots[n % RING]
                if n >= RING and n - RING in tile_at:
                    sp.wait_ge(tile_split, 2 * tile_at[n - RING] + 2)
                elif n >= RING:
                    sp.wait_ge(acc_ready, loads[n - RING][1] + 1)
                if what[0] == "w_in":
                    _, c0, w = what
                    dst = s.rearrange("p (k c) -> p k c", k=KD)[:, :, 0:w]
                    src = A["w_in"][0, :, c0:c0 + w].rearrange("(k p) c -> p k c", p=P)
                elif what[0] == "v":
                    dst = s.rearrange("p (k c) -> p k c", k=8)
                    src = A["w_in"][0, DR * what[1]:DR * (what[1] + 1), O_V:O_V + KVW].rearrange(
                        "(k p) c -> p k c", p=P)
                elif what[0] == "w_out":
                    dst = s.rearrange("p (k c) -> p k c", k=KD)
                    src = A["w_out"][0, :, what[1]:what[1] + P].rearrange("(k p) c -> p k c", p=P)
                else:
                    dst = s.rearrange("p (k c) -> p k c", k=8)
                    src = A[what[0]][0, :, what[1]:what[1] + 2 * P].rearrange("(k p) c -> p k c", p=P)
                sp.dma_start(dst, src).then_inc(wfull[n % RING], 16)

            for n in range(RING):
                weight(n)
            sp.dma_start(const[:, head:], A["consts"][:, head:]).then_inc(consts_in, 16)
            sp.wait_ge(zeroed, 1)
            for w, name in ((wa, "w_a"), (wx, "w_x")):
                for hf in range(2):
                    sp.dma_start(w[HD * hf:HD * (hf + 1), :, HD * hf:HD * (hf + 1)],
                                 A[name][0].rearrange("(c f) i j -> f i c j", f=2)[hf]).then_inc(gates_in, 16)
            sp.wait_ge(xt_cp, KD)
            sp.dma_start(x_spill.rearrange("p (k t) -> p k t", k=KD), x0).then_inc(spill_out, 16)
            front = next(n for n in range(len(loads)) if loads[n][1] >= unit_at[("gr", 1)])
            for n in range(RING, front):
                weight(n)
            sp.wait_ge(kout_cp, 3)
            for u in (unit_at[("v", 0)], unit_at[("v", 1)]):
                sp.wait_ge(*freed(u))
            for tt, (t0, n) in enumerate(TILES):
                w = "prompt" if tt < 2 else "sample"

                def dst(name, width):
                    if tt < 2:
                        return O[f"{name}_prompt"][0, 0, t0:t0 + n].rearrange(
                            "s h d -> s (h d)" if name != "kidx" else "s d -> s d")
                    return O[f"{name}_sample"][0].rearrange(
                        "b t h d -> (b t) (h d)" if name != "kidx" else "b t d -> (b t) d")

                sp.dma_start(dst("k", KVW), kout[0:n, tt, 0:KVW]).then_inc(outs_out, 16)
                sp.dma_start(dst("kidx", HD), kout[0:n, tt, KVW:KVW + HD]).then_inc(outs_out, 16)
                sp.dma_start(dst("v", KVW), vtok[0:n, tt, :]).then_inc(outs_out, 16)
            for n in range(front, len(loads)):
                weight(n)
                kind, j, _ = units[loads[n - 4][1]]
                if j % 2 and (kind == "brr" or (kind == "gma" and j < GSPILL)):
                    for i in (j - 1, j):
                        sp.wait_ge(*freed(unit_at[(kind, i)]))
                    r = (j if kind == "brr" else KD + j) - 1
                    sp.wait_ge(spill_out, 16 * (r // 2 + 1))
                    sp.dma_start(branch_spill[:, T * r:T * (r + 2)].rearrange("p (k t) -> p k t", k=2),
                                 sgm[:, r % 4:r % 4 + 2, :]).then_inc(spill_out, 16)
                if loads[n][1] == first_bra + 1:
                    sp.wait_ge(spill_out, 16 * ((KD + GSPILL) // 2 + 1))
                    sp.wait_ge(sa_vmm, NB)
                    sp.dma_start(back, branch_spill.rearrange("p (k t) -> p k t", k=KD + GSPILL)).then_inc(spill_in, 16)
                    sp.dma_start(XT, x_spill.rearrange("p (k t) -> p k t", k=KD)).then_inc(spill_in, 16)
            sp.wait_ge(tail_cp, 2)
            sp.dma_start(O["conv_prompt"][0, 0], tail_raw[0:3, :]).then_inc(states_out, 16)
            sp.dma_start(O["conv_sample"][0].rearrange("b j c -> (b j) c"), tail_raw[3:27, :]).then_inc(states_out, 16)
            sp.dma_start(O["h_prompt"][0], tail_raw[27:28, :]).then_inc(states_out, 16)
            sp.dma_start(O["h_sample"][0], tail_raw[28:36, :]).then_inc(states_out, 16)
            second_sp(sp)

        @block.gpsimd
        def _(pool):
            nc.gpsimd.memset(wa[:], 0.0)
            nc.gpsimd.memset(wx[:], 0.0).then_inc(zeroed, 1)
            nc.gpsimd.memset(xpad[:], 0.0).then_inc(zeroed, 1)

            def page(b, g):
                return pool.value_load(A["page_table"][b:b + 1, g:g + 1], min_val=0, max_val=A["cache_k"].shape[1] - 1)

            for p in range(4):
                if p == 0:
                    pool.wait_ge(xt_cp, KD)
                if p >= 2:
                    pool.wait_ge(si_tmm, 2 * p - 2)
                for b2 in range(2):
                    for g in range(NPG):
                        r = page(2 * p + b2, g)
                        pool.dma_start(kx_raw[:, p % 2, b2, g, :],
                                       A["cache_kidx"][0, bass.ds(r, 1)].rearrange("a p d -> (a p) d")
                                       ).then_inc(kx_in[p % 2], 16)
                if p == 1:
                    pool.wait_ge(spill_out, 16)
                    pool.wait_ge(h_ready, KD)
                    nc.gpsimd.memset(qz[:], 0.0)
                    nc.gpsimd.memset(qiz[:], 0.0).then_inc(zeroed, 1)

            def low(t):
                hi, lo = stage[t % 2]
                raw = slots[tiles[t] % RING]
                for a in range(2):
                    c = slice(1024 * a, 1024 * (a + 1))
                    pool.wait_ge(tile_high, 2 * t + a + 1)
                    if a == 0:
                        pool.wait_ge(tile_split, 2 * t)
                    nc.gpsimd.tensor_tensor(lo[:, c], raw[:, c], hi[:, c].bitcast(F32), ALU.subtract
                                            ).then_inc(tile_split, 1)

            def keys(b, hf):
                if b == 0:
                    pool.wait_ge(si_tmm, 8)
                else:
                    pool.wait_ge(sa_tmm, 4 * (b - 1) + 2 * hf + 2)
                for g in range(4 * hf, 4 * hf + 4):
                    r = page(b, g)
                    pool.dma_start(k_r[:, g, :],
                                   A["cache_k"][0, bass.ds(r, 1)].rearrange("a p h d -> (a p) (h d)")
                                   ).then_inc(k_in[hf], 16)

            def values(b):
                if b == 0:
                    pool.wait_ge(pbias_ready, 2)
                else:
                    pool.wait_ge(sa_vmm, b)
                for g in range(NPG):
                    r = page(b, g)
                    pool.dma_start(v_r[:, g, :], A["cache_v"][0, bass.ds(r, 1)].rearrange("a p h d -> (a p) (h d)")
                                   ).then_inc(v_in, 16)

            for what, i in pool_steps:
                if what == "split":
                    for t in split_before[i]:
                        low(t)
                elif (what, i) == ("pa_l", 2):
                    keys(0, 0)
                    keys(0, 1)
                elif (what, i) == ("pa_l", 4):
                    values(0)
            keys(1, 0)
            keys(1, 1)
            for b in range(1, NB):
                if b < NB - 1:
                    keys(b + 1, 0)
                values(b)
                if b < NB - 1:
                    keys(b + 1, 1)

        @block.tensor
        def _(pe):
            mm = nc.tensor.matmul

            pe.wait_ge(consts_in, 16)
            pe.wait_ge(x_in, 48)

            def sum_sq(norm, k):
                pe.wait_ge(sq_ready, KD * norm + k + 1)
                mm(bank(1, T), C("ones"), (sq if norm == 0 else sq2)[:, k % 2, :], start=(k == 0),
                   stop=(k == KD - 1)).then_inc(ss_mm, 1)

            for k in range(KD):
                if k >= 4:
                    pe.wait_ge(xt_cp, k - 3)
                for tt, (t0, n) in enumerate(TILES):
                    last = nc.tensor.transpose(bank(4 + k % 4)[:, t0:t0 + n], xtok[0:n, tt, P * k:P * (k + 1)],
                                               ident[0:n, 0:n])
                last.then_inc(xt_mm, 1)
                if k >= 2:
                    sum_sq(0, k - 2)
            pe.wait_ge(vecs_in, 16 * 14)
            nc.tensor.transpose(bank(2)[:, 0:NV], vec_raw[0:NV, :], ident[0:NV, 0:NV]).then_inc(pre_t, 1)
            for c in range(CR):
                last = nc.tensor.transpose(bank(3)[:, 32 * c:32 * c + 32], st_raw[0:32, P * c:P * (c + 1)],
                                           ident[0:32, 0:32])
            last.then_inc(pre_t, 1)
            sum_sq(0, KD - 2)
            sum_sq(0, KD - 1)

            opened = set()

            def first_half(u):
                opened.add(u)
                unit(u, range(KD // 2))

            def unit(u, ks=None):
                kind, i, ls = units[u]
                if ks is None:
                    ks = range(KD // 2 if u in opened else 0, KD)
                if ks[0] == 0 and u >= 2:
                    pe.wait_ge(acc_free[u % 2], u // 2)
                acc = bank(u % 2)
                if kind == "v":
                    for tt in ((0, 1) if i == 0 else (2,)):
                        t0, n = TILES[tt]
                        for k in range(KD):
                            t = tile_at[ls[k // 8]]
                            if tt == 0 and k % 4 == 0:
                                pe.wait_ge(tile_split, 2 * t + k % 8 // 4 + 1)
                            for a, (x, y) in enumerate(parts3(parts_in[k], stage[t % 2])):
                                last = mm(acc[0:n, KVW * (tt % 2):KVW * (tt % 2 + 1)], x[:, t0:t0 + n],
                                          y[:, KVW * (k % 8):KVW * (k % 8 + 1)], start=(k == 0 and a == 0),
                                          stop=(k == KD - 1 and a == 2))
                elif kind in ("ga", "gx"):
                    if kind == "ga" and i == 0:
                        pe.wait_ge(gates_in, 64)
                    pe.wait_ge(conv_ready, i + 1)
                    last = mm(acc[:, 0:XC], (wa if kind == "ga" else wx)[:, i, :], xc[:, i % 2, :], start=True,
                              stop=True)
                elif kind in ("brr", "bra"):
                    pe.wait_ge(wfull[ls[0] % RING], 16 * (ls[0] // RING + 1))
                    if kind == "brr":
                        pe.wait_ge(lru_done, CR)
                    w = slots[ls[0] % RING].rearrange("p (k c) -> p k c", k=8)[:, :, P * (i % 2):P * (i % 2 + 1)]
                    for k in range(8):
                        last = mm(acc[:, 0:T], w[:, k, :], (rnnT if kind == "brr" else qT)[:, k, :], start=(k == 0),
                                  stop=(k == 7))
                else:
                    t = tile_at[ls[0]]
                    m = HD + NIH if kind == "ki" else P
                    for k in ks:
                        if k % 8 == 0:
                            pe.wait_ge(tile_split, 2 * t + k // 8 + 1)
                        if u == 0:
                            pe.wait_ge(in_split, k + 1)
                        if u == first_out:
                            pe.wait_ge(in_split, KD + k + 1)
                        for n, (x, y) in enumerate(parts3(stage[t % 2], parts_in[k])):
                            last = mm(acc[0:m, 0:T], x[:, P * k:P * k + m], y[:],
                                      start=(k == 0 and n == 0), stop=(k == KD - 1 and n == 2))
                if ks[-1] == KD - 1:
                    last.then_inc(acc_ready, 1)

            def rope(t):
                kind, i = ropes[t]
                u = unit_at[(kind, i)]
                pe.wait_ge(*freed(u))
                if t >= 2:
                    pe.wait_ge(rope_out, t - 1)
                m = HD if kind == "ki" else P
                if kind in "qk":
                    mm(bank(2 + 2 * (t % 2), T), C("bones"), sq[:, t % 2, :], start=True, stop=True)
                mm(bank(3 + 2 * (t % 2))[0:m, 0:T], C("rot")[0:m, 0:m], ropeb[0:m, t % 2, :], start=True,
                   stop=True).then_inc(rope_mm, 1)

            pe.wait_ge(consts_in, 32)
            for t in range(len(ropes)):
                unit(unit_at[ropes[t]])
                if t:
                    rope(t - 1)
            unit(unit_at[("v", 0)])
            rope(len(ropes) - 1)
            unit(unit_at[("v", 1)])
            pe.wait_ge(*freed(unit_at[("ki", 0)]))
            pe.wait_ge(rope_out, len(ropes))
            for qt in range(2):
                nc.tensor.transpose(bank(2)[:, NIH * qt:NIH * (qt + 1)], wiT[0:NIH, P * qt:P * (qt + 1)],
                                    ident[0:NIH, 0:NIH])
            mm(bank(3)[:, 0:NS], C("e8")[0:NIH, :], wiT[0:NIH, SEQ:T], start=True, stop=True).then_inc(wi_mm, 1)
            for tt, (t0, n) in enumerate(TILES):
                if tt == 2:
                    pe.wait_ge(kout_cp, 1)
                b = 6 + tt % 2
                for j in range(2):
                    nc.tensor.transpose(bank(b)[0:n, P * j:P * (j + 1)], kT[:, j, t0:t0 + n], ident)
                nc.tensor.transpose(bank(b)[0:n, KVW:KVW + HD], kiT[0:HD, t0:t0 + n],
                                    ident[0:HD, 0:HD]).then_inc(kout_mm, 1)
            pe.wait_ge(prep_done, 1)

            def half(ap, h):
                return ap[HD * h:HD * (h + 1)]

            def pi(qt):
                if qt == 0:
                    pe.wait_ge(wi_done, 1)
                    pe.wait_ge(kout_cp, 3)
                else:
                    pe.wait_ge(pi_read, 1)
                nk = P * (qt + 1)
                for h in range(NIH):
                    b, c = 2 + 2 * (h % 2) + h // 4, 256 * (h // 2 % 2)
                    last = mm(psum[:, b, c:c + nk],
                              half(qiT, h % 2)[:, h // 2, P * qt:P * (qt + 1)], half(kiT, h % 2)[:, 0:nk],
                              start=True, stop=True)
                last.then_inc(pi_mm, 1)

            def si_t(x):
                p, c = divmod(x, 3)
                if c == 2:
                    return
                if c == 0:
                    pe.wait_ge(kx_in[p % 2], 16 * 16 * (p // 2 + 1))
                n = 2 * p + c
                if n == 0:
                    pe.wait_ge(pi_read, 2)
                else:
                    pe.wait_ge(kx_cp, n)
                for b2 in range(2):
                    for g in range(4):
                        last = nc.tensor.transpose(bank(2 + b2)[0:HD, P * g:P * (g + 1)],
                                                   kx_raw[:, p % 2, b2, 4 * c + g, :], ident)
                last.then_inc(si_tmm, 1)

            def si_s(x):
                p, c = divmod(x, 3)
                if c < 2:
                    pe.wait_ge(kx_dup, 2 * p + c + 1)
                if x:
                    pe.wait_ge(si_relu, x)
                w = 512 if c < 2 else NS
                for b2 in range(2):
                    last = mm(bank(4)[HD * b2:HD * (b2 + 1), 0:w], qiz[:, 2 * p + b2, :],
                              kxT[:, b2, 512 * c:512 * c + w], start=True, stop=True)
                last.then_inc(si_smm, 1)

            def si_w(x):
                p, c = divmod(x, 3)
                pe.wait_ge(si_relu, x + 1)
                w = 512 if c < 2 else NS
                mm(bank(5 + c)[0:NS, 0:w], wp[:, p, :], srelu[:, x % 2, 0:w], start=(p == 0),
                   stop=(p == 3)).then_inc(si_wmm, 1)

            def pa_l(m):
                qt, g = divmod(m, NKV)
                if m == 0:
                    pe.wait_ge(kx_cp, 8)
                    pe.wait_ge(sc_read, 1)
                else:
                    pe.wait_ge(pa_lg, m)
                nk = P * (qt + 1)
                for i in range(4):
                    h = 4 * g + i
                    src = kT if g % 2 == h % 2 else kTs
                    last = mm(psum[:, 2 + i % 2, 256 * (i // 2):256 * (i // 2) + nk],
                              half(qT, h % 2)[:, h // 2, P * qt:P * (qt + 1)], half(src, h % 2)[:, g // 2, 0:nk],
                              start=True, stop=True)
                last.then_inc(pa_lmm, 1)

            def pa_t(m):
                qt, g = divmod(m, NKV)
                pe.wait_ge(pa_prob, m + 1)
                if m:
                    pe.wait_ge(pa_pT, m)
                pl = prob[:, 0:4 * P * (qt + 1)].rearrange("p (h k) -> p h k", h=4)
                for kb in range(qt + 1):
                    for i in range(4):
                        last = nc.tensor.transpose(bank(4 + kb)[:, P * i:P * (i + 1)],
                                                   pl[:, i, P * kb:P * (kb + 1)], ident)
                last.then_inc(pa_tmm, 1)

            def pa_v(m):
                qt, g = divmod(m, NKV)
                pe.wait_ge(pa_pT, m + 1)
                if m:
                    pe.wait_ge(pa_out, m)
                for ip in range(2):
                    for kb in range(qt + 1):
                        last = mm(bank(6)[HD * ip:HD * (ip + 1), 0:2 * P], vtok[:, kb, HD * g:HD * (g + 1)],
                                  pT4[:, kb, 2 * ip:2 * ip + 2, :], start=(kb == 0),
                                  stop=(kb == qt))
                last.then_inc(pa_vmm, 1)

            def sa_t(x):
                b, hp = divmod(x, 2)
                pe.wait_ge(k_in[hp], 16 * 4 * (b + 1))
                if x == 0:
                    pe.wait_ge(pa_lg, 8)
                elif x >= 3:
                    pe.wait_ge(sa_pT, (x - 1) // 2)
                for j in range(2):
                    s = 2 * hp + j
                    if 4 * b + s >= 2:
                        pe.wait_ge(sa_kcp, 4 * b + s - 1)
                    for g in range(4):
                        last = nc.tensor.transpose(bank(2 + s % 2)[:, P * g:P * (g + 1)],
                                                   k_r[:, 4 * hp + g, P * j:P * (j + 1)], ident)
                    last.then_inc(sa_tmm, 1)

            def sa_l(b):
                pe.wait_ge(sa_kcp, 4 * b + 4)
                if b == 0:
                    pe.wait_ge(sbias_ready, 2)
                    pe.wait_ge(pa_pT, 8)
                    pe.wait_ge(pa_out, 8)
                else:
                    pe.wait_ge(sa_exp, b)
                for c in range(3):
                    w = 512 if c < 2 else NS
                    mm(bank(5 + c, w), C("rep")[0:NS, P * b:P * (b + 1)], score[0:NS, 512 * c:512 * c + w],
                       start=True, stop=False)
                    for j in range(2):
                        last = mm(bank(5 + c, w), qz[:, j, b, :], KT[:, j, 512 * c:512 * c + w], start=False,
                                  stop=(j == 1))
                last.then_inc(sa_lmm, 1)

            def sa_p(b):
                pe.wait_ge(sa_prob, b + 1)
                if b < NB - 1:
                    pe.wait_ge(sa_kcp, 4 * b + 6)
                if b:
                    pe.wait_ge(sa_out, b)
                for g in range(8):
                    nc.tensor.transpose(bank(2 + g // 4)[:, P * (g % 4):P * (g % 4 + 1)], prob[:, P * g:P * (g + 1)],
                                        ident)
                nc.tensor.transpose(bank(4)[0:NS, 0:P], prob[:, PAST:KEYS], ident).then_inc(sa_pmm, 1)

            def sa_v(b):
                pe.wait_ge(sa_pT, b + 1)
                pe.wait_ge(v_in, 16 * NPG * (b + 1))
                for j in range(2):
                    out = bank(4)[:, 64 * j:64 * (j + 1)]
                    for g in range(9):
                        if g < 8:
                            last = mm(out, v_r[:, g, P * j:P * (j + 1)], probT3[:, g, 64 * j:64 * (j + 1)],
                                      start=(g == 0), stop=False)
                        else:
                            last = mm(out, vtok[0:NS, 2, P * j:P * (j + 1)], probT3[0:NS, 8, 64 * j:64 * (j + 1)],
                                      start=False, stop=True)
                last.then_inc(sa_vmm, 1)

            todo = {"pi": pi, "si_t": si_t, "si_s": si_s, "si_w": si_w, "pa_l": pa_l, "pa_t": pa_t, "pa_v": pa_v,
                    "sa_t": sa_t, "sa_l": sa_l, "sa_p": sa_p, "sa_v": sa_v, "half": first_half, "unit": unit}
            for what, i in steps:
                if what in todo:
                    todo[what](i)
            pe.wait_ge(lru_done, CR)
            pe.wait_ge(sa_pT, NB)
            for c in range(CR):
                nc.tensor.transpose(bank(2 + c // 4)[0:36, P * (c % 4):P * (c % 4 + 1)], tail[:, c, :],
                                    ident).then_inc(tail_mm, 1)
            pe.wait_ge(sa_out, NB)
            for u in range(first_bra, len(units)):
                unit(u)
            second_pe(pe, sum_sq)

        @block.scalar
        def _(act):
            act_n = [0]

            def link(ins):
                act_n[0] += 1
                ins.then_inc(act_chain, 1)
                act.wait_ge(act_chain, act_n[0])

            def squares(norm, k, src):
                if k >= 2:
                    act.wait_ge(ss_mm, KD * norm + k - 1)
                nc.scalar.activation((sq if norm == 0 else sq2)[:, k % 2, :], src, ACT.Square).then_inc(sq_ready, 1)

            def root(norm):
                act.wait_ge(var_ready, norm + 1)
                nc.scalar.activation(rstd[:], rstd[:], ACT.Sqrt).then_inc(rstd_ready, 1)

            for k in range(KD):
                act.wait_ge(xt_cp, k + 1)
                squares(0, k, x0[:, k, :])
            act.wait_ge(lam_dve, 1)
            link(nc.scalar.activation(spt[:, 1, :], spt[:, 0, :], ACT.Abs))
            nc.scalar.activation(spt[:, 1, :], spt[:, 1, :], ACT.Exp, scale=-1.0).then_inc(lam_act, 1)

            def high(t):
                n = tiles[t]
                act.wait_ge(wfull[n % RING], 16 * (n // RING + 1))
                if t >= 2:
                    act.wait_ge(acc_ready, loads[tiles[t - 2]][1] + 1)
                for a in range(2):
                    c = slice(1024 * a, 1024 * (a + 1))
                    nc.scalar.activation(stage[t % 2][0][:, c], slots[n % RING][:, c], ACT.Identity
                                         ).then_inc(tile_high, 1)

            def input_high(k):
                nc.scalar.activation(parts_in[k][0][:], G[:, k, :], ACT.Identity).then_inc(in_high, 1)

            for t in split_before[0]:
                high(t)
            root(0)
            for k in range(KD):
                act.wait_ge(h_ready, k + 1)
                input_high(k)

            def evac(u):
                kind, i, _ = units[u]
                acc = bank(u % 2)
                if kind == "bra":
                    act.wait_ge(mix_ready, i + 1)
                    input_high(i)
                if kind in ("brr", "bra", "out"):
                    return
                act.wait_ge(acc_ready, u + 1)
                free = acc_free[u % 2]
                if kind in ("q", "k", "qi", "ki"):
                    t = ropes.index((kind, i))
                    m = HD if kind == "ki" else P
                    if t >= 2:
                        act.wait_ge(rope_out, t - 1)
                    if kind in "qk":
                        at = V_QN if kind == "q" else V_KN
                        nc.scalar.activation(ropeb[:, t % 2, :], acc[:, 0:T], ACT.Identity, scale=vec[:, at:at + 1])
                        nc.scalar.activation(sq[:, t % 2, :], acc[:, 0:T], ACT.Square).then_inc(free, 1)
                    else:
                        if kind == "ki":
                            nc.scalar.activation(wiT[0:NIH, :], acc[HD:HD + NIH, 0:T], ACT.Identity, scale=WI_SCALE)
                        nc.scalar.activation(ropeb[0:m, t % 2, :], acc[0:m, 0:T], ACT.Identity).then_inc(free, 1)
                elif kind == "v" and i == 0:
                    nc.scalar.activation(vtok[:, 0:2, :], acc.rearrange("p (t d) -> p t d", t=2),
                                         ACT.Identity).then_inc(free, 1)
                elif kind == "v":
                    nc.scalar.activation(vtok[0:NS, 2, :], acc[0:NS, 0:KVW], ACT.Identity).then_inc(free, 1)
                elif kind == "xr":
                    if i == 0:
                        act.wait_ge(zeroed, 2)
                    if i >= 2:
                        act.wait_ge(conv_ready, i - 1)
                    if i == 0 or i >= 2:
                        act.wait_ge(pre_cp, 2)
                    seg = xpad[:, i % 2, S0:XP].rearrange("p (b s) -> p b s", b=NB)
                    nc.scalar.activation(xpad[:, i % 2, PAD:S0], acc[:, 0:SEQ], ACT.Identity)
                    nc.scalar.activation(seg[:, :, 0:PAD], stT[:, i, 0:24].rearrange("p (b j) -> p b j", b=NB),
                                         ACT.Identity)
                    nc.scalar.activation(seg[:, :, PAD:SEGB], acc[:, SEQ:T].rearrange("p (b t) -> p b t", b=NB),
                                         ACT.Identity).then_inc(free, 1)
                    if i >= 2:
                        lru_root(i - 2)
                elif kind == "gr":
                    if i == 0:
                        act.wait_ge(spill_out, 16)
                    nc.scalar.activation(rnnT[:, i, :], acc[:, 0:T], ACT.Gelu_apprx_tanh).then_inc(free, 1)
                elif kind == "ga":
                    if i == CR - 1:
                        lru_root(CR - 2)
                    nc.scalar.activation(g_r[:], acc[:, 0:XC], ACT.Sigmoid, bias=vec[:, V_BA + i:V_BA + i + 1]
                                         ).then_inc(free, 1)
                elif kind == "gx":
                    if i == 0:
                        act.wait_ge(lam_dve, 2)
                    else:
                        act.wait_ge(lru_done, i)
                    nc.scalar.activation(g_i[:], acc[:, 0:XC], ACT.Sigmoid, bias=vec[:, V_BX + i:V_BX + i + 1]
                                         ).then_inc(free, 1)
                    act.wait_ge(*freed(u))
                    nc.scalar.activation(g_th[:], g_r[:], ACT.Tanh, scale=sp8[:, i:i + 1])
                    nc.scalar.activation(g_a[:], g_r[:], ACT.Exp, scale=nsp8[:, i:i + 1]).then_inc(lru_a, 1)
                    if i == CR - 1:
                        lru_root(CR - 1)
                elif kind in ("gmr", "gma"):
                    r = i if kind == "gmr" else KD + i
                    if r >= 4:
                        act.wait_ge(spill_out, 16 * (r // 2))
                    nc.scalar.activation(sgm[:, i % 4, :], acc[:, 0:T], ACT.Sigmoid).then_inc(free, 1)

            def highs(u):
                for t in split_before[u]:
                    high(t)

            def lru_root(c):
                act.wait_ge(lru_w, c + 1)
                nc.scalar.activation(g_th[:], g_th[:], ACT.Sqrt, scale=2.0).then_inc(lru_s, 1)

            def rope_root(t):
                if ropes[t][0] in "qk":
                    act.wait_ge(rope_var, t + 1)
                    nc.scalar.activation(rstd[:], rstd[:], ACT.Sqrt).then_inc(rope_rstd, 1)

            for t in range(len(ropes)):
                if t:
                    highs(unit_at[ropes[t]])
                evac(unit_at[ropes[t]])
                if t:
                    rope_root(t - 1)
            for i in range(2):
                highs(unit_at[("v", i)])
                evac(unit_at[("v", i)])

            def si_t(x):
                p, c = divmod(x, 3)
                if c == 2:
                    return
                n = 2 * p + c
                act.wait_ge(si_tmm, n + 1)
                if p:
                    act.wait_ge(si_smm, 3 * (p - 1) + c + 1)
                nc.scalar.activation(kxT[0:HD, 0, 512 * c:512 * (c + 1)], bank(2)[0:HD, :], ACT.Identity)
                nc.scalar.activation(kxT[0:HD, 1, 512 * c:512 * (c + 1)], bank(3)[0:HD, :],
                                     ACT.Identity).then_inc(kx_cp, 1)

            def si_s(x):
                w = 512 if x % 3 < 2 else NS
                act.wait_ge(si_smm, x + 1)
                if x == 0:
                    act.wait_ge(outs_out, 16 * 9)
                if x >= 2:
                    act.wait_ge(si_wmm, x - 1)
                nc.scalar.activation(srelu[:, x % 2, 0:w], bank(4, w), ACT.Relu).then_inc(si_relu, 1)

            def pa_l(m):
                nk = P * (m // NKV + 1)
                act.wait_ge(pa_nb, m + 1)
                pl = prob[:, 0:4 * nk].rearrange("p (h k) -> p h k", h=4)
                for i in range(4):
                    last = nc.scalar.activation(pl[:, i, :], pl[:, i, :], ACT.Exp, bias=small[:, 4 + i:5 + i],
                                                scale=QK_SCALE, accum_out=small[:, 8 + i:9 + i])
                last.then_inc(pa_exp, 1)

            def pa_t(m):
                qt = m // NKV
                act.wait_ge(pa_tmm, m + 1)
                if m:
                    act.wait_ge(pa_vmm, m)
                for kb in range(qt + 1):
                    last = nc.scalar.activation(pT4[:, kb], bank(4 + kb).rearrange("p (h q) -> p h q", h=4),
                                                ACT.Identity)
                last.then_inc(pa_pT, 1)

            def sa_t(x):
                b, hp = divmod(x, 2)
                for j in range(2):
                    s = 2 * hp + j
                    act.wait_ge(sa_tmm, 4 * b + s + 1)
                    if b == 0:
                        act.wait_ge(sbias_ready, 1)
                    else:
                        act.wait_ge(sa_lmm, b)
                    nc.scalar.activation(KT[:, j, 512 * hp:512 * (hp + 1)], bank(2 + s % 2),
                                         ACT.Identity).then_inc(sa_kcp, 1)

            def sa_l(b):
                act.wait_ge(sa_nb, b + 1)
                if b:
                    act.wait_ge(sa_pmm, b)
                else:
                    act.wait_ge(pa_tmm, 8)
                logits = psum[:, 5:8, :].rearrange("p a b -> p (a b)")[:, 0:KEYS]
                nc.scalar.activation(prob[:], logits, ACT.Exp, bias=small[:, 17:18], scale=QK_SCALE,
                                     accum_out=small[:, 18:19]).then_inc(sa_exp, 1)

            def sa_p(b):
                act.wait_ge(sa_pmm, b + 1)
                if b:
                    act.wait_ge(sa_vmm, b)
                else:
                    act.wait_ge(pa_vmm, 8)
                nc.scalar.activation(probT[:, 0:512], bank(2), ACT.Identity)
                nc.scalar.activation(probT[:, 512:1024], bank(3), ACT.Identity)
                nc.scalar.activation(probT[0:NS, 1024:1152], bank(4)[0:NS, 0:P], ACT.Identity).then_inc(sa_pT, 1)

            todo = {"split": highs, "si_t": si_t, "si_s": si_s, "pa_l": pa_l, "pa_t": pa_t, "sa_t": sa_t, "sa_l": sa_l,
                    "sa_p": sa_p,
                    "unit": evac}
            for what, i in steps:
                if what in todo:
                    todo[what](i)
            act.wait_ge(sa_lmm, NB)
            act.wait_ge(tail_mm, CR)
            act.wait_ge(sa_vmm, NB)
            for hf in range(2):
                nc.scalar.activation(tail_raw[0:36, 512 * hf:512 * (hf + 1)], bank(2 + hf)[0:36, :],
                                     ACT.Identity).then_inc(tail_cp, 1)
            for u in range(first_bra, len(units)):
                highs(u)
                evac(u)
            second_act(act, squares, root, input_high)

        @block.vector
        def _(dve):
            v = nc.vector
            dve_n = [0]

            def link(ins):
                dve_n[0] += 1
                ins.then_inc(dve_chain, 1)
                dve.wait_ge(dve_chain, dve_n[0])

            for k in range(KD):
                dve.wait_ge(xt_mm, k + 1)
                v.tensor_copy(x0[:, k, :], bank(4 + k % 4, T)).then_inc(xt_cp, 1)
            dve.wait_ge(pre_t, 1)
            link(v.tensor_copy(vec[:], bank(2)[:, 0:NV]))
            v.tensor_scalar(spt[:, 0, :], vec[:, V_LAM:V_LAM + CR], -1.0, None, ALU.mult).then_inc(lam_dve, 1)
            dve.wait_ge(pre_t, 2)
            v.tensor_copy(stT[:], bank(3)[:, 0:256].rearrange("p (c s) -> p c s", c=CR)).then_inc(pre_cp, 2)

            def decay_rate():
                dve.wait_ge(lam_act, 1)
                e, z, z2, acc = spt[:, 1, :], spt[:, 2, :], spt[:, 3, :], sp8[:]
                link(v.tensor_scalar(z, e, 2.0, None, ALU.add))
                link(v.reciprocal(z, z))
                link(v.tensor_tensor(z, z, e, ALU.mult))
                link(v.tensor_tensor(z2, z, z, ALU.mult))
                link(v.tensor_scalar(acc, z2, 1.0 / 19, 1.0 / 17, ALU.mult, ALU.add))
                for n in range(15, 0, -2):
                    link(v.tensor_tensor(acc, acc, z2, ALU.mult))
                    link(v.tensor_scalar(acc, acc, 1.0 / n, None, ALU.add))
                link(v.tensor_tensor(acc, acc, z, ALU.mult))
                link(v.tensor_scalar(acc, acc, 16.0, None, ALU.mult))
                link(v.tensor_scalar(z, spt[:, 0, :], 0.0, 8.0, ALU.max, ALU.mult))
                link(v.tensor_tensor(acc, acc, z, ALU.add))
                v.tensor_scalar(nsp8[:], acc, -1.0, None, ALU.mult).then_inc(lam_dve, 1)

            def normalise(norm, src, at, dst, also=None):
                dve.wait_ge(ss_mm, KD * (norm + 1))
                link(v.tensor_scalar(rstd[:], bank(1, T), 1.0 / D, EPS, ALU.mult, ALU.add))
                v.reciprocal(rstd[:], rstd[:]).then_inc(var_ready, 1)
                dve.wait_ge(rstd_ready, norm + 1)
                for k in range(KD):
                    v.scalar_tensor_tensor(out=dst[:, k, :], in0=src[:, k, :], scalar=vec[:, at + k:at + k + 1],
                                           in1=rstd[:], op0=ALU.mult, op1=ALU.mult).then_inc(h_ready, 1)
                    if also and k >= 2:
                        also(k - 2)
                if also:
                    also(KD - 2)
                    also(KD - 1)

            def low(t):
                hi, lo = stage[t % 2]
                raw = slots[tiles[t] % RING]
                for a in range(2):
                    c = slice(1024 * a, 1024 * (a + 1))
                    dve.wait_ge(tile_high, 2 * t + a + 1)
                    if a == 0 and t - 1 in on_pool:
                        dve.wait_ge(tile_split, 2 * t)
                    v.tensor_tensor(lo[:, c], raw[:, c], hi[:, c].bitcast(F32), ALU.subtract).then_inc(tile_split, 1)

            def input_low(n, k):
                dve.wait_ge(in_high, KD * n + k + 1)
                hi, lo = parts_in[k]
                v.tensor_tensor(lo[:], G[:, k, :], hi[:].bitcast(F32), ALU.subtract).then_inc(in_split, 1)

            def lows(u):
                for t in split_before[u]:
                    if t not in on_pool:
                        low(t)

            low(0)
            normalise(0, x0, V_LN1, G, lambda k: input_low(0, k))
            low(1)
            decay_rate()

            def rope(t):
                kind, i = ropes[t]
                dst = {"q": qT, "k": kT, "qi": qiT}[kind][:, i, :] if kind != "ki" else kiT[0:HD, :]
                m = HD if kind == "ki" else P
                x = ropeb[0:m, t % 2, :]
                dve.wait_ge(rope_mm, t + 1)
                if kind in "qk":
                    dve.wait_ge(h_ready, KD)
                    if t:
                        dve.wait_ge(rope_out, t)
                    link(v.tensor_scalar(rstd[:], bank(2 + 2 * (t % 2), T), 1.0 / HD, EPS, ALU.mult, ALU.add))
                    v.reciprocal(rstd[:], rstd[:]).then_inc(rope_var, 1)
                v.tensor_tensor(x, x, C("cos")[0:m], ALU.mult)
                link(v.tensor_tensor(dst, bank(3 + 2 * (t % 2))[0:m, 0:T], C("sin")[0:m], ALU.mult))
                if kind in "qk":
                    link(v.tensor_tensor(x, x, dst, ALU.add))
                    dve.wait_ge(rope_rstd, t + 1)
                    v.tensor_tensor(dst, x, rstd[:], ALU.mult).then_inc(rope_out, 1)
                else:
                    v.tensor_tensor(dst, x, dst, ALU.add).then_inc(rope_out, 1)

            for t in range(len(ropes)):
                lows(unit_at[ropes[t]] + 1)
                rope(t)
            lows(unit_at[("v", 1)])
            dve.wait_ge(rope_out, len(ropes))
            dve.wait_ge(zeroed, 3)
            for hf in range(2):
                v.tensor_copy(kTs[HD * hf:HD * (hf + 1)], kT[HD * (1 - hf):HD * (2 - hf)])
            link(v.tensor_copy(kiT[HD:P, :], kiT[0:HD, :]))
            for hf in range(2):
                v.tensor_copy(qiz[HD * hf:HD * (hf + 1)].rearrange("p b (a f t) -> p a b f t", a=4, f=2)[:, :, :, hf, :],
                              qiT[HD * hf:HD * (hf + 1), :, SEQ:T].rearrange("p a (b t) -> p a b t", b=NB))
            for g in range(NKV):
                j, pp = divmod(g, 2)
                for i in range(4):
                    h = 4 * g + i
                    v.tensor_copy(qz[HD * pp:HD * (pp + 1), j, :, TS * h:TS * (h + 1)],
                                  qT[HD * (h % 2):HD * (h % 2 + 1), h // 2, SEQ:T].rearrange("p (b t) -> p b t", b=NB))
            dve.wait_ge(xt_cp, KD)
            for b2 in range(2):
                last = v.tensor_copy(kxT[:, b2, PAST:KEYS], kiT[:, SEQ:T])
            last.then_inc(prep_done, 1)
            dve.wait_ge(wi_mm, 1)
            v.tensor_copy(wtok.rearrange("p t (f a) -> p t f a", f=2),
                          bank(2)[:, 0:2 * NIH].rearrange("p (t a f) -> p t f a", t=2, f=2))
            v.tensor_tensor(wp[:], C("mpair").rearrange("p (a s) -> p a s", a=4),
                            bank(3)[:, 0:NS].rearrange("p (a s) -> p a s", a=1).broadcast_to((P, 4, NS)),
                            ALU.mult).then_inc(wi_done, 1)
            for tt, (t0, n) in enumerate(TILES):
                dve.wait_ge(kout_mm, tt + 1)
                v.tensor_copy(kout[0:n, tt, :], bank(6 + tt % 2)[0:n, 0:320]).then_inc(kout_cp, 1)

            def select(sc, scr, n, k, thr, causal, done):
                gt, eq, cum = scr
                r = sc.shape[0]
                cnt = small[0:r, 20:21]
                link(v.tensor_scalar(gt, sc, thr, 0.0, ALU.is_gt, ALU.add, accum_out=cnt))
                v.tensor_scalar(eq, sc, thr, None, ALU.is_equal)
                link(v.tensor_scalar(cnt, cnt, -1.0, float(k), ALU.mult, ALU.add))
                link(v.tensor_tensor_scan(cum, eq, eq, 0.0, ALU.add, ALU.bypass))
                link(v.scalar_tensor_tensor(out=eq, in0=cum, scalar=cnt, in1=eq, op0=ALU.is_le, op1=ALU.mult))
                link(v.tensor_tensor(gt, gt, eq, ALU.add))
                if causal:
                    link(v.tensor_tensor(gt[:, n - P:n], gt[:, n - P:n], C("tri"), ALU.mult))
                v.tensor_scalar(sc, gt, BIG, -BIG, ALU.mult, ALU.add).then_inc(done, 1)

            def pi(qt):
                nk = P * (qt + 1)
                dve.wait_ge(pi_mm, qt + 1)
                s = psum[:, 2:6, :].rearrange("p a (b k) -> p (a b) k", b=2)[:, :, 0:nk]
                wb = wtok[:, qt, :].rearrange("p (h k) -> p h k", k=1).broadcast_to((P, NIH, nk))
                v.scalar_tensor_tensor(out=pi_tmp[:, :, 0:nk], in0=s, scalar=0.0, in1=wb, op0=ALU.max,
                                       op1=ALU.mult).then_inc(pi_read, 1)
                dve.wait_ge(pi_read, qt + 1)
                sc = pbias[qt]
                v.tensor_reduce(sc[:, 0:nk], pi_tmp[:, :, 0:nk].rearrange("p h k -> p k h"), AX_X,
                                ALU.add).then_inc(pi_red, 1)
                dve.wait_ge(pi_red, qt + 1)
                link(v.tensor_tensor(sc[:, nk - P:nk], sc[:, nk - P:nk], C("tri"), ALU.mult))
                link(v.tensor_tensor(sc[:, nk - P:nk], sc[:, nk - P:nk], C("trib"), ALU.add))

            def ptk(x):
                qt, part = divmod(x, 3)
                nk = P * (qt + 1)
                w = vraw[:, 0:nk]
                sc = pbias[qt][:, 0:nk]
                if part == 0:
                    link(v.tensor_copy(w, sc))
                if part < 2:
                    for it in range(4 * part, 4 * part + 4):
                        link(v.max(m8[:], w))
                        if it < TOPK_P // 8 - 1:
                            link(v.match_replace(w, m8[:], w, FMIN))
                    return
                select(sc, [vraw[:, 256 * (a + 1):256 * (a + 1) + nk] for a in range(3)], nk, TOPK_P, m8[:, 7:8], True,
                       pbias_ready)

            def si_t(x):
                p, c = divmod(x, 3)
                if c == 2:
                    return
                dve.wait_ge(kx_cp, 2 * p + c + 1)
                v.tensor_copy(kxT[HD:P, :, 512 * c:512 * (c + 1)],
                              kxT[0:HD, :, 512 * c:512 * (c + 1)]).then_inc(kx_dup, 1)

            def sc(_):
                dve.wait_ge(si_wmm, 12)
                v.tensor_copy(score[0:NS, 0:PAST], psum[0:NS, 5:7, :].rearrange("p a b -> p (a b)"))
                link(v.tensor_tensor(score[0:NS, PAST:KEYS], bank(7)[0:NS, 0:NS], C("nk")[0:NS], ALU.mult))
                v.tensor_tensor(score[0:NS, PAST:KEYS], score[0:NS, PAST:KEYS], C("nkb")[0:NS],
                                ALU.add).then_inc(sc_read, 1)
                dve.wait_ge(sc_read, 1)
                link(v.tensor_copy(work[0:NS, :], score[0:NS, :]))

            def tk(it):
                link(v.max(small[0:NS, 24:32], work[0:NS, :]))
                if it < TOPK_S // 8 - 1:
                    link(v.match_replace(work[0:NS, :], small[0:NS, 24:32], work[0:NS, :], FMIN))

            def sel(_):
                dve.wait_ge(pa_tmm, 8)
                select(score[0:NS, :], [work[0:NS, :], eqb[0:NS, :], prob[0:NS, :]], KEYS, TOPK_S, small[0:NS, 31:32],
                       False, sbias_ready)
                dve.wait_ge(sbias_ready, 1)
                for j in range(2):
                    last = v.tensor_copy(KT[:, j, PAST:KEYS], kT[:, j, SEQ:T])
                last.then_inc(sbias_ready, 1)

            def pa_l(m):
                nk = P * (m // NKV + 1)
                dve.wait_ge(pa_lmm, m + 1)
                if m:
                    dve.wait_ge(pa_tmm, m)
                pl = prob[:, 0:4 * nk].rearrange("p (h k) -> p h k", h=4)
                s = psum[:, 2:4, :].rearrange("p a (b k) -> p (a b) k", b=2)[:, :, 0:nk]
                bias = pbias[m // NKV][:, 0:nk].rearrange("p (h k) -> p h k", h=1).broadcast_to((P, 4, nk))
                if m % 4 == 0:
                    dve.wait_ge(pbias_ready, m // 4 + 1)
                v.tensor_tensor(pl, s, bias, ALU.add).then_inc(pa_lg, 1)
                dve.wait_ge(pa_lg, m + 1)
                link(v.tensor_reduce(small[:, 0:4], pl, AX_X, ALU.max))
                v.tensor_scalar(small[:, 4:8], small[:, 0:4], -QK_SCALE, None, ALU.mult).then_inc(pa_nb, 1)

            def pa_t(m):
                nk = P * (m // NKV + 1)
                pl = prob[:, 0:4 * nk].rearrange("p (h k) -> p h k", h=4)
                dve.wait_ge(pa_exp, m + 1)
                link(v.reciprocal(small[:, 12:16], small[:, 8:12]))
                v.tensor_tensor(pl, pl, small[:, 12:16].rearrange("p (h k) -> p h k", k=1).broadcast_to((P, 4, nk)),
                                ALU.mult).then_inc(pa_prob, 1)

            def pa_v(m):
                qt, g = divmod(m, NKV)
                dve.wait_ge(pa_vmm, m + 1)
                v.tensor_copy(qT[:, 2 * g:2 * g + 2, P * qt:P * (qt + 1)],
                              bank(6)[:, 0:256].rearrange("p (a q) -> p a q", a=2)).then_inc(pa_out, 1)

            def sa_l(b):
                dve.wait_ge(sa_lmm, b + 1)
                if b:
                    dve.wait_ge(sa_exp, b)
                logits = psum[:, 5:8, :].rearrange("p a b -> p (a b)")[:, 0:KEYS]
                link(v.tensor_reduce(small[:, 16:17], logits, AX_X, ALU.max))
                v.tensor_scalar(small[:, 17:18], small[:, 16:17], -QK_SCALE, None, ALU.mult).then_inc(sa_nb, 1)

            def sa_p(b):
                dve.wait_ge(sa_exp, b + 1)
                link(v.reciprocal(small[:, 19:20], small[:, 18:19]))
                v.tensor_scalar(prob[:], prob[:], small[:, 19:20], None, ALU.mult).then_inc(sa_prob, 1)

            def sa_v(b):
                dve.wait_ge(sa_vmm, b + 1)
                for pp in range(2):
                    for ip in range(2):
                        src = bank(4)[HD * pp:HD * (pp + 1), 0:128].rearrange(
                            "p (j g a i t) -> p j g a i t", j=2, g=2, a=2, i=2)[:, :, pp, :, ip, :]
                        dst = tokens(qT, b)[HD * ip:HD * (ip + 1)].rearrange(
                            "p (j g a) t -> p j g a t", j=2, g=2)[:, :, pp]
                        last = v.tensor_copy(dst, src)
                last.then_inc(sa_out, 1)

            def lru_gain(c):
                dve.wait_ge(lru_a, c + 1)
                if c:
                    dve.wait_ge(lru_done, c)
                link(v.tensor_scalar(g_u[:], g_th[:], 1.0, None, ALU.add))
                link(v.reciprocal(g_u[:], g_u[:]))
                v.tensor_tensor(g_th[:], g_th[:], g_u[:], ALU.mult).then_inc(lru_w, 1)
                dve.wait_ge(lru_w, c + 1)
                link(v.tensor_tensor(g_u[:], g_i[:], xc[:, c % 2, :], ALU.mult))

            def starts(ap):
                return ap[:, SEQ + PAD - 1:SEQ + PAD - 1 + SEGB * (NB - 1) + 1:SEGB]

            def lru_scan(c):
                dve.wait_ge(lru_s, c + 1)
                link(v.tensor_tensor(g_u[:], g_u[:], g_th[:], ALU.mult))
                link(v.tensor_scalar(starts(g_a), starts(g_a), 0.0, None, ALU.mult))
                link(v.tensor_copy(starts(g_u), stT[:, c, 24:32]))
                link(v.tensor_tensor_scan(g_u[:], g_a[:], g_u[:], 0.0, ALU.mult, ALU.add))
                seg = g_u[:, S0:S0 + SEGB * (NB - 1) + TS]
                v.tensor_copy(tail[:, c, 27:28], g_u[:, SEQ - 1:SEQ])
                v.tensor_copy(tail[:, c, 28:36], g_u[:, S0 + TS - 1:S0 + TS - 1 + SEGB * (NB - 1) + 1:SEGB])
                v.tensor_tensor(rnnT[:, c, 0:SEQ], rnnT[:, c, 0:SEQ], g_u[:, 0:SEQ], ALU.mult)
                hs = arena_seg(g_u)
                v.tensor_tensor(rnnT[:, c, SEQ:T].rearrange("p (b t) -> p b t", b=NB),
                                rnnT[:, c, SEQ:T].rearrange("p (b t) -> p b t", b=NB), hs, ALU.mult).then_inc(lru_done, 1)

            def arena_seg(ap):
                a = ap[:, S0:S0 + TS]
                return bass.AP(tensor=a.tensor, offset=a.offset, ap=[a.ap[0], [SEGB, NB], [1, TS]])

            def evac(u):
                kind, i, _ = units[u]
                acc = bank(u % 2)
                free = acc_free[u % 2]
                if kind == "xr":
                    dve.wait_ge(*freed(u))
                    x = xpad[:, i % 2, :]
                    cw = [vec[:, V_CW + CR * j + i:V_CW + CR * j + i + 1] for j in range(CW)]
                    c = xc[:, i % 2, :]
                    v.tensor_copy(tail[:, i, 0:3], x[:, S0 - 3:S0])
                    v.tensor_copy(tail[:, i, 3:27].rearrange("p (b j) -> p b j", b=NB),
                                  x[:, S0:XP].rearrange("p (b s) -> p b s", b=NB)[:, :, TS:SEGB])
                    if i >= 2:
                        dve.wait_ge(acc_ready, unit_at[("gx", i - 2)] + 1)
                    link(v.tensor_scalar(c, x[:, 0:XC], cw[0], vec[:, V_CB + i:V_CB + i + 1], ALU.mult, ALU.add))
                    for j in range(1, CW):
                        last = v.scalar_tensor_tensor(out=c, in0=x[:, j:j + XC], scalar=cw[j], in1=c, op0=ALU.mult,
                                                      op1=ALU.add)
                        if j < CW - 1:
                            link(last)
                    last.then_inc(conv_ready, 1)
                    if i >= 2:
                        lru_scan(i - 2)
                elif kind == "ga":
                    if i == CR - 1:
                        lru_scan(CR - 2)
                elif kind == "gx":
                    lru_gain(i)
                    if i == CR - 1:
                        lru_scan(CR - 1)
                elif kind == "brr":
                    dve.wait_ge(acc_ready, u + 1)
                    dve.wait_ge(*freed(unit_at[("gmr", i)]))
                    v.tensor_tensor(sgm[:, i % 4, :], bank(u % 2, T), sgm[:, i % 4, :], ALU.mult).then_inc(free, 1)
                elif kind == "bra":
                    dve.wait_ge(acc_ready, u + 1)
                    dve.wait_ge(*freed(unit_at[("gma", i)]))
                    if i == 0:
                        dve.wait_ge(spill_in, 32)
                    gate = back[:, KD + i, :] if i < GSPILL else sgm[:, i % 4, :]
                    v.tensor_tensor(gate, bank(u % 2, T), gate, ALU.mult).then_inc(free, 1)
                    dve.wait_ge(*freed(u))
                    v.tensor_tensor(G[:, i, :], back[:, i, :], gate, ALU.add).then_inc(mix_ready, 1)
                    if i:
                        input_low(1, i - 1)
                    if i == KD - 1:
                        input_low(1, i)
                elif kind == "out":
                    dve.wait_ge(acc_ready, u + 1)
                    v.tensor_tensor(XT[:, i, :], bank(u % 2, T), XT[:, i, :], ALU.add).then_inc(free, 1)

            todo = {"split": lows, "pi": pi, "si_t": si_t, "sc": sc, "tk": tk, "ptk": ptk, "sel": sel, "pa_l": pa_l, "pa_t": pa_t, "pa_v": pa_v,
                    "sa_l": sa_l, "sa_p": sa_p, "sa_v": sa_v, "unit": evac}
            for what, i in vector_order(steps, units):
                if what in todo:
                    todo[what](i)
            for u in range(first_bra, len(units)):
                lows(u)
                evac(u)
            second_dve(dve, link, normalise, input_low)


_INS = ["x_prompt", "x_sample", "p_prompt", "p_sample", "cache_k", "cache_v", "cache_kidx", "state_conv", "state_h",
        "page_table", "ln1", "w_in", "q_norm", "k_norm", "conv_w", "conv_b", "w_a", "b_a", "w_x", "b_x", "lam",
        "w_br_rnn", "w_br_attn", "w_out", "ln2", "w_rg", "b_rg", "w_re", "b_re", "w1", "w3", "w2", "ln3",
        "w_ple_gate", "w_ple_proj"]
_OUTS = [("y_prompt", (1, SEQ, D)), ("y_sample", (NB, TS, D)), ("k_prompt", (1, 1, SEQ, NKV, HD)),
         ("v_prompt", (1, 1, SEQ, NKV, HD)), ("kidx_prompt", (1, 1, SEQ, HD)), ("conv_prompt", (1, 1, PAD, DR)),
         ("h_prompt", (1, 1, DR)), ("k_sample", (1, NB, TS, NKV, HD)), ("v_sample", (1, NB, TS, NKV, HD)),
         ("kidx_sample", (1, NB, TS, HD)), ("conv_sample", (1, NB, PAD, DR)), ("h_sample", (1, NB, DR))]


def kernel(**inputs):
    import concourse.bacc as _bacc
    from concourse.bass_utils import run_bass_kernel_spmd as _run

    nc = _bacc.Bacc("TRN2", target_bir_lowering=False, num_devices=1)
    arrays, A, O = {}, {}, {}
    data = {name: np.ascontiguousarray(inputs[name]) for name in _INS}
    data["consts"] = constants()[0]
    for name, a in data.items():
        arrays[f"in_{name}"] = a
        A[name] = nc.dram_tensor(f"in_{name}", a.shape, mybir.dt.from_np(a.dtype), kind="ExternalInput").ap()
    for name, shape in _OUTS:
        O[name] = nc.dram_tensor(f"out_{name}", shape, F32, kind="ExternalOutput").ap()
    build_program(nc, A, O)
    r = _run(nc, [arrays], core_ids=[0])
    return tuple(r.results[0][f"out_{name}"] for name, _ in _OUTS)
```
